# Optimizing a Trainium2 kernel written in Bass

```python
import jax, jax.numpy as jnp
from jax import lax
import numpy as np

D_MODEL = 1024
BATCH = 1
SEQ = 256
DEPTH = 1

HEAD_DIM = 64
RMS_EPS = 1e-6
NEG_INF = -1e30
ATTN_SCALE = HEAD_DIM ** -0.5

POOL_WIDTH = 512
POOL_GROUPS = 4
POOL_GROUP_DIM = POOL_WIDTH // POOL_GROUPS
POOL_WINDOWS = (2, 4, 8, 16)

SWA_Q_HEADS = 8
SWA_KV_HEADS = 2
SWA_GROUP = SWA_Q_HEADS // SWA_KV_HEADS
SWA_WINDOW = 128
SWA_BLOCK = 128
SWA_WIDTH = SWA_Q_HEADS * HEAD_DIM
SWA_KV_WIDTH = SWA_KV_HEADS * HEAD_DIM

MOBA_HEADS = 8
MOBA_BLOCK = 256
MOBA_TOPK = 3
MOBA_Q_CHUNK = 64
MOBA_WIDTH = MOBA_HEADS * HEAD_DIM

N_BRANCH = 3
IN_SIZES = (POOL_WIDTH, POOL_WIDTH,
            SWA_WIDTH, SWA_KV_WIDTH, SWA_KV_WIDTH, SWA_WIDTH,
            MOBA_WIDTH, MOBA_WIDTH, MOBA_WIDTH, MOBA_WIDTH,
            N_BRANCH * D_MODEL)
IN_WIDTH = sum(IN_SIZES)


def _rmsnorm(x, g):
    x32 = x.astype(jnp.float32)
    y = x32 * lax.rsqrt(jnp.mean(x32 * x32, axis=-1, keepdims=True) + RMS_EPS)
    return (y * g.astype(jnp.float32)).astype(x.dtype)

def _pool_mixer(xa, w_pool, scale):
    b, s, _ = xa.shape
    x32 = xa.astype(jnp.float32)
    cs = jnp.cumsum(x32, axis=1)
    t = jnp.arange(s)
    outs = []
    for gi, w in enumerate(POOL_WINDOWS):
        cg = cs[..., gi * POOL_GROUP_DIM:(gi + 1) * POOL_GROUP_DIM]
        lag = jnp.pad(cg, ((0, 0), (w, 0), (0, 0)))[:, :s]
        cnt = jnp.minimum(t + 1, w).astype(jnp.float32)
        outs.append((cg - lag) / cnt[None, :, None])
    pooled = (jnp.concatenate(outs, axis=-1) - x32).astype(xa.dtype)
    pooled = pooled.reshape(b, s, POOL_GROUPS, POOL_GROUP_DIM)
    mixed = jnp.einsum('bsgc,gcd->bsgd', pooled, w_pool).reshape(b, s, POOL_WIDTH)
    return mixed * scale

def _swa_attention(q, k, v, sinks):
    b, s = q.shape[0], q.shape[1]
    nb = s // SWA_BLOCK
    qb = q.reshape(b, nb, SWA_BLOCK, SWA_KV_HEADS, SWA_GROUP, HEAD_DIM)
    kb = k.reshape(b, nb, SWA_BLOCK, SWA_KV_HEADS, HEAD_DIM)
    vb = v.reshape(b, nb, SWA_BLOCK, SWA_KV_HEADS, HEAD_DIM)

    def with_prev(t):
        prev = jnp.pad(t[:, :-1], ((0, 0), (1, 0), (0, 0), (0, 0), (0, 0)))
        return jnp.concatenate([prev, t], axis=2)

    kk = with_prev(kb)
    vv = with_prev(vb)
    sc = jnp.einsum('bnqhgd,bnkhd->bnhgqk', qb, kk,
                    preferred_element_type=jnp.float32) * ATTN_SCALE
    qi = jnp.arange(SWA_BLOCK)[:, None] + SWA_BLOCK
    kj = jnp.arange(2 * SWA_BLOCK)[None, :]
    diff = qi - kj
    band = (diff >= 0) & (diff < SWA_WINDOW)
    kpos = jnp.arange(nb)[:, None, None] * SWA_BLOCK + kj[None] - SWA_BLOCK
    valid = band[None] & (kpos >= 0)
    sc = jnp.where(valid[None, :, None, None], sc, NEG_INF)
    sink = sinks.astype(jnp.float32).reshape(1, 1, SWA_KV_HEADS, SWA_GROUP, 1)
    m = jnp.maximum(jnp.max(sc, axis=-1), sink)
    p = jnp.exp(sc - m[..., None])
    denom = jnp.sum(p, axis=-1) + jnp.exp(sink - m)
    p = (p / denom[..., None]).astype(v.dtype)
    o = jnp.einsum('bnhgqk,bnkhd->bnqhgd', p, vv)
    return o.reshape(b, s, SWA_WIDTH)

def _moba_attention(q, k, v):
    b, s = q.shape[0], q.shape[1]
    nblk = -(-s // MOBA_BLOCK)
    s_pad = nblk * MOBA_BLOCK
    pad = ((0, 0), (0, s_pad - s), (0, 0), (0, 0))
    q = jnp.pad(q, pad)
    k = jnp.pad(k, pad)
    v = jnp.pad(v, pad)
    topk = min(MOBA_TOPK, nblk)
    kb = k.reshape(b, nblk, MOBA_BLOCK, MOBA_HEADS, HEAD_DIM)
    vb = v.reshape(b, nblk, MOBA_BLOCK, MOBA_HEADS, HEAD_DIM)
    k_mean = jnp.mean(kb.astype(jnp.float32), axis=2)
    k_bh = kb.transpose(0, 3, 1, 2, 4)
    v_bh = vb.transpose(0, 3, 1, 2, 4)
    bi = jnp.arange(b)[:, None, None, None]
    hi = jnp.arange(MOBA_HEADS)[None, None, :, None]
    n_chunks = s_pad // MOBA_Q_CHUNK

    def chunk_fn(c):
        q0 = c * MOBA_Q_CHUNK
        blk = q0 // MOBA_BLOCK
        qpos = q0 + jnp.arange(MOBA_Q_CHUNK)
        qc = lax.dynamic_slice_in_dim(q, q0, MOBA_Q_CHUNK, axis=1)
        gate = jnp.einsum('bqhd,bnhd->bqhn', qc.astype(jnp.float32), k_mean)
        past = jnp.arange(nblk) < blk
        gate = jnp.where(past[None, None, None, :], gate, NEG_INF)
        _, idx = lax.top_k(gate, topk)
        slot_valid = jnp.arange(topk) < blk
        k_sel = k_bh[bi, hi, idx]
        v_sel = v_bh[bi, hi, idx]
        s_sel = jnp.einsum('bqhd,bqhjkd->bqhjk', qc, k_sel,
                           preferred_element_type=jnp.float32) * ATTN_SCALE
        s_sel = jnp.where(slot_valid[:, None], s_sel, NEG_INF)
        s_sel = s_sel.reshape(b, MOBA_Q_CHUNK, MOBA_HEADS, topk * MOBA_BLOCK)
        k_own = lax.dynamic_slice_in_dim(kb, blk, 1, axis=1)[:, 0]
        v_own = lax.dynamic_slice_in_dim(vb, blk, 1, axis=1)[:, 0]
        s_own = jnp.einsum('bqhd,bkhd->bqhk', qc, k_own,
                           preferred_element_type=jnp.float32) * ATTN_SCALE
        kpos = blk * MOBA_BLOCK + jnp.arange(MOBA_BLOCK)
        causal = kpos[None, :] <= qpos[:, None]
        s_own = jnp.where(causal[None, :, None, :], s_own, NEG_INF)
        p = jax.nn.softmax(jnp.concatenate([s_sel, s_own], axis=-1), axis=-1).astype(v.dtype)
        p_sel = p[..., :topk * MOBA_BLOCK].reshape(b, MOBA_Q_CHUNK, MOBA_HEADS, topk, MOBA_BLOCK)
        p_own = p[..., topk * MOBA_BLOCK:]
        o = (jnp.einsum('bqhjk,bqhjkd->bqhd', p_sel, v_sel)
             + jnp.einsum('bqhk,bkhd->bqhd', p_own, v_own))
        return o.astype(q.dtype)

    outs = lax.map(chunk_fn, jnp.arange(n_chunks))
    o = outs.transpose(1, 0, 2, 3, 4).reshape(b, s_pad, MOBA_WIDTH)
    return o[:, :s]

def _layer(x, norm_g, w_in, pool_w, pool_scale, sinks, w_proj_a, w_proj_b, w_proj_c, w_out):
    b, s, _ = x.shape
    h = _rmsnorm(x, norm_g)
    u = h @ w_in
    offsets = np.cumsum(IN_SIZES)[:-1].tolist()
    (a_x, a_z, b_q, b_k, b_v, b_z, c_q, c_k, c_v, c_z, gate_logits) = jnp.split(u, offsets, axis=-1)
    ya = _pool_mixer(a_x, pool_w, pool_scale) * jax.nn.silu(a_z)
    yb = _swa_attention(b_q.reshape(b, s, SWA_Q_HEADS, HEAD_DIM),
                        b_k.reshape(b, s, SWA_KV_HEADS, HEAD_DIM),
                        b_v.reshape(b, s, SWA_KV_HEADS, HEAD_DIM), sinks) * jax.nn.silu(b_z)
    yc = _moba_attention(c_q.reshape(b, s, MOBA_HEADS, HEAD_DIM),
                         c_k.reshape(b, s, MOBA_HEADS, HEAD_DIM),
                         c_v.reshape(b, s, MOBA_HEADS, HEAD_DIM)) * jax.nn.silu(c_z)
    ga, gb, gc = jnp.split(jax.nn.sigmoid(gate_logits), N_BRANCH, axis=-1)
    merged = ga * (ya @ w_proj_a) + gb * (yb @ w_proj_b) + gc * (yc @ w_proj_c)
    return x + merged @ w_out

def first_inputs(seed: int = 0) -> dict:
    key = jax.random.key(seed)
    ks = jax.random.split(key, 11)
    nrm = jax.random.normal
    x = nrm(ks[0], (BATCH, SEQ, D_MODEL), jnp.float32)
    norm_g = 1.0 + 0.05 * nrm(ks[1], (DEPTH, D_MODEL), jnp.float32)
    w_in = nrm(ks[2], (DEPTH, D_MODEL, IN_WIDTH), jnp.float32) * D_MODEL ** -0.5
    pool_w = nrm(ks[3], (DEPTH, POOL_GROUPS, POOL_GROUP_DIM, POOL_GROUP_DIM), jnp.float32) * POOL_GROUP_DIM ** -0.5
    pool_scale = 1.0 + 0.1 * nrm(ks[4], (DEPTH, POOL_WIDTH), jnp.float32)
    sink_logits = 0.5 * nrm(ks[5], (DEPTH, SWA_Q_HEADS), jnp.float32)
    w_proj_a = nrm(ks[6], (DEPTH, POOL_WIDTH, D_MODEL), jnp.float32) * POOL_WIDTH ** -0.5
    w_proj_b = nrm(ks[7], (DEPTH, SWA_WIDTH, D_MODEL), jnp.float32) * SWA_WIDTH ** -0.5
    w_proj_c = nrm(ks[8], (DEPTH, MOBA_WIDTH, D_MODEL), jnp.float32) * MOBA_WIDTH ** -0.5
    w_out = nrm(ks[9], (DEPTH, D_MODEL, D_MODEL), jnp.float32) * D_MODEL ** -0.5
    final_norm_g = 1.0 + 0.05 * nrm(ks[10], (D_MODEL,), jnp.float32)
    return {"x": x, "norm_g": norm_g, "w_in": w_in, "pool_w": pool_w, "pool_scale": pool_scale,
            "sink_logits": sink_logits, "w_proj_a": w_proj_a, "w_proj_b": w_proj_b,
            "w_proj_c": w_proj_c, "w_out": w_out, "final_norm_g": final_norm_g}

def first_block(x, norm_g, w_in, pool_w, pool_scale, sink_logits, w_proj_a, w_proj_b, w_proj_c,
              w_out, final_norm_g):
    for l in range(DEPTH):
        x = _layer(x, norm_g[l], w_in[l], pool_w[l], pool_scale[l], sink_logits[l],
                   w_proj_a[l], w_proj_b[l], w_proj_c[l], w_out[l])
    return _rmsnorm(x, final_norm_g)


DEPTH_2 = 2

CHUNK = 64
LEFT_CHUNKS = 8
BAND_CHUNKS = LEFT_CHUNKS + 1
BAND = BAND_CHUNKS * CHUNK
MIX_WIDTH = D_MODEL
RWKV_WIDTH = MIX_WIDTH // 2
ATT_WIDTH = MIX_WIDTH - RWKV_WIDTH
RWKV_HEADS = RWKV_WIDTH // HEAD_DIM
ATT_HEADS = ATT_WIDTH // HEAD_DIM
DECAY_LORA = 64
AAA_LORA = 64
GATE_LORA = 128
RWKV_COLS = 3 * RWKV_WIDTH + DECAY_LORA + AAA_LORA + GATE_LORA
IN_COLS = RWKV_COLS + 3 * ATT_WIDTH
MAX_REL = 2 * CHUNK
CONV_WIDTH = 31
D_FF = 4 * D_MODEL
NORM_EPS = 1e-6
LN_EPS = 1e-5
GN_EPS = 64e-5


def rmsnorm(x, g):
    x32 = x.astype(jnp.float32)
    y = x32 * lax.rsqrt(jnp.mean(x32 * x32, axis=-1, keepdims=True) + NORM_EPS)
    return (y * g.astype(jnp.float32)).astype(x.dtype)

def token_shift(p):
    return jnp.pad(p, ((0, 0), (1, 0), (0, 0)))[:, :-1]

def rwkv7_scan(r, decay, k, v, kk, a):
    B, T, H, N = r.shape
    def step(S, inp):
        r_t, w_t, k_t, v_t, kk_t, a_t = inp
        sa = jnp.einsum('bhij,bhj->bhi', S, -kk_t)
        S = (S * w_t[:, :, None, :]
             + sa[..., None] * (kk_t * a_t)[:, :, None, :]
             + v_t[..., None] * k_t[:, :, None, :])
        y = jnp.einsum('bhij,bhj->bhi', S, r_t)
        return S, y
    xs = tuple(jnp.moveaxis(z.astype(jnp.float32), 1, 0) for z in (r, decay, k, v, kk, a))
    S0 = jnp.zeros((B, H, N, N), jnp.float32)
    _, ys = lax.scan(step, S0, xs)
    return jnp.moveaxis(ys, 0, 1)

def rwkv7_group(p, mu, w0, w2, a0, a2, g2, k_k, k_a, r_k, lnx_w, lnx_b):
    B, T, _ = p.shape
    p = p + (token_shift(p) - p) * mu
    split_at = [RWKV_WIDTH, 2 * RWKV_WIDTH, 3 * RWKV_WIDTH,
                3 * RWKV_WIDTH + DECAY_LORA, 3 * RWKV_WIDTH + DECAY_LORA + AAA_LORA]
    r, k, v, xw, xa, xg = jnp.split(p, split_at, axis=-1)
    w = -jax.nn.softplus(-(w0 + jnp.tanh(xw) @ w2)) - 0.5
    decay = jnp.exp(-jnp.exp(w.astype(jnp.float32)))
    a = jax.nn.sigmoid(a0 + xa @ a2)
    g = jax.nn.sigmoid(xg) @ g2
    heads = lambda z: z.reshape(B, T, RWKV_HEADS, HEAD_DIM)
    kk = heads(k * k_k).astype(jnp.float32)
    kk = kk / jnp.maximum(jnp.sqrt(jnp.sum(kk * kk, axis=-1, keepdims=True)), 1e-12)
    k = k * (1 + (a - 1) * k_a)
    rh, kh, vh, ah = heads(r), heads(k), heads(v), heads(a)
    y = rwkv7_scan(rh, heads(decay), kh, vh, kk, ah)
    mean = jnp.mean(y, axis=-1, keepdims=True)
    var = jnp.mean(jnp.square(y - mean), axis=-1, keepdims=True)
    y = (y - mean) * lax.rsqrt(var + GN_EPS)
    y = y * lnx_w.reshape(RWKV_HEADS, HEAD_DIM).astype(jnp.float32) + lnx_b.reshape(RWKV_HEADS, HEAD_DIM).astype(jnp.float32)
    bonus = jnp.sum((rh * kh * r_k.reshape(RWKV_HEADS, HEAD_DIM)).astype(jnp.float32), axis=-1, keepdims=True) * vh.astype(jnp.float32)
    y = (y + bonus).reshape(B, T, RWKV_WIDTH).astype(p.dtype)
    return y * g

def chunk_band_attention(q, k, v, rel_bias):
    B, T, _ = q.shape
    nc = T // CHUNK
    shp = (B, nc, CHUNK, ATT_HEADS, HEAD_DIM)
    qc, kc, vc = q.reshape(shp), k.reshape(shp), v.reshape(shp)
    pad = ((0, 0), (LEFT_CHUNKS, 0), (0, 0), (0, 0), (0, 0))
    band_idx = jnp.arange(nc)[:, None] + jnp.arange(BAND_CHUNKS)[None, :]
    kb = jnp.pad(kc, pad)[:, band_idx].reshape(B, nc, BAND, ATT_HEADS, HEAD_DIM)
    vb = jnp.pad(vc, pad)[:, band_idx].reshape(B, nc, BAND, ATT_HEADS, HEAD_DIM)
    valid = jnp.repeat(band_idx >= LEFT_CHUNKS, CHUNK, axis=1)
    rel = jnp.arange(CHUNK)[:, None] + LEFT_CHUNKS * CHUNK - jnp.arange(BAND)[None, :]
    bias = rel_bias[:, jnp.clip(rel, -MAX_REL, MAX_REL) + MAX_REL]
    s = jnp.einsum('bcqhd,bckhd->bhcqk', qc, kb).astype(jnp.float32) * (HEAD_DIM ** -0.5)
    s = s + bias[:, None].astype(jnp.float32)
    s = jnp.where(valid[:, None, :], s, -1e30)
    probs = jax.nn.softmax(s, axis=-1).astype(v.dtype)
    o = jnp.einsum('bhcqk,bckhd->bcqhd', probs, vb)
    return o.reshape(B, T, ATT_WIDTH)

def rwkv_attention_mixer(h, w_in, mu, w0, w2, a0, a2, g2, k_k, k_a, r_k, lnx_w, lnx_b, rel_bias, w_out):
    proj = h @ w_in
    p_rwkv, q, k, v = jnp.split(proj, [RWKV_COLS, RWKV_COLS + ATT_WIDTH, RWKV_COLS + 2 * ATT_WIDTH], axis=-1)
    y_rwkv = rwkv7_group(p_rwkv, mu, w0, w2, a0, a2, g2, k_k, k_a, r_k, lnx_w, lnx_b)
    y_att = chunk_band_attention(q, k, v, rel_bias)
    return jnp.concatenate([y_rwkv, y_att], axis=-1) @ w_out

def conformer_conv(h, pw1, pw1_b, dw, dw_b, ln_w, ln_b, pw2, pw2_b):
    u = jax.nn.glu(h @ pw1 + pw1_b, axis=-1)
    u = lax.conv_general_dilated(u, dw[:, None, :].astype(u.dtype), (1,), [(CONV_WIDTH - 1, 0)],
                                 dimension_numbers=('NWC', 'WIO', 'NWC'),
                                 feature_group_count=D_MODEL) + dw_b
    u32 = u.astype(jnp.float32)
    mean = jnp.mean(u32, axis=-1, keepdims=True)
    var = jnp.mean(jnp.square(u32 - mean), axis=-1, keepdims=True)
    u = ((u32 - mean) * lax.rsqrt(var + LN_EPS) * ln_w.astype(jnp.float32) + ln_b.astype(jnp.float32)).astype(h.dtype)
    return jax.nn.silu(u) @ pw2 + pw2_b

def sq_relu_mlp(h, up, down):
    return jnp.square(jax.nn.relu(h @ up)) @ down

def second_inputs(seed: int = 0) -> dict:
    key = jax.random.key(seed)
    ks = jax.random.split(key, 40)
    nrm = lambda i, shape, scale: jax.random.normal(ks[i], shape, jnp.float32) * scale
    gain = lambda i, n: 1.0 + 0.05 * jax.random.normal(ks[i], (n,), jnp.float32)
    return {
        "x": nrm(0, (BATCH, SEQ, D_MODEL), 1.0),
        "l0_norm_mix": gain(1, D_MODEL),
        "l0_w_in": nrm(2, (D_MODEL, IN_COLS), D_MODEL ** -0.5),
        "l0_shift_mu": jax.random.uniform(ks[3], (RWKV_COLS,), jnp.float32),
        "l0_w0": jax.random.uniform(ks[4], (RWKV_WIDTH,), jnp.float32, -6.0, 1.0),
        "l0_w2": nrm(5, (DECAY_LORA, RWKV_WIDTH), DECAY_LORA ** -0.5),
        "l0_a0": nrm(6, (RWKV_WIDTH,), 0.1),
        "l0_a2": nrm(7, (AAA_LORA, RWKV_WIDTH), AAA_LORA ** -0.5),
        "l0_g2": nrm(8, (GATE_LORA, RWKV_WIDTH), GATE_LORA ** -0.5),
        "l0_k_k": 0.85 + nrm(9, (RWKV_WIDTH,), 0.05),
        "l0_k_a": 1.0 + nrm(10, (RWKV_WIDTH,), 0.05),
        "l0_r_k": nrm(11, (RWKV_WIDTH,), 0.1),
        "l0_lnx_w": gain(12, RWKV_WIDTH),
        "l0_lnx_b": nrm(13, (RWKV_WIDTH,), 0.02),
        "l0_rel_bias": nrm(14, (ATT_HEADS, 2 * MAX_REL + 1), 0.5),
        "l0_w_out": nrm(15, (MIX_WIDTH, D_MODEL), MIX_WIDTH ** -0.5),
        "l0_norm_ffn": gain(16, D_MODEL),
        "l0_ffn_up": nrm(17, (D_MODEL, D_FF), D_MODEL ** -0.5),
        "l0_ffn_down": nrm(18, (D_FF, D_MODEL), D_FF ** -0.5),
        "l1_norm_mix": gain(19, D_MODEL),
        "l1_pw1": nrm(20, (D_MODEL, 2 * D_MODEL), D_MODEL ** -0.5),
        "l1_pw1_b": nrm(21, (2 * D_MODEL,), 0.02),
        "l1_dw": nrm(22, (CONV_WIDTH, D_MODEL), CONV_WIDTH ** -0.5),
        "l1_dw_b": nrm(23, (D_MODEL,), 0.02),
        "l1_ln_w": gain(24, D_MODEL),
        "l1_ln_b": nrm(25, (D_MODEL,), 0.02),
        "l1_pw2": nrm(26, (D_MODEL, D_MODEL), D_MODEL ** -0.5),
        "l1_pw2_b": nrm(27, (D_MODEL,), 0.02),
        "l1_norm_ffn": gain(28, D_MODEL),
        "l1_ffn_up": nrm(29, (D_MODEL, D_FF), D_MODEL ** -0.5),
        "l1_ffn_down": nrm(30, (D_FF, D_MODEL), D_FF ** -0.5),
        "final_norm": gain(31, D_MODEL),
    }

def second_block(x, l0_norm_mix, l0_w_in, l0_shift_mu, l0_w0, l0_w2, l0_a0, l0_a2, l0_g2,
              l0_k_k, l0_k_a, l0_r_k, l0_lnx_w, l0_lnx_b, l0_rel_bias, l0_w_out,
              l0_norm_ffn, l0_ffn_up, l0_ffn_down,
              l1_norm_mix, l1_pw1, l1_pw1_b, l1_dw, l1_dw_b, l1_ln_w, l1_ln_b,
              l1_pw2, l1_pw2_b, l1_norm_ffn, l1_ffn_up, l1_ffn_down, final_norm):
    mix_norms = (l0_norm_mix, l1_norm_mix)
    mix_params = (
        (l0_w_in, l0_shift_mu, l0_w0, l0_w2, l0_a0, l0_a2, l0_g2, l0_k_k, l0_k_a,
         l0_r_k, l0_lnx_w, l0_lnx_b, l0_rel_bias, l0_w_out),
        (l1_pw1, l1_pw1_b, l1_dw, l1_dw_b, l1_ln_w, l1_ln_b, l1_pw2, l1_pw2_b),
    )
    ffn_params = ((l0_norm_ffn, l0_ffn_up, l0_ffn_down), (l1_norm_ffn, l1_ffn_up, l1_ffn_down))
    for layer in range(DEPTH_2):
        h = rmsnorm(x, mix_norms[layer])
        if layer % 2 == 0:
            x = x + rwkv_attention_mixer(h, *mix_params[layer])
        else:
            x = x + conformer_conv(h, *mix_params[layer])
        g_ffn, up, down = ffn_params[layer]
        x = x + sq_relu_mlp(rmsnorm(x, g_ffn), up, down)
    return rmsnorm(x, final_norm)


def setup_inputs(seed=0):
    out = dict(first_inputs(seed))
    for name, value in second_inputs(seed + 1).items():
        if name != "x":
            out[name + "_2"] = value
    return out


def reference(
    x, norm_g, w_in, pool_w, pool_scale, sink_logits, w_proj_a, w_proj_b, w_proj_c, w_out,
    final_norm_g, l0_norm_mix_2, l0_w_in_2, l0_shift_mu_2, l0_w0_2, l0_w2_2, l0_a0_2, l0_a2_2,
    l0_g2_2, l0_k_k_2, l0_k_a_2, l0_r_k_2, l0_lnx_w_2, l0_lnx_b_2, l0_rel_bias_2, l0_w_out_2,
    l0_norm_ffn_2, l0_ffn_up_2, l0_ffn_down_2, l1_norm_mix_2, l1_pw1_2, l1_pw1_b_2, l1_dw_2,
    l1_dw_b_2, l1_ln_w_2, l1_ln_b_2, l1_pw2_2, l1_pw2_b_2, l1_norm_ffn_2, l1_ffn_up_2,
    l1_ffn_down_2, final_norm_2,
):
    x = first_block(
        x, norm_g, w_in, pool_w, pool_scale, sink_logits, w_proj_a, w_proj_b, w_proj_c, w_out,
        final_norm_g,
    )
    return second_block(
        x, l0_norm_mix_2, l0_w_in_2, l0_shift_mu_2, l0_w0_2, l0_w2_2, l0_a0_2, l0_a2_2, l0_g2_2,
        l0_k_k_2, l0_k_a_2, l0_r_k_2, l0_lnx_w_2, l0_lnx_b_2, l0_rel_bias_2, l0_w_out_2,
        l0_norm_ffn_2, l0_ffn_up_2, l0_ffn_down_2, l1_norm_mix_2, l1_pw1_2, l1_pw1_b_2, l1_dw_2,
        l1_dw_b_2, l1_ln_w_2, l1_ln_b_2, l1_pw2_2, l1_pw2_b_2, l1_norm_ffn_2, l1_ffn_up_2,
        l1_ffn_down_2, final_norm_2,
    )


_drawn_inputs = setup_inputs


def setup_inputs(seed=0):
    import zlib

    import numpy as np

    out = dict(_drawn_inputs(seed))
    spreads = {}
    factors = {'sink_logits': 8.0,
     'l0_a0_2': 3.565,
     'l0_k_k_2': 4.249,
     'l0_lnx_b_2': 6.618,
     'l1_pw1_b_2': 6.966,
     'l1_dw_b_2': 3.564,
     'l1_ln_b_2': 7.48,
     'l1_pw2_b_2': 4.721}
    for name, (base, spread) in spreads.items():
        noise = np.random.default_rng([zlib.crc32(name.encode()), seed]).standard_normal(out[name].shape)
        drawn = base * np.exp(spread * noise) if base else spread * noise
        out[name] = __import__('jax').numpy.asarray(drawn.astype(out[name].dtype))
    for name, factor in factors.items():
        out[name] = (out[name] * factor).astype(out[name].dtype)
    return out
```

```python
from contextlib import ExitStack
import math

import numpy as np
import concourse.bass as bass
from concourse import mybir

F32 = mybir.dt.float32
F32R = mybir.dt.float32r
ALU = mybir.AluOpType
ACT = mybir.ActivationFunctionType
AX_X = mybir.AxisListType.X

P = 128
T = 256
NT = T // P
DM = 1024
KC = DM // P
HD = 64
NEG = -1e30
SCALE = HD ** -0.5
UNIT = 2048
RAWS, WBUFS = 4, 3
C = 32
NCH = T // C
DECAY = math.exp(-0.5)
TAPS = 31
PAD = TAPS - 1
POOL_WINDOWS = (2, 4, 8, 16)
FF_STEPS = 16

AX, AZ, BQ, BKV, BZ, CQ, CK, CV, CZ, GATES = 0, 512, 1024, 1536, 1792, 2304, 2816, 3328, 3840, 4352
Q2, K2, V2 = 1792, 2304, 2816


def shape_constants():
    names, parts, at = {}, [], 0

    def put(name, a):
        nonlocal at
        a = np.asarray(a, np.float32)
        names[name] = (at, at + a.shape[1])
        parts.append(a)
        at += a.shape[1]

    i = np.arange(P)[:, None]
    j = np.arange(P)[None, :]
    put("ident", i == j)
    put("ones", np.ones((P, P)))
    put("head_ones", (i // HD) == (j // HD))
    causal = np.where(j <= i, 0.0, NEG)
    prev = np.where(j > i, 0.0, NEG)
    put("mask_swa", np.concatenate([causal, prev, causal], 1))
    put("mask_causal", np.concatenate([causal, np.zeros((P, P)), causal], 1))
    same32, same16 = (i // 32) == (j // 32), (i // 16) == (j // 16)
    put("up16", same16 & (i < j))
    put("low16", same16 & (i > j))
    put("cross", same32 & ~same16 & (i < j))
    put("up32", same32 & (i < j))
    put("upinc32", same32 & (i <= j))
    keep = at
    t = np.arange(T)[None, :]
    for w in POOL_WINDOWS:
        put(f"pool{w}", ((i <= t) & (t < i + w)) / np.minimum(t + 1, w) - (i == t))
    for w in POOL_WINDOWS:
        put(f"late{w}", ((i <= j) & (j < i + w)) / w - (i == j))
    put("scan_keep", np.tile((np.arange(T) % C != 0).astype(np.float32), (P, 4)))
    return names, keep, np.ascontiguousarray(np.concatenate(parts, 1))


CONST, NKEEP, CONSTS = shape_constants()

VECS = [("norm_g", 8), ("pool_scale", 4), ("l0_norm_mix_2", 8), ("l0_shift_mu_2", 14),
        ("l0_w0_2", 4), ("l0_a0_2", 4), ("l0_k_k_2", 4), ("l0_k_a_2", 4), ("l0_r_k_2", 4),
        ("l0_lnx_w_2", 4), ("l0_lnx_b_2", 4), ("l0_norm_ffn_2", 8), ("l1_norm_mix_2", 8),
        ("l1_pw1_b_2", 16), ("l1_dw_b_2", 8), ("l1_ln_w_2", 8), ("l1_ln_b_2", 8),
        ("l1_norm_ffn_2", 8)]
VROW = {}
NVROWS = 0
for _name, _k in VECS:
    VROW[_name] = NVROWS
    NVROWS += _k

INVERSE = [("GN", "dve"), ("GA", "dve"), ("GD", "dve"), ("AV", "act"), ("N2", "act"), ("D2", "dve"),
           ("N4", "act"), ("X2", "dve"), ("D4", "act"), ("X4", "dve"), ("D8", "act"), ("X8", "dve"),
           ("Z1", "act"), ("EZ", "act"), ("ZZ", "dve")]


class Plan:

    def __init__(self):
        self.units, self.uses, self.count, self.done = [], {}, [0] * 8, {}
        self.turn = 0

    def use(self, name, bank=None):
        if bank is None:
            bank = self.turn
            self.turn ^= 1
        assert name not in self.uses
        self.uses[name] = (bank, self.count[bank])
        self.count[bank] += 1
        return name

    def unit(self, kind, w, row, col, last):
        self.units.append((kind, w, row, col))
        self.done[len(self.units) - 1] = last


def plan():
    s = Plan()

    def norm(tag):
        for q in range(4):
            s.use(f"{tag}_t{q}", q)

    def t_units(tag, w, col, n):
        for i in range(n):
            s.unit("T", w, 0, col + 256 * i, s.use(f"{tag}{i}"))

    def nat_units(tag, w, col, banks):
        s.unit("N", w, 0, col, None)
        for b, bank in enumerate(banks):
            s.use(f"{tag}{b}", bank)
        s.unit("N", w, 512, col, f"{tag}1")

    def proj_out(tag, w):
        for c in range(2):
            nat_units(f"{tag}{c}_", w, 512 * c, (4 + 2 * c, 5 + 2 * c))

    def heads(first, n):
        for a in range(first, first + n):
            s.use(f"sc{a}", 2 + a % 2)
            s.use(f"pt{a}", 4)
            if a % 2:
                s.use(f"o{a // 2}", 5)

    s.use("vec0")
    norm("n0")
    nat_units("ax", "w_in", AX, (6, 7))
    t_units("az", "w_in", AZ, 2)
    s.use("vec1")
    for name in ("pool0", "pool1", "mix0", "mix1"):
        s.use(name)
    t_units("bq", "w_in", BQ, 2)
    s.use("bk")
    s.unit("KV", "w_in", 0, BKV, s.use("bv"))
    t_units("bz", "w_in", BZ, 2)
    t_units("cq", "w_in", CQ, 2)
    t_units("ck", "w_in", CK, 2)
    nat_units("cv", "w_in", CV, (6, 7))
    t_units("cz", "w_in", CZ, 2)
    for m, w in enumerate(("w_proj_a", "w_proj_b", "w_proj_c")):
        t_units(f"g{m}_", "w_in", GATES + m * DM, 4)
        for i in range(2):
            s.use(f"pr{m}_{2 * i}")
            s.unit("TH", w, 0, 512 * i, s.use(f"pr{m}_{2 * i + 1}"))
    heads(0, 16)
    proj_out("wo", "w_out")
    norm("n2")
    t_units("q2_", "l0_w_in_2", Q2, 2)
    t_units("k2_", "l0_w_in_2", K2, 2)
    nat_units("v2_", "l0_w_in_2", V2, (6, 7))
    t_units("rw", "l0_w_in_2", 0, 7)
    heads(16, 8)
    for name in ("z0", "z1", "a0", "a1", "gg0", "gg1", "kn0", "kn1", "bo0", "bo1"):
        s.use(name)
    for name in ("an", "bn", "kn", "vn"):
        s.use(f"nat_{name}0"), s.use(f"nat_{name}1")
    rot = 0
    for pair in range(2):
        for name, _ in INVERSE:
            for g in (2 * pair, 2 * pair + 1):
                s.use(f"{name}_{g}", rot % 8)
                rot += 1
    s.use("wt0"), s.use("wt1")
    for c in range(NCH):
        s.use(f"sae{c}", 2), s.use(f"sao{c}", 3)
        if c < NCH - 1:
            s.use(f"st{c}", 4)
    for g in range(4):
        s.use(f"A3_{g}"), s.use(f"A4_{g}")
        if g % 2:
            s.use(f"y{g // 2}", 5 + g // 2)
    for name in ("gm0", "gm1", "gv0", "gv1"):
        s.use(name)
    proj_out("wp", "l0_w_out_2")

    def ffn(tag, up, down):
        norm(tag)
        for i in range(FF_STEPS + 1):
            if i < FF_STEPS:
                s.unit("T", up, 0, 256 * i, s.use(f"up{tag}_{i}"))
            if i >= 1:
                if i == FF_STEPS:
                    for b in range(4):
                        s.use(f"dn{tag}_{b}", 4 + b)
                s.unit("D", down, 256 * (i - 1), 0, f"dn{tag}_3" if i == FF_STEPS else None)

    ffn("f0", "l0_ffn_up_2", "l0_ffn_down_2")
    norm("n4")
    for i in range(4):
        s.unit("T", "l1_pw1_2", 0, 256 * i, s.use(f"pa{i}"))
        s.unit("T", "l1_pw1_2", 0, DM + 256 * i, s.use(f"pb{i}"))
        s.use(f"taps{i}", 4 + i)
    s.use("lnm"), s.use("lnv")
    proj_out("pw", "l1_pw2_2")
    ffn("f1", "l1_ffn_up_2", "l1_ffn_down_2")
    return s


STOP = 99
PE_TAPS = 12
DOWN = {"f0": "l0_ffn_down_2", "f1": "l1_ffn_down_2"}
UP = {"f0": "l0_ffn_up_2", "f1": "l1_ffn_up_2"}
GAIN = {"n0": "norm_g", "n2": "l0_norm_mix_2", "f0": "l0_norm_ffn_2", "n4": "l1_norm_mix_2",
        "f1": "l1_norm_ffn_2"}


def build(nc, A, consts_d, ext_d, out_d):
    PL = plan()
    UNITS = PL.units
    NU = len(UNITS)
    UID = {u: n for n, u in enumerate(UNITS)}
    PARTIAL = [n for n in range(NU) if PL.done[n] is None]

    def mat(name):
        a = A[name]
        return a[0] if len(a.shape) == 3 else a

    def vec(name):
        a = A[name]
        return a[0] if len(a.shape) == 2 else a

    ctx = ExitStack()
    with ctx:
        def sb(name, shape, dt=F32):
            return ctx.enter_context(nc.sbuf_tensor(name, shape, dt))

        sems = {}

        def E(name):
            if name not in sems:
                sems[name] = ctx.enter_context(nc.semaphore(name))
            return sems[name]

        raw = sb("raw", [P, RAWS, UNIT])
        wh = sb("wh", [P, WBUFS, UNIT], F32R)
        wl = sb("wl", [P, WBUFS, UNIT], F32R)
        yh = sb("yh", [P, 12, T], F32R)
        yl = sb("yl", [P, 12, T], F32R)
        xn = sb("xn", [P, NT, DM])
        cst = sb("cst", [P, NKEEP])
        vt = sb("vt", [P, NVROWS])
        dwt = sb("dwt", [P, TAPS * 8])
        small = sb("small", [P, 128])
        att = sb("att", [P, 2, 384])
        ptb = sb("ptb", [P, 2, 384])
        ytmp = sb("ytmp", [P, 2, 512])
        thb = sb("thb", [P, 2, 514])
        with ExitStack() as split_ctx:
            xh = split_ctx.enter_context(nc.sbuf_tensor("xh", [P, KC, T], F32R))
            xl = split_ctx.enter_context(nc.sbuf_tensor("xl", [P, KC, T], F32R))
        over = sb("over", [P, 2 * KC * T])
        NSLOT = 13
        arena = sb("arena", [P, NSLOT * 1024])
        banks = ctx.enter_context(nc.psum_tensor("banks", [P, 8, 512], F32))

        def const(name):
            a, b = CONST[name]
            return cst[:, a:b]

        ident = const("ident")

        def slot(n, count=1):
            return arena[:, n * 1024:(n + count) * 1024]

        def oslot(n, count=1):
            return over[:, n * 1024:(n + count) * 1024]

        def chunks(ap):
            return ap.rearrange("p (c t) -> p c t", t=T)

        def tiles(ap):
            return ap.rearrange("p (s n) -> p s n", s=NT)

        def vcol(name, i=0):
            return vt[:, VROW[name] + i:VROW[name] + i + 1]

        MS = small[:, 0:2]
        SS = small[:, 116:120]
        RSTD, MHALF, NMAX = small[:, 2:4], small[:, 4:6], small[:, 8:24]
        DEN, ES = small[:, 24:40], small[:, 40:56]
        HSCALE, EPSG, EPSL = small[:, 72:76], small[:, 76:77], small[:, 77:78]
        HW0, HA0 = small[:, 78:82], small[:, 82:86]
        sinkb = small[:, 86:94]
        hb = small[:, 94:102]
        omu = small[:, 102:116]
        pcs = sb("pcs", [P, 32])

        ax, pooled = tiles(slot(0)), chunks(slot(1))
        sz = [chunks(slot(2 + m)) for m in range(3)]
        bq, cq, ck = chunks(slot(5)), chunks(slot(6)), chunks(slot(7))
        cv = tiles(slot(8))
        bk = chunks(arena[:, 9216:9216 + 512])
        bv = tiles(arena[:, 9216 + 512:9216 + 768])
        poolw = arena[:, 10240:10240 + 512].rearrange("p (g d) -> p g d", g=4)
        pool_m = arena[:, 10752:10752 + 1536]
        late = pool_m[:, 1024:1536]
        gate = chunks(slot(11, 2))
        merged = chunks(slot(0, 2))
        vrows = arena[:, 6 * 1024:6 * 1024 + P]
        dwrows = arena[:, 6 * 1024 + P:6 * 1024 + 3 * P]
        scratch = slot(11, 2)
        gfin = slot(5)
        band = arena[:, 4096:6144].rearrange("p (h m) -> p h m", h=8)
        extr = arena[0:8, 3 * 1024:3 * 1024 + 384]
        rT, kT, vT = chunks(slot(0)), chunks(slot(1)), chunks(slot(2))
        xwa, xg = arena[:, 3072:3072 + T], arena[:, 3072 + T:3072 + 2 * T]
        q2, k2, v2 = chunks(slot(7)), chunks(slot(8)), tiles(slot(12))
        keep = slot(9)
        lora = arena[:, 10240:10240 + 1536].rearrange("p (m n) -> p m n", m=3)
        LD, aT, gT, kk, Lc = (slot(n) for n in (4, 5, 6, 7, 8))
        rk, bonus = slot(12), oslot(3)
        Pc, Pinv, Pprev = slot(9), oslot(0), oslot(1)
        aTil, bTil, kTil, rTil = oslot(2), slot(5), slot(1), slot(0)
        bHat, kHat = slot(7), slot(4)
        An, Bn, Kn, Vn = tiles(slot(8)), tiles(slot(3)), tiles(slot(10)), tiles(slot(11))
        Z = oslot(0, 2).rearrange("p (w s h d) -> p w s h d", w=2, s=NT, h=8)
        tset = [[slot(n)[:, 512 * (i % 2):512 * (i % 2) + 512] for i, n in enumerate(ns)]
                for ns in ((2, 2, 4, 4, 7, 7), (9, 9, 12, 12, 12, 12))]
        extra_t = sb("extra_t", [P, 2, 512])
        tset[1][4], tset[1][5] = extra_t[:, 0, :], extra_t[:, 1, :]
        WT = chunks(slot(2))

        def S(c):
            place = extra_t if c < 4 else over[:, 2048:3072].rearrange("p (i n) -> p i n", i=2)
            return place[:, (c % 4) // 2, (c % 2) * 256:(c % 2) * 256 + 256]
        SA = tiles(slot(4))
        YT = chunks(slot(12))
        acc = chunks(slot(0, 2))
        upad = arena[:, 2048:2048 + 8 * (PAD + T)].rearrange("p (c t) -> p c t", t=PAD + T)
        lnsq = chunks(slot(5, 2))
        lnmean, lnsd = slot(7)[:, 0:T], slot(7)[:, T:2 * T]
        pw2b = slot(8)

        def tap_diag(i, j, tap):
            n = j * PE_TAPS + tap
            places = ((9, 10, 11), (12, 5, 6))[i % 2]
            return slot(places[n // 8])[:, (n % 8) * P:(n % 8 + 1) * P]

        filled = [E(f"filled{b}") for b in range(8)]
        emptied = [E(f"emptied{b}") for b in range(8)]

        def bank(name):
            return banks[:, PL.uses[name][0], :]

        def wait_full(eng, name):
            b, n = PL.uses[name]
            eng.wait_ge(filled[b], n + 1)

        def wait_empty(eng, name):
            b, n = PL.uses[name]
            eng.wait_ge(emptied[b], n + 1)

        def full(name):
            return filled[PL.uses[name][0]]

        def empty(name):
            return emptied[PL.uses[name][0]]

        def wait_unit_used(eng, u):
            if PL.done[u] is None:
                eng.wait_ge(E("unit_summed"), PARTIAL.index(u) + 1)
            else:
                wait_full(eng, PL.done[u])

        def wait_residual(eng, tag):
            for i in range(4):
                wait_empty(eng, f"{tag}_{i}" if tag.startswith("dn") else f"{tag}{i // 2}_{i % 2}")

        def wait_pv(eng, a):
            if a % 2:
                wait_full(eng, f"o{a // 2}")
            else:
                eng.wait_ge(E("pv_even"), a // 2 + 1)

        def head_views(a):
            kind, h = divmod(a, 8)
            hp, pair = HD * (h % 2), h // 2
            q = (bq, cq, q2)[kind][hp:hp + HD, pair, :]
            if kind == 0:
                return q, bk[hp:hp + HD, pair // 2, :], bv[:, :, HD * (h // 4):HD * (h // 4) + HD]
            return q, (ck, k2)[kind - 1][hp:hp + HD, pair, :], (cv, v2)[kind - 1][:, :, HD * h:HD * h + HD]

        def exps_done(a):
            return 3 * min(a + 1, 8) + 2 * max(0, a - 7)

        def combo_cols(g):
            tt, par = divmod(g, 2)
            return [(tt, par + 2 * i) for i in range(4)]

        block = ctx.enter_context(nc.Block())
        last_unit = {1: UID[("TH", "w_proj_c", 0, 512)], 2: UID[("N", "w_out", 512, 512)],
                     3: UID[("T", "l0_w_in_2", 0, 1536)], 4: UID[("T", "l0_w_in_2", 0, 1536)],
                     5: UID[("N", "l0_w_out_2", 512, 512)], 6: UID[("D", "l0_ffn_down_2", 3840, 0)],
                     7: UID[("T", "l1_pw1_2", 0, DM + 768)], 8: UID[("N", "l1_pw2_2", 512, 512)]}
        NLOAD = min(NU, last_unit.get(STOP, NU) + 3)

        @block.sync
        def _(sp):
            for s in range(NT):
                sp.dma_start(xn[:, s, :], A["x"][0, s * P:(s + 1) * P, :]).then_inc(E("x_loaded"), 16)
            sp.dma_start(cst[:, :], consts_d[:, 0:NKEEP]).then_inc(E("consts_loaded"), 16)
            for n in range(NLOAD):
                kind, w, r, c = UNITS[n]
                rows, cols = {"TH": (512, 512), "N": (512, 512), "D": (256, 1024)}.get(kind, (1024, 256))
                if n >= RAWS:
                    sp.wait_ge(E("lo_split"), n - RAWS + 1)
                sp.dma_start(raw[:, n % RAWS, :].rearrange("p (j n) -> p j n", n=cols),
                             mat(w)[r:r + rows, c:c + cols].rearrange("(j p) n -> p j n", p=P))\
                    .then_inc(E(f"unit_loaded{n % RAWS}"), 16)
            if STOP < 99:
                return
            sp.wait_ge(E("out_ready"), 2)
            sp.dma_start(out_d[0].rearrange("(s p) n -> p s n", p=P), xn[:, :, :]).then_inc(E("out_stored"), 16)
            sp.wait_ge(E("out_stored"), 16)

        @block.gpsimd
        def _(pool):
            nc.gpsimd.memset(MHALF, -0.5).then_inc(E("pool_consts"), 1)
            nc.gpsimd.memset(EPSG, 64e-5).then_inc(E("pool_consts"), 1)
            nc.gpsimd.memset(EPSL, 1e-5).then_inc(E("pool_consts"), 1)
            pool.wait_ge(E("pool_consts"), 1)
            norms = [0]

            def rstd(first):
                for t in range(NT):
                    pool.wait_ge(E("squares_summed"), 4 * norms[0] + (first, 4)[t])
                    nc.gpsimd.tensor_scalar(MS[:, t:t + 1], SS[:, 2 * t:2 * t + 1], SS[:, 2 * t + 1:2 * t + 2], 1e-6,
                                            ALU.add, ALU.add).then_inc(E("mean_square"), 1)
                    pool.wait_ge(E("mean_square"), 2 * norms[0] + t + 1)
                    nc.gpsimd.tensor_tensor(RSTD[:, t:t + 1], MS[:, t:t + 1], MHALF[:, 0:1], ALU.pow)\
                        .then_inc(E("rstd_ready"), 1)
                norms[0] += 1

            rstd(2)
            for name, k in VECS[1:]:
                r = VROW[name]
                pool.dma_start(vrows[r:r + k, :], vec(name).rearrange("(k c) -> k c", c=P))\
                    .then_inc(E("vectors_loaded"), 16)
            for i in range(2):
                pool.dma_start(dwrows[0:124, i * P:(i + 1) * P],
                               A["l1_dw_2"].rearrange("t (k c) -> (t k) c", c=P)[124 * i:124 * i + 124, :])\
                    .then_inc(E("vectors_loaded"), 16)
            pool.dma_start(poolw, A["pool_w"][0].rearrange("g c d -> c g d")).then_inc(E("poolw_loaded"), 16)
            pool.dma_start(sinkb, bass.AP(tensor=A["sink_logits"].tensor, offset=0, ap=[[0, P], [1, 8]]))\
                .then_inc(E("sinks_loaded"), 16)
            wait_full(pool, "n0_t2")
            wait_full(pool, "n0_t3")
            pool.dma_start(pool_m, consts_d[:, CONST["pool2"][0]:CONST["pool2"][0] + 1536])\
                .then_inc(E("pool_m_loaded"), 16)
            if STOP < 1:
                return
            pool.wait_ge(E("merged_lo"), 8)
            pool.dma_start(gfin, bass.AP(tensor=A["final_norm_g"].tensor, offset=0, ap=[[0, P], [1, DM]]))\
                .then_inc(E("gain_loaded"), 16)
            pool.dma_start(keep, consts_d[:, CONST["scan_keep"][0]:CONST["scan_keep"][1]]).then_inc(E("keep_loaded"), 16)
            pool.dma_start(extr[:, 0:257], A["l0_rel_bias_2"]).then_inc(E("rel_loaded"), 16)
            pool.wait_ge(E("rel_loaded"), 16)
            nc.gpsimd.tensor_copy(extr[:, 257:384], extr[:, 256:257].broadcast_to([8, 127])).then_inc(E("rel_extended"), 1)
            pool.wait_ge(E("rel_extended"), 1)
            pool.dma_start(ext_d, extr).then_inc(E("rel_stored"), 16)
            for i in range(2):
                for j in range(2):
                    nc.gpsimd.memset(thb[:, i, 257 * j:257 * j + 1], 0.0).then_inc(E("shift_zeroed"), 1)
            if STOP < 2:
                return
            rstd(3)
            pool.wait_ge(E("normed_natural"), 2)
            pool.wait_ge(E("rel_stored"), 16)
            pool.dma_start(band, bass.AP(tensor=ext_d.tensor, offset=1, ap=[[1, P], [384, 8], [1, T]]))\
                .then_inc(E("band_loaded"), 16)
            pool.wait_ge(E("band_loaded"), 16)
            nc.gpsimd.memset(band[0:64, :, 0:64], NEG).then_inc(E("band_ready"), 1)
            rstd(2)
            wait_full(pool, "n2_t2")
            wait_full(pool, "n2_t3")
            pool.dma_start(lora[0:64, 0, :], A["l0_w2_2"]).then_inc(E("lora_loaded"), 16)
            pool.dma_start(lora[64:128, 1, :], A["l0_a2_2"]).then_inc(E("lora_loaded"), 16)
            pool.dma_start(lora[:, 2, :], A["l0_g2_2"]).then_inc(E("lora_loaded"), 16)
            if STOP < 6:
                return
            rstd(3)
            if STOP < 7:
                return
            rstd(2)
            for c in range(8):
                nc.gpsimd.memset(upad[:, c, 0:PAD], 0.0).then_inc(E("pad_zeroed"), 1)
            pool.dma_start(pw2b, bass.AP(tensor=A["l1_pw2_b_2"].tensor, offset=0, ap=[[0, P], [1, DM]]))\
                .then_inc(E("pw2b_loaded"), 16)
            if STOP < 9:
                return
            rstd(3)
            pool.dma_start(gfin, bass.AP(tensor=A["final_norm_2"].tensor, offset=0, ap=[[0, P], [1, DM]]))\
                .then_inc(E("gain_loaded"), 16)
            rstd(2)

        @block.scalar
        def _(act):
            chain = [0]
            unit = [0]
            ysplit = [0]

            def mark(ins):
                chain[0] += 1
                ins.then_inc(E("act_steps"), 1)

            def sync():
                act.wait_ge(E("act_steps"), chain[0])

            def split(u):
                if u >= NLOAD:
                    return
                act.wait_ge(E(f"unit_loaded{u % RAWS}"), 16 * (u // RAWS + 1))
                if u >= WBUFS:
                    wait_unit_used(act, u - WBUFS)
                nc.scalar.activation(wh[:, u % WBUFS, :], raw[:, u % RAWS, :], ACT.Copy).then_inc(E("hi_split"), 1)

            def next_unit():
                split(unit[0] + 2)
                unit[0] += 1

            def copy_out(dst, name, cols=512, scale=1.0):
                wait_full(act, name)
                src = bank(name)[:, 0:cols]
                if len(dst.shape) == 3:
                    src = src.rearrange("p (a b) -> p a b", a=dst.shape[1])
                nc.scalar.activation(dst, src, ACT.Copy, scale=scale).then_inc(empty(name), 1)

            def squares(residual=None):
                order = [(0, 0), (0, 1), (1, 0), (1, 1)]
                if residual and not residual.startswith("dn"):
                    order = [(0, 0), (1, 0), (0, 1), (1, 1)]
                for t, c in order:
                    if residual:
                        wait_empty(act, f"{residual}_{2 * t + c}" if residual.startswith("dn") else f"{residual}{c}_{t}")
                    nc.scalar.activation(scratch[:, t * DM + c * 512:t * DM + c * 512 + 512],
                                         xn[:, t, 512 * c:512 * c + 512], ACT.Square, scale=DM ** -0.5,
                                         accum_out=SS[:, 2 * t + c:2 * t + c + 1]).then_inc(E("squares_summed"), 1)

            def split_norm(tag):
                for q in range(4):
                    wait_full(act, f"{tag}_t{q}")
                    for i in range(2):
                        k = 2 * q + i
                        nc.scalar.activation(xh[:, k, :], bank(f"{tag}_t{q}")[:, i * T:(i + 1) * T], ACT.Copy,
                                             scale=vcol(GAIN[tag], k)).then_inc(E("norm_hi"), 1)

            def silu_tanh(name, k):
                wait_full(act, name)
                if k >= 2:
                    wait_empty(act, f"{'abc'[k // 2 - 1]}z{k % 2}")
                nc.scalar.activation(thb[:, k % 2, 0:512], bank(name), ACT.Tanh, scale=0.5).then_inc(E("silu_tanh"), 1)

            def split_y(chunk, n, use):
                k = ysplit[0]
                ysplit[0] += 1
                wait_empty(act, use)
                nc.scalar.activation(yh[:, chunk:chunk + n, :], chunks(ytmp[:, k % 2, 0:n * T]), ACT.Copy)\
                    .then_inc(E("y_hi"), 1)

            def exps(a):
                act.wait_ge(E("neg_max"), a + 1)
                k = a % 8
                m = NMAX[:, 2 * k:2 * k + 2]
                for i, (lo, hi) in enumerate(((0, P), (P, 384))):
                    nc.scalar.activation(att[:, a % 2, lo:hi], att[:, a % 2, lo:hi], ACT.Exp, bias=m[:, i:i + 1],
                                         accum_out=DEN[:, 2 * k + i:2 * k + i + 1]).then_inc(E("exp_done"), 1)
                if a < 8:
                    nc.scalar.activation(ES[:, 2 * k:2 * k + 2], m, ACT.Exp, bias=sinkb[:, a:a + 1])\
                        .then_inc(E("exp_done"), 1)

            def heads_step(s, base, n, with_unit=True):
                if 1 <= s <= n:
                    a = base + s - 1
                    wait_full(act, f"pt{a}")
                    if a >= 2:
                        wait_pv(act, a - 2)
                    nc.scalar.activation(ptb[:, a % 2, :], bank(f"pt{a}")[:, 0:384], ACT.Copy).then_inc(emptied[4], 1)
                if with_unit:
                    next_unit()
                if s < n:
                    exps(base + s)
                a = base + s - 2
                if s >= 2 and a % 2:
                    if base == 0:
                        split_y(4 + a // 2, 1, f"o{a // 2}")
                    else:
                        wait_full(act, f"o{a // 2}")
                        nc.scalar.activation(yh[:, 4 + (a - base) // 2, :], bank(f"o{a // 2}")[:, 0:T], ACT.Copy)\
                            .then_inc(E("o_hi"), 1)

            act.dma_start(vrows[0:8, :], vec("norm_g").rearrange("(k c) -> k c", c=P)).then_inc(E("norm_g_loaded"), 16)
            act.wait_ge(E("x_loaded"), 32)
            squares()
            split(0)
            copy_out(vt[:, 0:8], "vec0", 8)
            wait_empty(act, "vec0")
            split_norm("n0")
            split(1)
            next_unit()
            next_unit()
            copy_out(ax[:, 0, :], "ax0")
            copy_out(ax[:, 1, :], "ax1")
            for i in range(2):
                next_unit()
                silu_tanh(f"az{i}", i)
            wait_full(act, "vec1")
            mark(nc.scalar.activation(dwt[:, :], bank("vec1")[:, 0:TAPS * 8], ACT.Copy))
            nc.scalar.activation(vt[:, 8:NVROWS], bank("vec1")[:, 256 + 8:256 + NVROWS], ACT.Copy)\
                .then_inc(empty("vec1"), 1)
            wait_empty(act, "vec1")
            a, b = VROW["pool_scale"], VROW["l0_w0_2"]
            mark(nc.scalar.activation(HSCALE, vt[:, a:a + 4], ACT.Copy, scale=0.5))
            mark(nc.scalar.activation(HW0, vt[:, b:b + 4], ACT.Copy, scale=0.5))
            mark(nc.scalar.activation(HA0, vt[:, b + 4:b + 8], ACT.Copy, scale=0.5))
            b = VROW["l1_pw1_b_2"]
            mark(nc.scalar.activation(hb, vt[:, b + 8:b + 16], ACT.Copy, scale=0.5))
            b = VROW["l0_shift_mu_2"]
            nc.scalar.activation(omu, vt[:, b:b + 14], ACT.Copy, scale=-1.0, bias=1.0).then_inc(E("vec_cols_ready"), 1)
            for i in range(2):
                copy_out(pooled[:, 2 * i:2 * i + 2, :], f"pool{i}")
            for i in range(2):
                split_y(2 * i, 2, f"mix{i}")
            for i in range(2):
                next_unit()
                copy_out(bq[:, 2 * i:2 * i + 2, :], f"bq{i}")
            next_unit()
            wait_full(act, "bk")
            for g in range(2):
                r = slice(g * HD, (g + 1) * HD)
                ins = nc.scalar.activation(bk[r, g, :], bank("bk")[r, 0:T], ACT.Copy)
                if g:
                    ins.then_inc(empty("bk"), 1)
                else:
                    mark(ins)
            copy_out(bv, "bv", 256)
            wait_empty(act, "bk")
            sync()
            for g in range(2):
                act.dma_start(bk[(1 - g) * HD:(2 - g) * HD, g, :], bk[g * HD:(g + 1) * HD, g, :])\
                    .then_inc(E("keys_doubled"), 16)
            act.wait_ge(E("sinks_loaded"), 16)
            heads = iter(range(18))

            def step():
                s = next(heads, None)
                if s is None:
                    next_unit()
                else:
                    heads_step(s, 0, 16)

            next_unit()
            for i in range(2):
                silu_tanh(f"bz{i}", 2 + i)
                step()
            for i in range(2):
                copy_out(cq[:, 2 * i:2 * i + 2, :], f"cq{i}")
                step()
            for i in range(2):
                copy_out(ck[:, 2 * i:2 * i + 2, :], f"ck{i}")
                step()
            step()
            copy_out(cv[:, 0, :], "cv0")
            copy_out(cv[:, 1, :], "cv1")
            step()
            for i in range(2):
                silu_tanh(f"cz{i}", 4 + i)
                step()
            for m in range(3):
                for i in range(4):
                    name = f"g{m}_{i}"
                    wait_full(act, name)
                    if m == 0:
                        wait_full(act, "mix1")
                    else:
                        wait_empty(act, f"pr{m - 1}_{i}")
                    nc.scalar.activation(gate[:, 2 * i:2 * i + 2, :], chunks(bank(name)), ACT.Tanh, scale=0.5)\
                        .then_inc(empty(name), 1)
                    step()
                for i in range(2):
                    step()
            for k in range(8):
                act.wait_ge(E("merged"), k // 2 + 1)
                nc.scalar.activation(xh[:, k, :], merged[:, k, :], ACT.Copy, scale=0.5).then_inc(E("merged_hi"), 1)
            if STOP < 2:
                return
            for _ in range(3):
                next_unit()
            squares("wo")
            act.wait_ge(E("normed_natural"), 2)
            squares()
            split_norm("n2")
            if STOP < 3:
                return
            for i in range(2):
                next_unit()
                copy_out(q2[:, 2 * i:2 * i + 2, :], f"q2_{i}")
            for i in range(2):
                next_unit()
                copy_out(k2[:, 2 * i:2 * i + 2, :], f"k2_{i}")
            next_unit()
            next_unit()
            copy_out(v2[:, 0, :], "v2_0")
            copy_out(v2[:, 1, :], "v2_1")
            act.wait_ge(E("shift_zeroed"), 4)
            next_unit()
            for i in range(7):
                name = f"rw{i}"
                wait_full(act, name)
                if i >= 2:
                    wait_empty(act, f"rw{i - 2}")
                for j in range(2):
                    nc.scalar.activation(thb[:, i % 2, 257 * j + 1:257 * j + 257], bank(name)[:, j * T:(j + 1) * T],
                                         ACT.Copy, scale=vcol("l0_shift_mu_2", 2 * i + j)).then_inc(E("mu_part"), 1)
                heads_step(i, 16, 8, with_unit=i < 6)
            for s in range(7, 10):
                heads_step(s, 16, 8, with_unit=False)
            if STOP < 4:
                return
            wait_empty(act, "rw6")
            nc.scalar.activation(xwa[0:64, :], xwa[0:64, :], ACT.Tanh).then_inc(E("xw_tanh"), 1)
            nc.scalar.activation(xg, xg, ACT.Tanh, scale=0.5).then_inc(E("xg_tanh"), 1)
            wait_empty(act, "sc22")
            wait_empty(act, "sc23")
            for tag, dst, bias in (("z", LD, HW0), ("a", aT, HA0)):
                for i in range(2):
                    wait_full(act, f"{tag}{i}")
                    for j in range(2):
                        c = 2 * i + j
                        ins = nc.scalar.activation(chunks(dst)[:, c, :], bank(f"{tag}{i}")[:, j * T:(j + 1) * T],
                                                   ACT.Tanh, scale=0.5, bias=bias[:, c:c + 1])
                        if j:
                            ins.then_inc(empty(f"{tag}{i}"), 1)
                        else:
                            mark(ins)
            for i in range(2):
                copy_out(gT[:, 512 * i:512 * i + 512], f"gg{i}")
            wait_full(act, "pt23")
            wait_pv(act, 23)
            for c in range(4):
                mark(nc.scalar.activation(chunks(kk)[:, c, :], kT[:, c, :], ACT.Copy, scale=vcol("l0_k_k_2", c)))
            sync()
            nc.scalar.activation(rk, kk, ACT.Square).then_inc(E("kk_squares"), 1)
            for i in range(2):
                wait_full(act, f"kn{i}")
                nc.scalar.activation(Pinv[:, 512 * i:512 * i + 512], bank(f"kn{i}"), ACT.Sqrt).then_inc(empty(f"kn{i}"), 1)
            act.wait_ge(E("kk_ready"), 1)
            act.wait_ge(E("cumulated"), 1)
            nc.scalar.activation(Pc, Lc, ACT.Exp).then_inc(E("decay_exps"), 1)
            nc.scalar.activation(Pinv, Lc, ACT.Exp, scale=-1.0).then_inc(E("decay_exps"), 1)
            act.wait_ge(E("prev_log"), 1)
            nc.scalar.activation(Pprev, Pprev, ACT.Exp).then_inc(E("decay_exps"), 1)
            nc.scalar.activation(pcs[:, :], Lc[:, C - 1::C], ACT.Exp).then_inc(E("decay_exps"), 1)
            for name, dst in (("an", An), ("bn", Bn), ("kn", Kn), ("vn", Vn)):
                copy_out(dst[:, 0, :], f"nat_{name}0")
                copy_out(dst[:, 1, :], f"nat_{name}1")
            for pair in range(2):
                for name, who in INVERSE:
                    for g in (2 * pair, 2 * pair + 1):
                        if who != "act":
                            continue
                        ts = tset[g % 2]
                        use = f"{name}_{g}"
                        if name == "AV":
                            wait_full(act, use)
                            tt, par = divmod(g, 2)
                            nc.scalar.activation(Z[:, 1, tt, par::2, :],
                                                 bank(use)[:, 0:256].rearrange("p (h d) -> p h d", h=4), ACT.Copy)\
                                .then_inc(empty(use), 1)
                        else:
                            copy_out(ts[{"N2": 5, "N4": 0, "D4": 1, "D8": 5, "Z1": 0, "EZ": 1}[name]], use)
            for i in range(2):
                copy_out(WT[:, :, i * P:(i + 1) * P], f"wt{i}")
            for i in range(2):
                copy_out(YT[:, :, i * P:(i + 1) * P], f"y{i}")
            act.wait_ge(E("centred"), 1)
            nc.scalar.activation(slot(7), slot(2), ACT.Square).then_inc(E("gn_squares"), 1)
            for i in range(2):
                wait_full(act, f"gv{i}")
                nc.scalar.activation(slot(9)[:, 512 * i:512 * i + 512], bank(f"gv{i}"), ACT.Sqrt, scale=1.0 / HD,
                                     bias=EPSG).then_inc(empty(f"gv{i}"), 1)
            act.wait_ge(E("rwkv_out"), 1)
            nc.scalar.activation(yh[:, 0:4, :], chunks(slot(2)), ACT.Copy).then_inc(E("rwkv_hi"), 1)
            if STOP < 5:
                return
            for _ in range(4):
                next_unit()

            def ffn(tag, k0, residual):
                squares(residual)
                split_norm(tag)
                for i in range(FF_STEPS + 1):
                    if i < FF_STEPS:
                        next_unit()
                        k = k0 + i
                        name = f"up{tag}_{i}"
                        wait_full(act, name)
                        if k >= 2:
                            act.wait_ge(E("hidden_lo"), k - 1)
                        nc.scalar.activation(ytmp[:, k % 2, :], bank(name), ACT.Relu).then_inc(empty(name), 1)
                        wait_empty(act, name)
                        if i >= 3:
                            wait_unit_used(act, UID[("D", DOWN[tag], 256 * (i - 3), 0)])
                        nc.scalar.activation(yh[:, 2 * (i % 3):2 * (i % 3) + 2, :], chunks(ytmp[:, k % 2, :]),
                                             ACT.Square).then_inc(E("hidden_hi"), 1)
                    if i >= 1:
                        next_unit()

            if STOP < 6:
                return
            ffn("f0", 0, "wp")
            if STOP < 7:
                wait_residual(act, "dnf0")
                return
            squares("dnf0")
            split_norm("n4")
            def tap_diagonals(i):
                if i >= 2:
                    wait_full(act, f"taps{i - 2}")
                for j in range(2):
                    for tap in range(PE_TAPS):
                        w = tap * 8 + 2 * i + j
                        nc.scalar.activation(tap_diag(i, j, tap), ident, ACT.Copy, scale=dwt[:, w:w + 1])\
                            .then_inc(E("diagonals"), 1)

            def taps_out(i):
                wait_full(act, f"taps{i}")
                if i:
                    act.wait_ge(E("convolved"), 2 * i)
                for j in range(2):
                    ins = nc.scalar.activation(ytmp[:, 1, j * T:(j + 1) * T], bank(f"taps{i}")[:, j * T:(j + 1) * T],
                                               ACT.Identity, scale=0.5, bias=vcol("l1_dw_b_2", 2 * i + j))
                    if j:
                        ins.then_inc(empty(f"taps{i}"), 1)
                    else:
                        mark(ins)

            tap_diagonals(0)
            for i in range(4):
                next_unit()
                if i:
                    act.wait_ge(E("glu"), i)
                for tag, dst, fn, scale, bias in (("pa", ytmp, ACT.Identity, 1.0, lambda c: vcol("l1_pw1_b_2", c)),
                                                  ("pb", thb, ACT.Tanh, 0.5, lambda c: hb[:, c:c + 1])):
                    if tag == "pb":
                        next_unit()
                    wait_full(act, f"{tag}{i}")
                    for j in range(2):
                        ins = nc.scalar.activation(dst[:, 0, j * T:(j + 1) * T], bank(f"{tag}{i}")[:, j * T:(j + 1) * T],
                                                   fn, scale=scale, bias=bias(2 * i + j))
                        if j:
                            ins.then_inc(empty(f"{tag}{i}"), 1)
                        else:
                            mark(ins)
                if i:
                    taps_out(i - 1)
                if i < 3:
                    tap_diagonals(i + 1)
            taps_out(3)
            if STOP < 8:
                return
            wait_full(act, "lnm")
            nc.scalar.activation(lnmean, bank("lnm")[:, 0:T], ACT.Copy, scale=1.0 / DM).then_inc(empty("lnm"), 1)
            for k in range(4):
                act.wait_ge(E("ln_centred"), k + 1)
                nc.scalar.activation(lnsq[:, 2 * k:2 * k + 2, :], acc[:, 2 * k:2 * k + 2, :], ACT.Square)\
                    .then_inc(E("ln_squares"), 1)
            wait_full(act, "lnv")
            nc.scalar.activation(lnsd, bank("lnv")[:, 0:T], ACT.Sqrt, scale=1.0 / DM, bias=EPSL).then_inc(empty("lnv"), 1)
            for k in range(4):
                act.wait_ge(E("ln_divided"), k + 1)
                for c in (2 * k, 2 * k + 1):
                    mark(nc.scalar.activation(acc[:, c, :], acc[:, c, :], ACT.Identity, scale=vcol("l1_ln_w_2", c),
                                              bias=vcol("l1_ln_b_2", c)))
                sync()
                nc.scalar.activation(lnsq[:, 2 * k:2 * k + 2, :], acc[:, 2 * k:2 * k + 2, :], ACT.Tanh, scale=0.5)\
                    .then_inc(E("ln_tanh"), 1)
            for k in range(4):
                act.wait_ge(E("ln_silu"), k + 1)
                nc.scalar.activation(xh[:, 2 * k:2 * k + 2, :], lnsq[:, 2 * k:2 * k + 2, :], ACT.Copy, scale=0.5)\
                    .then_inc(E("ln_hi"), 1)
            for _ in range(4):
                next_unit()
            if STOP < 9:
                return
            ffn("f1", FF_STEPS, "pw")
            squares("dnf1")

        @block.vector
        def _(dve):
            chain = [0]
            unit = [0]
            ysplit = [0]

            def mark(ins):
                chain[0] += 1
                ins.then_inc(E("dve_steps"), 1)
                return chain[0]

            def sync(n=None):
                dve.wait_ge(E("dve_steps"), n or chain[0])

            def split(u):
                if u >= NLOAD:
                    return
                dve.wait_ge(E("hi_split"), u + 1)
                if u >= WBUFS:
                    wait_unit_used(dve, u - WBUFS)
                nc.vector.tensor_tensor(wl[:, u % WBUFS, :], raw[:, u % RAWS, :], wh[:, u % WBUFS, :].bitcast(F32),
                                        ALU.subtract).then_inc(E("lo_split"), 1)

            def next_unit():
                split(unit[0] + 2)
                unit[0] += 1

            norms = [0]
            xsplits = [0]

            def scale_rows(natural_gain=False):
                for s in range(NT):
                    dve.wait_ge(E("rstd_ready"), norms[0] + s + 1)
                    if natural_gain:
                        nc.vector.scalar_tensor_tensor(out=xn[:, s, :], in0=xn[:, s, :], scalar=RSTD[:, s:s + 1],
                                                       in1=gfin, op0=ALU.mult, op1=ALU.mult)\
                            .then_inc(E("out_ready" if natural_gain == 2 else "normed_natural"), 1)
                    else:
                        nc.vector.tensor_scalar(scratch[:, s * DM:(s + 1) * DM], xn[:, s, :], RSTD[:, s:s + 1], None,
                                                ALU.mult).then_inc(E("rows_scaled"), 1)
                norms[0] += NT

            def split_norm(tag):
                for q in range(4):
                    xsplits[0] += 2
                    dve.wait_ge(E("norm_hi"), xsplits[0])
                    for i in range(2):
                        k = 2 * q + i
                        ins = nc.vector.scalar_tensor_tensor(
                            out=xl[:, k, :], in0=bank(f"{tag}_t{q}")[:, i * T:(i + 1) * T], scalar=vcol(GAIN[tag], k),
                            in1=xh[:, k, :].bitcast(F32), op0=ALU.mult, op1=ALU.subtract)
                        if i:
                            ins.then_inc(empty(f"{tag}_t{q}"), 1)
                        else:
                            mark(ins)

            def silu(name, k):
                dve.wait_ge(E("silu_tanh"), k + 1)
                nc.vector.scalar_tensor_tensor(out=sz[k // 2][:, 2 * (k % 2):2 * (k % 2) + 2, :],
                                               in0=chunks(thb[:, k % 2, 0:512]), scalar=1.0, in1=chunks(bank(name)),
                                               op0=ALU.add, op1=ALU.mult).then_inc(empty(name), 1)

            def split_y(chunk, n):
                k = ysplit[0]
                ysplit[0] += 1
                dve.wait_ge(E("y_hi"), k + 1)
                nc.vector.tensor_tensor(yl[:, chunk:chunk + n, :], chunks(ytmp[:, k % 2, 0:n * T]),
                                        yh[:, chunk:chunk + n, :].bitcast(F32), ALU.subtract).then_inc(E("y_lo"), 1)

            def scores(a):
                k = a % 8
                buf = att[:, a % 2, :]
                wait_full(dve, f"sc{a}")
                if a >= 2:
                    wait_full(dve, f"pt{a - 2}")
                src = bank(f"sc{a}")
                if a < 16:
                    mask = const("mask_swa" if a < 8 else "mask_causal")
                    nc.vector.scalar_tensor_tensor(out=buf, in0=src[:, 0:384], scalar=SCALE, in1=mask, op0=ALU.mult,
                                                   op1=ALU.add).then_inc(empty(f"sc{a}"), 1)
                else:
                    b = band[:, a - 16, :]
                    mark(nc.vector.scalar_tensor_tensor(out=buf[:, 0:P], in0=src[:, 0:P], scalar=SCALE,
                                                        in1=b[:, P - 1::-1], op0=ALU.mult, op1=ALU.add))
                    nc.vector.scalar_tensor_tensor(out=buf[:, P:384], in0=src[:, P:384], scalar=SCALE,
                                                   in1=b[:, T - 1::-1], op0=ALU.mult, op1=ALU.add)\
                        .then_inc(empty(f"sc{a}"), 1)
                wait_empty(dve, f"sc{a}")
                mark(nc.vector.reduce_max(ES[:, 2 * k:2 * k + 1], buf[:, 0:P], AX_X))
                mark(nc.vector.reduce_max(ES[:, 2 * k + 1:2 * k + 2], buf[:, P:384], AX_X))
                sync()
                if a < 8:
                    nc.vector.tensor_scalar(NMAX[:, 2 * k:2 * k + 2], ES[:, 2 * k:2 * k + 2], sinkb[:, a:a + 1], -1.0,
                                            ALU.max, ALU.mult).then_inc(E("neg_max"), 1)
                else:
                    nc.vector.tensor_scalar(NMAX[:, 2 * k:2 * k + 2], ES[:, 2 * k:2 * k + 2], -1.0, None, ALU.mult)\
                        .then_inc(E("neg_max"), 1)

            def probabilities(a):
                k = a % 8
                dve.wait_ge(E("exp_done"), exps_done(a))
                den = DEN[:, 2 * k:2 * k + 2]
                if a < 8:
                    mark(nc.vector.tensor_tensor(den, den, ES[:, 2 * k:2 * k + 2], ALU.add))
                    sync()
                mark(nc.vector.reciprocal(den, den))
                sync()
                for i, (lo, hi) in enumerate(((0, P), (P, 384))):
                    nc.vector.tensor_scalar(att[:, a % 2, lo:hi], att[:, a % 2, lo:hi], den[:, i:i + 1], None, ALU.mult)\
                        .then_inc(E("probs_ready"), 1)

            def heads_step(s, base, n):
                if s < n:
                    scores(base + s)
                a = base + s - 2
                if s >= 2 and a % 2:
                    pair = a // 2
                    if base == 0:
                        k = ysplit[0]
                        wait_full(dve, f"o{pair}")
                        nc.vector.scalar_tensor_tensor(out=ytmp[:, k % 2, 0:T], in0=bank(f"o{pair}")[:, 0:T], scalar=0.5,
                                                       in1=sz[1 + pair // 4][:, pair % 4, :], op0=ALU.mult, op1=ALU.mult)\
                            .then_inc(empty(f"o{pair}"), 1)
                        split_y(4 + pair, 1)
                    else:
                        c = 4 + pair - base // 2
                        dve.wait_ge(E("o_hi"), pair - base // 2 + 1)
                        nc.vector.tensor_tensor(yl[:, c, :], bank(f"o{pair}")[:, 0:T], yh[:, c, :].bitcast(F32),
                                                ALU.subtract).then_inc(empty(f"o{pair}"), 1)

            def heads_after(s, base, n):
                if s < n:
                    probabilities(base + s)

            scale_rows()
            split_norm("n0")
            split(0)
            split(1)
            next_unit()
            next_unit()
            for i in range(2):
                next_unit()
                silu(f"az{i}", i)
            dve.wait_ge(E("vec_cols_ready"), 1)
            for i in range(2):
                wait_full(dve, f"mix{i}")
                for j in range(2):
                    g = 2 * i + j
                    ins = nc.vector.scalar_tensor_tensor(
                        out=ytmp[:, i, j * T:(j + 1) * T], in0=bank(f"mix{i}")[:, j * T:(j + 1) * T],
                        scalar=HSCALE[:, g:g + 1], in1=sz[0][:, g, :], op0=ALU.mult, op1=ALU.mult)
                    if j:
                        ins.then_inc(empty(f"mix{i}"), 1)
                    else:
                        mark(ins)
                split_y(2 * i, 2)
            for i in range(3):
                next_unit()
            head = [0]

            def step():
                if head[0] < 18:
                    heads_step(head[0], 0, 16)

            def after():
                next_unit()
                heads_after(head[0], 0, 16)
                head[0] += 1

            next_unit()
            for i in range(2):
                silu(f"bz{i}", 2 + i)
                step()
                after()
            for i in range(6):
                step()
                after()
            for i in range(2):
                silu(f"cz{i}", 4 + i)
                step()
                after()
            for m in range(3):
                for i in range(4):
                    step()
                    after()
                for i in range(2):
                    step()
                    for j in range(2):
                        q = 2 * i + j
                        name = f"pr{m}_{q}"
                        wait_full(dve, name)
                        wait_empty(dve, f"g{m}_{q}")
                        dst = merged[:, 2 * q:2 * q + 2, :] if m == 0 else chunks(thb[:, q % 2, 0:512])
                        nc.vector.scalar_tensor_tensor(out=dst, in0=gate[:, 2 * q:2 * q + 2, :], scalar=1.0,
                                                       in1=chunks(bank(name)), op0=ALU.add, op1=ALU.mult)\
                            .then_inc(empty(name), 1)
                        if m:
                            wait_empty(dve, name)
                            if m == 1:
                                wait_empty(dve, f"pr0_{q}")
                            else:
                                dve.wait_ge(E("gated"), q + 1)
                            nc.vector.tensor_tensor(merged[:, 2 * q:2 * q + 2, :], merged[:, 2 * q:2 * q + 2, :], dst,
                                                    ALU.add).then_inc(E("merged" if m == 2 else "gated"), 1)
                    after()
            for k in range(8):
                dve.wait_ge(E("merged_hi"), k + 1)
                nc.vector.scalar_tensor_tensor(out=xl[:, k, :], in0=merged[:, k, :], scalar=0.5,
                                               in1=xh[:, k, :].bitcast(F32), op0=ALU.mult, op1=ALU.subtract)\
                    .then_inc(E("merged_lo"), 1)
            if STOP < 2:
                return
            def add_residual(tag, split_before=0):
                for c in range(2):
                    for i in range(2):
                        if 2 * c + i >= split_before:
                            next_unit()
                    for s in range(NT):
                        name = f"{tag}{c}_{s}"
                        wait_full(dve, name)
                        nc.vector.tensor_tensor(xn[:, s, 512 * c:512 * c + 512], xn[:, s, 512 * c:512 * c + 512],
                                                bank(name), ALU.add).then_inc(empty(name), 1)

            add_residual("wo", split_before=1)
            dve.wait_ge(E("gain_loaded"), 16)
            scale_rows(1)
            scale_rows()
            split_norm("n2")
            if STOP < 3:
                return
            for i in range(6):
                next_unit()
            dve.wait_ge(E("band_ready"), 1)
            next_unit()
            for i in range(7):
                dve.wait_ge(E("mu_part"), 2 * i + 2)
                name = f"rw{i}"
                for j in range(2):
                    c = 2 * i + j
                    dst = (rT, kT, vT)[c // 4][:, c % 4, :] if c < 12 else (xwa, xg)[c - 12]
                    ins = nc.vector.scalar_tensor_tensor(
                        out=dst, in0=bank(name)[:, j * T:(j + 1) * T], scalar=omu[:, c:c + 1],
                        in1=thb[:, i % 2, 257 * j:257 * j + T], op0=ALU.mult, op1=ALU.add)
                    if j:
                        ins.then_inc(empty(name), 1)
                    else:
                        mark(ins)
                heads_step(i, 16, 8)
                if i < 6:
                    next_unit()
                heads_after(i, 16, 8)
            for s in range(7, 10):
                heads_step(s, 16, 8)
                heads_after(s, 16, 8)
            if STOP < 4:
                return
            mark(nc.vector.tensor_scalar(xg, xg, 1.0, 0.5, ALU.add, ALU.mult)) if False else None
            dve.wait_ge(E("xg_tanh"), 1)
            nc.vector.tensor_scalar(xg, xg, 1.0, 0.5, ALU.add, ALU.mult).then_inc(E("xg_ready"), 1)
            wait_empty(dve, "z1")
            mark(nc.vector.tensor_scalar(LD, LD, 1.0, -0.5 * DECAY, ALU.add, ALU.mult))
            wait_empty(dve, "a1")
            mark(nc.vector.tensor_scalar(aT, aT, 1.0, 0.5, ALU.add, ALU.mult))
            dve.wait_ge(E("keep_loaded"), 16)
            sync()
            nc.vector.tensor_tensor_scan(Lc, keep, LD, 0.0, ALU.mult, ALU.add).then_inc(E("cumulated"), 1)
            wait_empty(dve, "kn0")
            wait_empty(dve, "kn1")
            mark(nc.vector.tensor_scalar(Pinv, Pinv, 1e-12, None, ALU.max))
            sync()
            mark(nc.vector.reciprocal(Pinv, Pinv))
            sync()
            nc.vector.tensor_tensor(kk, kk, Pinv, ALU.mult).then_inc(E("kk_ready"), 1)
            for c in range(4):
                mark(nc.vector.tensor_scalar(chunks(rk)[:, c, :], chunks(aT)[:, c, :], 1.0, vcol("l0_k_a_2", c),
                                             ALU.subtract, ALU.mult))
            dve.wait_ge(E("cumulated"), 1)
            mark(nc.vector.tensor_tensor(Pprev, Lc, LD, ALU.subtract)).__class__ if False else None
            nc.vector.tensor_tensor(Pprev, Lc, LD, ALU.subtract).then_inc(E("prev_log"), 1)
            sync()
            mark(nc.vector.scalar_tensor_tensor(out=slot(1), in0=rk, scalar=1.0, in1=slot(1), op0=ALU.add, op1=ALU.mult))
            sync()
            mark(nc.vector.tensor_tensor(rk, slot(0), slot(1), ALU.mult))
            sync()
            for c in range(4):
                nc.vector.tensor_scalar(chunks(rk)[:, c, :], chunks(rk)[:, c, :], vcol("l0_r_k_2", c), None, ALU.mult)\
                    .then_inc(E("bonus_terms"), 1)
            dve.wait_ge(E("decay_exps"), 4)
            nc.vector.scalar_tensor_tensor(out=aTil, in0=kk, scalar=-1.0, in1=Pprev, op0=ALU.mult, op1=ALU.mult)\
                .then_inc(E("scaled_keys"), 1)
            dve.wait_ge(E("kk_ready"), 1)
            mark(nc.vector.tensor_tensor(aT, aT, kk, ALU.mult))
            mark(nc.vector.tensor_tensor(slot(1), slot(1), Pinv, ALU.mult))
            sync()
            nc.vector.tensor_tensor(bTil, aT, Pinv, ALU.mult).then_inc(E("scaled_keys"), 1)
            dve.wait_ge(E("scaled_keys"), 2)

            def by_chunk(ap):
                return ap.rearrange("p (c t) -> p c t", t=C)

            pcb = pcs[:, :].rearrange("p (c o) -> p c o", o=1).broadcast_to([P, 32, C])
            nc.vector.tensor_tensor(by_chunk(bHat), by_chunk(bTil), pcb, ALU.mult).then_inc(E("scaled_keys"), 1)
            nc.vector.tensor_tensor(by_chunk(kHat), by_chunk(kTil), pcb, ALU.mult).then_inc(E("scaled_keys"), 1)
            nc.vector.tensor_tensor(rTil, rTil, Pc, ALU.mult).then_inc(E("scaled_keys"), 1)
            for i in range(2):
                wait_full(dve, f"bo{i}")
                nc.vector.tensor_tensor(bonus[:, 512 * i:512 * i + 512], bank(f"bo{i}"), slot(2)[:, 512 * i:512 * i + 512],
                                        ALU.mult).then_inc(empty(f"bo{i}"), 1)
            wait_empty(dve, "bo1")
            wait_empty(dve, "nat_vn1")

            def four(ap):
                return ap.rearrange("p (h t) -> p h t", h=4)

            def masked(dst, use, mask, last=True):
                m = const(mask).rearrange("p (o t) -> p o t", o=1).broadcast_to([P, 4, P])
                ins = nc.vector.tensor_tensor(four(dst), four(bank(use)), m, ALU.mult)
                if last:
                    ins.then_inc(empty(use), 1)
                else:
                    mark(ins)

            for pair in range(2):
                for name, who in INVERSE:
                    for g in (2 * pair, 2 * pair + 1):
                        if who != "dve":
                            continue
                        use = f"{name}_{g}"
                        ts = tset[g % 2]
                        wait_full(dve, use)
                        if name == "GN":
                            if pair:
                                wait_empty(dve, f"ZZ_{g - 2}")
                            masked(ts[0], use, "up16", last=False)
                            masked(ts[2], use, "cross")
                            sync()
                            idb = ident.rearrange("p (o t) -> p o t", o=1).broadcast_to([P, 4, P])
                            nc.vector.tensor_tensor(four(ts[4]), four(ts[0]), idb, ALU.add).then_inc(E("series_begun"), 1)
                        elif name == "GA":
                            masked(ts[3], use, "up32")
                        elif name == "GD":
                            masked(ts[1], use, "low16")
                        elif name == "D2":
                            nc.vector.tensor_copy(ts[3], bank(use)).then_inc(empty(use), 1)
                        elif name in ("X2", "X4", "X8"):
                            if name == "X2":
                                dve.wait_ge(E("series_begun"), g + 1)
                            else:
                                wait_empty(dve, f"X{int(name[1]) // 2}_{g}")
                            nc.vector.tensor_tensor(ts[4], ts[4], bank(use), ALU.add).then_inc(empty(use), 1)
                        elif name == "ZZ":
                            tt, par = divmod(g, 2)
                            wait_empty(dve, f"Z1_{g}")
                            nc.vector.tensor_tensor(Z[:, :, tt, par::2, :].rearrange("p w h d -> p h w d"),
                                                    bank(use).rearrange("p (h w d) -> p h w d", h=4, w=2),
                                                    ts[0].rearrange("p (h w d) -> p h w d", h=4, w=2), ALU.add)\
                                .then_inc(empty(use), 1)
            nc.vector.memset(S(0), 0.0).then_inc(E("state_zeroed"), 1)
            dve.wait_ge(E("state_zeroed"), 1)
            for c in range(NCH):
                tt, pb = c // 4, 32 * (c % 4)
                if c < NCH - 1:
                    if c:
                        wait_empty(dve, f"st{c - 1}")
                    pc1 = pcs[:, c::NCH].rearrange("p (c o) -> p c o", o=1).broadcast_to([P, 4, HD])
                    decayed = thb[:, 0, 0:256].rearrange("p (c d) -> p c d", c=4)
                    if c:
                        wait_empty(dve, f"st{c - 1}")
                    mark(nc.vector.tensor_tensor(decayed, S(c).rearrange("p (c d) -> p c d", c=4), pc1, ALU.mult))
                if c == 0:
                    wait_empty(dve, "wt1")
                for par, tag in enumerate(("sae", "sao")):
                    wait_full(dve, f"{tag}{c}")
                    dst = SA[pb:pb + C, tt, :].rearrange("p (h d) -> p h d", h=8)[:, par::2, :]
                    nc.vector.tensor_tensor(dst, bank(f"{tag}{c}")[pb:pb + C, 0:256].rearrange("p (h d) -> p h d", h=4),
                                            Z[pb:pb + C, 1, tt, par::2, :], ALU.add).then_inc(empty(f"{tag}{c}"), 1)
                if c < NCH - 1:
                    wait_full(dve, f"st{c}")
                    sync()
                    nc.vector.tensor_tensor(S(c + 1), bank(f"st{c}")[:, 0:256], thb[:, 0, 0:256], ALU.add)\
                        .then_inc(empty(f"st{c}"), 1)
            for g in range(4):
                for tag, off in (("A3", 0), ("A4", 512)):
                    use = f"{tag}_{g}"
                    wait_full(dve, use)
                    if g >= 2:
                        wait_full(dve, "y0")
                    masked(slot(7 if g % 2 == 0 else 9)[:, off:off + 512], use, "upinc32")
            wait_empty(dve, "y1")
            wait_empty(dve, "y0")
            for i in range(2):
                wait_full(dve, f"gm{i}")
                nc.vector.scalar_tensor_tensor(out=slot(2)[:, 512 * i:512 * i + 512], in0=bank(f"gm{i}"), scalar=-1.0 / HD,
                                               in1=slot(12)[:, 512 * i:512 * i + 512], op0=ALU.mult, op1=ALU.add)\
                    .then_inc(empty(f"gm{i}"), 1)
            wait_empty(dve, "gm0")
            wait_empty(dve, "gm1")
            mark(nc.vector.tensor_copy(small[:, 120:121], slot(2)[:, 0:1]))
            nc.vector.tensor_copy(small[:, 121:122], slot(2)[:, 512:513]).then_inc(E("centred"), 1)
            wait_empty(dve, "gv0")
            wait_empty(dve, "gv1")
            mark(nc.vector.reciprocal(slot(9), slot(9)))
            sync()
            mark(nc.vector.tensor_tensor(slot(2), slot(2), slot(9), ALU.mult))
            sync()
            for c in range(4):
                mark(nc.vector.tensor_scalar(chunks(slot(2))[:, c, :], chunks(slot(2))[:, c, :], vcol("l0_lnx_w_2", c),
                                             vcol("l0_lnx_b_2", c), ALU.mult, ALU.add))
            sync()
            mark(nc.vector.tensor_tensor(slot(2), slot(2), bonus, ALU.add))
            sync()
            nc.vector.tensor_tensor(slot(2), slot(2), gT, ALU.mult).then_inc(E("rwkv_out"), 1)
            dve.wait_ge(E("rwkv_hi"), 1)
            nc.vector.tensor_tensor(yl[:, 0:4, :], chunks(slot(2)), yh[:, 0:4, :].bitcast(F32), ALU.subtract)\
                .then_inc(E("rwkv_lo"), 1)
            if STOP < 5:
                return
            add_residual("wp")
            if STOP < 6:
                return

            def ffn(tag, k0):
                scale_rows()
                split_norm(tag)
                for i in range(FF_STEPS + 1):
                    if i < FF_STEPS:
                        next_unit()
                        k = k0 + i
                        hid = ytmp[:, k % 2, :]
                        dve.wait_ge(E("hidden_hi"), k + 1)
                        mark(nc.vector.tensor_tensor(hid, hid, hid, ALU.mult))
                        sync()
                        nc.vector.tensor_tensor(yl[:, 2 * (i % 3):2 * (i % 3) + 2, :], chunks(hid),
                                                yh[:, 2 * (i % 3):2 * (i % 3) + 2, :].bitcast(F32), ALU.subtract)\
                            .then_inc(E("hidden_lo"), 1)
                    if i >= 1:
                        next_unit()
                for s in range(NT):
                    for c in range(2):
                        name = f"dn{tag}_{2 * s + c}"
                        wait_full(dve, name)
                        nc.vector.tensor_tensor(xn[:, s, 512 * c:512 * c + 512], xn[:, s, 512 * c:512 * c + 512],
                                                bank(name), ALU.add).then_inc(empty(name), 1)

            ffn("f0", 0)
            if STOP < 7:
                return
            scale_rows()
            split_norm("n4")
            dve.wait_ge(E("pad_zeroed"), 8)
            def glu(i):
                wait_empty(dve, f"pa{i}")
                wait_empty(dve, f"pb{i}")
                nc.vector.scalar_tensor_tensor(out=upad[:, 2 * i:2 * i + 2, PAD:PAD + T], in0=chunks(thb[:, 0, 0:512]),
                                               scalar=1.0, in1=chunks(ytmp[:, 0, :]), op0=ALU.add, op1=ALU.mult)\
                    .then_inc(E("glu"), 1)

            next_unit()
            next_unit()
            glu(0)
            taps = [0] * 8
            for i in range(4):
                dve.wait_ge(E("glu"), i + 1)
                for tap in range(PE_TAPS, TAPS):
                    for c in (2 * i, 2 * i + 1):
                        src, w = upad[:, c, tap:tap + T], dwt[:, tap * 8 + c:tap * 8 + c + 1]
                        if tap == PE_TAPS:
                            taps[c] = mark(nc.vector.tensor_scalar(acc[:, c, :], src, w, None, ALU.mult))
                        else:
                            sync(taps[c])
                            taps[c] = mark(nc.vector.scalar_tensor_tensor(out=acc[:, c, :], in0=src, scalar=w,
                                                                          in1=acc[:, c, :], op0=ALU.mult, op1=ALU.add))
                    if i < 3 and tap == PE_TAPS + 8:
                        next_unit()
                    if i < 3 and tap == PE_TAPS + 13:
                        next_unit()
                        glu(i + 1)
                wait_empty(dve, f"taps{i}")
                for j in range(2):
                    c = 2 * i + j
                    sync(taps[c])
                    nc.vector.scalar_tensor_tensor(out=acc[:, c, :], in0=acc[:, c, :], scalar=0.5,
                                                   in1=ytmp[:, 1, j * T:(j + 1) * T], op0=ALU.mult, op1=ALU.add)\
                        .then_inc(E("convolved"), 1)
            if STOP < 8:
                return
            wait_empty(dve, "lnm")

            def on_pairs(col):
                return col.rearrange("p (o t) -> p o t", o=1).broadcast_to([P, 2, T])

            for k in range(4):
                nc.vector.tensor_tensor(acc[:, 2 * k:2 * k + 2, :], acc[:, 2 * k:2 * k + 2, :], on_pairs(lnmean), ALU.subtract)\
                    .then_inc(E("ln_centred"), 1)
            wait_empty(dve, "lnv")
            dve.wait_ge(E("ln_centred"), 4)
            mark(nc.vector.reciprocal(lnsd, lnsd))
            sync()
            for k in range(4):
                nc.vector.tensor_tensor(acc[:, 2 * k:2 * k + 2, :], acc[:, 2 * k:2 * k + 2, :], on_pairs(lnsd), ALU.mult)\
                    .then_inc(E("ln_divided"), 1)
            for k in range(4):
                dve.wait_ge(E("ln_tanh"), k + 1)
                nc.vector.scalar_tensor_tensor(out=lnsq[:, 2 * k:2 * k + 2, :], in0=lnsq[:, 2 * k:2 * k + 2, :], scalar=1.0,
                                               in1=acc[:, 2 * k:2 * k + 2, :], op0=ALU.add, op1=ALU.mult)\
                    .then_inc(E("ln_silu"), 1)
            for k in range(4):
                dve.wait_ge(E("ln_hi"), k + 1)
                nc.vector.scalar_tensor_tensor(out=xl[:, 2 * k:2 * k + 2, :], in0=lnsq[:, 2 * k:2 * k + 2, :], scalar=0.5,
                                               in1=xh[:, 2 * k:2 * k + 2, :].bitcast(F32), op0=ALU.mult,
                                               op1=ALU.subtract).then_inc(E("ln_lo"), 1)
            dve.wait_ge(E("pw2b_loaded"), 16)
            for s in range(NT):
                mark(nc.vector.tensor_tensor(xn[:, s, :], xn[:, s, :], pw2b, ALU.add))
            sync()
            add_residual("pw")
            if STOP < 9:
                return
            ffn("f1", FF_STEPS)
            dve.wait_ge(E("gain_loaded"), 32)
            scale_rows(2)

        @block.tensor
        def _(pe):
            mm = nc.tensor.matmul
            seen = [0] * 8
            unit = [0]

            def take(name):
                b, n = PL.uses[name]
                assert n == seen[b], name
                seen[b] += 1
                if n:
                    pe.wait_ge(emptied[b], n)
                return bank(name)

            def give(ins, name):
                ins.then_inc(full(name), 1)

            def wait_chunk(source, k):
                if source == "merged":
                    pe.wait_ge(E("merged_lo"), k + 1)
                elif source == "ln":
                    pe.wait_ge(E("ln_lo"), k // 2 + 1)
                elif source:
                    wait_empty(pe, f"{source}_t{k // 2}")

            def three(out, hh, hl, mh, ml, start, stop):
                mm(out, hh, mh, start=start, stop=False)
                mm(out, hh, ml, start=False, stop=False)
                return mm(out, hl, mh, start=False, stop=stop)

            def arrived(u):
                assert u == unit[0], (u, unit)
                unit[0] += 1
                pe.wait_ge(E("hi_split"), u + 1)
                pe.wait_ge(E("lo_split"), u + 1)

            def w_views(u, cols):
                return (wh[:, u % WBUFS, :].rearrange("p (j n) -> p j n", n=cols),
                        wl[:, u % WBUFS, :].rearrange("p (j n) -> p j n", n=cols))

            def t_unit(name, source=None):
                u = unit[0]
                arrived(u)
                h, l = w_views(u, 256)
                out = take(name)
                for t in range(2):
                    for k in range(KC):
                        if t == 0:
                            wait_chunk(source, k)
                        c = slice(t * P, (t + 1) * P)
                        ins = three(out[:, t * T:(t + 1) * T], h[:, k, c], l[:, k, c], xh[:, k, :], xl[:, k, :],
                                    k == 0, k == KC - 1)
                give(ins, name)

            def th_unit(names, chunk):
                u = unit[0]
                arrived(u)
                h, l = w_views(u, 512)
                for t in range(4):
                    if t % 2 == 0:
                        out = take(names[t // 2])
                    for k in range(4):
                        c = slice(t * P, (t + 1) * P)
                        ins = three(out[:, (t % 2) * T:(t % 2 + 1) * T], h[:, k, c], l[:, k, c], yh[:, chunk + k, :],
                                    yl[:, chunk + k, :], k == 0, k == 3)
                    if t % 2:
                        give(ins, names[t // 2])

            def nat_unit(names, half, ah=xh, al=xl, source=None):
                u = unit[0]
                arrived(u)
                h, l = w_views(u, 512)
                for s in range(NT):
                    out = take(names[s]) if half == 0 else bank(names[s])
                    for k in range(4):
                        c, rows = 4 * half + k, slice(s * P, (s + 1) * P)
                        if s == 0:
                            wait_chunk(source, c)
                        ins = three(out, ah[:, c, rows], al[:, c, rows], h[:, k, :], l[:, k, :],
                                    half == 0 and k == 0, half == 1 and k == 3)
                    if half:
                        give(ins, names[s])
                if not half:
                    ins.then_inc(E("unit_summed"), 1)

            def proj_out(tag, ah, al, source=None):
                for c in range(2):
                    for half in range(2):
                        nat_unit((f"{tag}{c}_0", f"{tag}{c}_1"), half, ah, al, None if c else source)

            rows_scaled = [0]

            def norm_transposes(tag):
                for s in range(NT):
                    rows_scaled[0] += 1
                    pe.wait_ge(E("rows_scaled"), rows_scaled[0])
                    for q in range(4):
                        out = take(f"{tag}_t{q}") if s == 0 else bank(f"{tag}_t{q}")
                        for i in range(2):
                            k = 2 * q + i
                            ins = nc.tensor.transpose(out[:, i * T + s * P:i * T + s * P + P],
                                                      scratch[:, s * DM + k * P:s * DM + k * P + P], ident)
                        if s:
                            give(ins, f"{tag}_t{q}")

            def heads_step(s, base, n):
                if s < n:
                    a = base + s
                    q, k, _ = head_views(a)
                    out = take(f"sc{a}")
                    mm(out[:, 0:P], q[:, 0:P], k[:, 0:P], start=True, stop=True)
                    give(mm(out[:, P:384], q[:, P:T], k, start=True, stop=True), f"sc{a}")
                if 1 <= s <= n:
                    a = base + s - 1
                    pe.wait_ge(E("probs_ready"), 2 * (a + 1))
                    out = take(f"pt{a}")
                    for i in range(3):
                        ins = nc.tensor.transpose(out[:, i * P:(i + 1) * P], att[:, a % 2, i * P:(i + 1) * P], ident)
                    give(ins, f"pt{a}")
                if s >= 2:
                    a = base + s - 2
                    h = a % 8
                    _, _, v = head_views(a)
                    name = f"o{a // 2}"
                    out = take(name) if a % 2 == 0 else bank(name)
                    out = out[HD * (h % 2):HD * (h % 2) + HD, 0:T]
                    wait_empty(pe, f"pt{a}")
                    p = ptb[:, a % 2, :]
                    mm(out, v[:, 0, :], p[:, 0:T], start=True, stop=False)
                    ins = mm(out[:, P:T], v[:, 1, :], p[:, T:384], start=False, stop=True)
                    if a % 2 == 0:
                        ins.then_inc(E("pv_even"), 1)
                    else:
                        give(ins, name)

            pe.wait_ge(E("consts_loaded"), 16)
            pe.wait_ge(E("norm_g_loaded"), 16)
            out = take("vec0")
            give(nc.tensor.transpose(out[:, 0:8], vrows[0:8, :], ident[0:8, 0:8]), "vec0")
            norm_transposes("n0")
            nat_unit(("ax0", "ax1"), 0, source="n0")
            nat_unit(("ax0", "ax1"), 1, source="n0")
            t_unit("az0")
            t_unit("az1")
            pe.wait_ge(E("vectors_loaded"), 16 * (len(VECS) + 1))
            out = take("vec1")
            for i in range(2):
                ins = nc.tensor.transpose(out[:, 124 * i:124 * i + 124], dwrows[0:124, i * P:(i + 1) * P],
                                          ident[0:124, 0:124])
            ins = nc.tensor.transpose(out[:, 256:256 + NVROWS], vrows[0:NVROWS, :], ident[0:NVROWS, 0:NVROWS])
            give(ins, "vec1")
            pe.wait_ge(E("pool_m_loaded"), 16)
            pe.wait_ge(E("poolw_loaded"), 16)
            wait_empty(pe, "ax0")
            wait_empty(pe, "ax1")
            for i in range(2):
                out = take(f"pool{i}")
                for j in range(2):
                    g = 2 * i + j
                    m = pool_m[:, g * T:(g + 1) * T]
                    o = out[:, j * T:(j + 1) * T]
                    mm(o, ax[:, 0, g * P:(g + 1) * P], m, start=True, stop=False)
                    ins = mm(o[:, P:T], ax[:, 1, g * P:(g + 1) * P], late[:, g * P:(g + 1) * P], start=False, stop=True)
                give(ins, f"pool{i}")
            for i in range(2):
                out = take(f"mix{i}")
                wait_empty(pe, f"pool{i}")
                for j in range(2):
                    g = 2 * i + j
                    ins = mm(out[:, j * T:(j + 1) * T], poolw[:, g, :], pooled[:, g, :], start=True, stop=True)
                give(ins, f"mix{i}")
            t_unit("bq0")
            t_unit("bq1")
            u = unit[0]
            arrived(u)
            h, l = w_views(u, 256)
            out = take("bk")
            for k in range(KC):
                ins = three(out[:, 0:T], h[:, k, 0:P], l[:, k, 0:P], xh[:, k, :], xl[:, k, :], k == 0, k == KC - 1)
            give(ins, "bk")
            out = take("bv")
            for s in range(NT):
                for k in range(KC):
                    r = slice(s * P, (s + 1) * P)
                    ins = three(out[:, s * P:(s + 1) * P], xh[:, k, r], xl[:, k, r], h[:, k, P:2 * P], l[:, k, P:2 * P],
                                k == 0, k == KC - 1)
            give(ins, "bv")
            wait_empty(pe, "bv")
            pe.wait_ge(E("keys_doubled"), 32)
            heads = iter(range(18))

            def step():
                s = next(heads, None)
                if s is not None:
                    heads_step(s, 0, 16)
                if s == 7:
                    wait_empty(pe, "cq0"), wait_empty(pe, "cq1"), wait_empty(pe, "ck0"), wait_empty(pe, "ck1")
                if s == 9:
                    wait_empty(pe, "cv0"), wait_empty(pe, "cv1")

            for name in ("bz0", "bz1", "cq0", "cq1", "ck0", "ck1"):
                t_unit(name)
                step()
            for half in range(2):
                nat_unit(("cv0", "cv1"), half)
                step()
            for name in ("cz0", "cz1"):
                t_unit(name)
                step()
            for m in range(3):
                for i in range(4):
                    t_unit(f"g{m}_{i}")
                    step()
                if m == 0:
                    pe.wait_ge(E("y_lo"), 2)
                else:
                    pe.wait_ge(E("y_lo"), 2 + 4 * m)
                for i in range(2):
                    th_unit((f"pr{m}_{2 * i}", f"pr{m}_{2 * i + 1}"), 4 * m)
                    step()
            if STOP < 2:
                return
            proj_out("wo", xh, xl, "merged")
            norm_transposes("n2")
            if STOP < 3:
                return
            for name in ("q2_0", "q2_1", "k2_0", "k2_1"):
                t_unit(name, "n2" if name == "q2_0" else None)
            for half in range(2):
                nat_unit(("v2_0", "v2_1"), half)
            for i in range(7):
                t_unit(f"rw{i}")
                if i == 0:
                    for name in ("q2_0", "q2_1", "k2_0", "k2_1", "v2_0", "v2_1"):
                        wait_empty(pe, name)
                heads_step(i, 16, 8)
            for s in range(7, 10):
                heads_step(s, 16, 8)
            if STOP < 4:
                return
            pe.wait_ge(E("lora_loaded"), 48)
            pe.wait_ge(E("xw_tanh"), 1)
            for tag, rows, m, x, sem in (("z", slice(0, 64), 0, xwa, None), ("a", slice(64, 128), 1, xwa, None),
                                         ("gg", slice(0, 128), 2, xg, "xg_ready")):
                if sem:
                    pe.wait_ge(E(sem), 1)
                for i in range(2):
                    out = take(f"{tag}{i}")
                    for j in range(2):
                        c = 2 * i + j
                        ins = mm(out[:, j * T:(j + 1) * T], lora[rows, m, c * P:(c + 1) * P], x[rows, :], start=True, stop=True)
                    give(ins, f"{tag}{i}")
            head_ones = const("head_ones")

            def head_sums(tag, src, sem, n):
                for i in range(2):
                    pe.wait_ge(E(sem), n)
                    out = take(f"{tag}{i}")
                    give(mm(out, head_ones, src[:, 512 * i:512 * i + 512], start=True, stop=True), f"{tag}{i}")

            head_sums("kn", rk, "kk_squares", 1)
            head_sums("bo", rk, "bonus_terms", 4)
            for name, src, n in (("an", aTil, 1), ("bn", bHat, 3), ("kn", kHat, 4), ("vn", slot(2), 0)):
                if n:
                    pe.wait_ge(E("scaled_keys"), n)
                for tt in range(NT):
                    out = take(f"nat_{name}{tt}")
                    for p in range(4):
                        ins = nc.tensor.transpose(out[:, p * P:(p + 1) * P], src[:, p * T + tt * P:p * T + tt * P + P], ident)
                    give(ins, f"nat_{name}{tt}")

            def htile(ap, tt, h):
                hp = HD * (h % 2)
                return ap[hp:hp + HD, (h // 2) * T + tt * P:(h // 2) * T + tt * P + P]

            wait_empty(pe, "bo1")
            wait_empty(pe, "nat_vn1")
            wait_empty(pe, "nat_kn1"), wait_empty(pe, "nat_an1"), wait_empty(pe, "nat_an0")
            wait_empty(pe, "nat_vn0"), wait_empty(pe, "nat_kn0"), wait_empty(pe, "nat_bn0"), wait_empty(pe, "nat_bn1")
            pe.wait_ge(E("scaled_keys"), 5)
            needs = {"AV": ("GA",), "N2": ("GD", "GN"), "D2": ("AV",), "N4": ("N2", "D2"), "X2": (), "D4": ("N4",),
                     "X4": ("D4", "X2"), "D8": (), "X8": ("D8", "X4"), "Z1": ("X8", "AV"), "EZ": ("Z1",), "ZZ": ("EZ",)}
            for pair in range(2):
                for name, _ in INVERSE:
                    for g in (2 * pair, 2 * pair + 1):
                        ts = tset[g % 2]
                        for need in needs.get(name, ()):
                            wait_empty(pe, f"{need}_{g}")
                        if name == "X2":
                            pe.wait_ge(E("series_begun"), g + 1)
                        out = take(f"{name}_{g}")
                        for i, (tt, h) in enumerate(combo_cols(g)):
                            def m(ap):
                                return ap[:, i * P:(i + 1) * P]
                            o = m(out)
                            if name == "GN":
                                ins = mm(o, htile(bTil, tt, h), htile(aTil, tt, h), start=True, stop=True)
                            elif name == "GA":
                                ins = mm(o, htile(kTil, tt, h), htile(aTil, tt, h), start=True, stop=True)
                            elif name == "GD":
                                ins = mm(o, htile(aTil, tt, h), htile(bTil, tt, h), start=True, stop=True)
                            elif name == "AV":
                                ins = mm(out[:, i * HD:(i + 1) * HD], m(ts[3]), Vn[:, tt, h * HD:(h + 1) * HD],
                                         start=True, stop=True)
                            elif name == "Z1":
                                mm(o[:, 0:HD], m(ts[4]), An[:, tt, h * HD:(h + 1) * HD], start=True, stop=True)
                                ins = mm(o[:, HD:P], m(ts[4]), Z[:, 1, tt, h, :], start=True, stop=True)
                            else:
                                lhs, rhs = {"N2": (1, 0), "D2": (0, 1), "N4": (3, 5), "X2": (3, 4), "D4": (5, 3),
                                            "X4": (1, 4), "D8": (0, 1), "X8": (5, 4), "EZ": (2, 0), "ZZ": (4, 1)}[name]
                                ins = mm(o, m(ts[lhs]), m(ts[rhs]), start=True, stop=True)
                        give(ins, f"{name}_{g}")
            for g in range(4):
                wait_empty(pe, f"ZZ_{g}")
            for tt in range(NT):
                out = take(f"wt{tt}")
                for p in range(4):
                    ins = nc.tensor.transpose(out[:, p * P:(p + 1) * P], Z[:, 0, tt, 2 * p:2 * p + 2, :].rearrange("p h d -> p (h d)"), ident)
                give(ins, f"wt{tt}")
            wait_empty(pe, "wt0"), wait_empty(pe, "wt1")
            pe.wait_ge(E("state_zeroed"), 1)
            for c in range(NCH):
                tt, pb = c // 4, 32 * (c % 4)
                rows = slice(pb, pb + C)
                if c:
                    wait_empty(pe, f"st{c - 1}")
                for par, tag in enumerate(("sae", "sao")):
                    out = take(f"{tag}{c}")
                    hp = HD * par
                    for p in range(4):
                        ins = mm(out[rows, p * HD:(p + 1) * HD], WT[hp:hp + HD, p, c * C:(c + 1) * C],
                                 S(c)[hp:hp + HD, p * HD:(p + 1) * HD], start=True, stop=True)
                    give(ins, f"{tag}{c}")
                if c == NCH - 1:
                    continue
                out = take(f"st{c}")
                for par, tag in enumerate(("sae", "sao")):
                    wait_empty(pe, f"{tag}{c}")
                    for p in range(4):
                        h = 2 * p + par
                        o = out[HD * par:HD * par + HD, p * HD:(p + 1) * HD]
                        hc = slice(h * HD, (h + 1) * HD)
                        mm(o, Kn[rows, tt, hc], Vn[rows, tt, hc], start=True, stop=False)
                        ins = mm(o, Bn[rows, tt, hc], SA[rows, tt, hc], start=False, stop=True)
                give(ins, f"st{c}")
            wait_empty(pe, f"sae{NCH - 1}"), wait_empty(pe, f"sao{NCH - 1}")
            for g in range(4):
                for tag, src in (("A3", bTil), ("A4", kTil)):
                    out = take(f"{tag}_{g}")
                    for i, (tt, h) in enumerate(combo_cols(g)):
                        ins = mm(out[:, i * P:(i + 1) * P], htile(src, tt, h), htile(rTil, tt, h), start=True, stop=True)
                    give(ins, f"{tag}_{g}")
                wait_empty(pe, f"A3_{g}"), wait_empty(pe, f"A4_{g}")
                out = take(f"y{g // 2}") if g % 2 == 0 else bank(f"y{g // 2}")
                am = slot(7 if g % 2 == 0 else 9)
                for i, (tt, h) in enumerate(combo_cols(g)):
                    hp = HD * (h % 2)
                    o = out[hp:hp + HD, (h // 2) * P:(h // 2) * P + P]
                    hc = slice(h * HD, (h + 1) * HD)
                    mm(o, SA[:, tt, hc], am[:, i * P:(i + 1) * P], start=True, stop=False)
                    mm(o, Vn[:, tt, hc], am[:, 512 + i * P:512 + (i + 1) * P], start=False, stop=False)
                    for j in range(4):
                        c = 4 * tt + j
                        ins = mm(o[:, j * C:(j + 1) * C], S(c)[hp:hp + HD, (h // 2) * HD:(h // 2) * HD + HD],
                                 rTil[hp:hp + HD, (h // 2) * T + c * C:(h // 2) * T + (c + 1) * C], start=False, stop=j == 3)
                if g % 2:
                    give(ins, f"y{g // 2}")
            wait_empty(pe, "y0"), wait_empty(pe, "y1")
            for i in range(2):
                out = take(f"gm{i}")
                give(mm(out, head_ones, slot(12)[:, 512 * i:512 * i + 512], start=True, stop=True), f"gm{i}")
            head_sums("gv", slot(7), "gn_squares", 1)
            if STOP < 5:
                return
            pe.wait_ge(E("rwkv_lo"), 1)
            wait_empty(pe, "o11")
            proj_out("wp", yh, yl)
            if STOP < 6:
                return

            def ffn(tag, k0):
                norm_transposes(tag)
                for i in range(FF_STEPS + 1):
                    if i < FF_STEPS:
                        t_unit(f"up{tag}_{i}", None if i else tag)
                    if i == 0:
                        continue
                    u, j = unit[0], i - 1
                    arrived(u)
                    h, l = w_views(u, DM)
                    pe.wait_ge(E("hidden_lo"), k0 + j + 1)
                    buf = 2 * (j % 3)
                    for s in range(NT):
                        for c in range(2):
                            b = 4 + 2 * s + c
                            if j == 0:
                                pe.wait_ge(emptied[b], PL.uses[f"dn{tag}_{2 * s + c}"][1])
                                seen[b] += 1
                            for k in range(2):
                                cs, rs = slice(512 * c, 512 * c + 512), slice(s * P, (s + 1) * P)
                                ins = three(banks[:, b, :], yh[:, buf + k, rs], yl[:, buf + k, rs], h[:, k, cs], l[:, k, cs],
                                            j == 0 and k == 0, j == FF_STEPS - 1 and k == 1)
                            if j == FF_STEPS - 1:
                                give(ins, f"dn{tag}_{2 * s + c}")
                    if j < FF_STEPS - 1:
                        ins.then_inc(E("unit_summed"), 1)

            ffn("f0", 0)
            if STOP < 7:
                return
            norm_transposes("n4")
            def conv_taps(i):
                pe.wait_ge(E("diagonals"), 2 * PE_TAPS * (i + 1))
                pe.wait_ge(E("glu"), i + 1)
                out = take(f"taps{i}")
                for j in range(2):
                    for tap in range(PE_TAPS):
                        ins = mm(out[:, j * T:(j + 1) * T], tap_diag(i, j, tap), upad[:, 2 * i + j, tap:tap + T],
                                 start=tap == 0, stop=tap == PE_TAPS - 1)
                give(ins, f"taps{i}")

            for i in range(4):
                t_unit(f"pa{i}", None if i else "n4")
                t_unit(f"pb{i}")
                if i:
                    conv_taps(i - 1)
            conv_taps(3)
            if STOP < 8:
                return
            ones = const("ones")
            out = take("lnm")
            for c in range(8):
                pe.wait_ge(E("convolved"), c + 1)
                ins = mm(out[:, 0:T], ones, acc[:, c, :], start=c == 0, stop=c == 7)
            give(ins, "lnm")
            out = take("lnv")
            for c in range(8):
                pe.wait_ge(E("ln_squares"), c // 2 + 1)
                ins = mm(out[:, 0:T], ones, lnsq[:, c, :], start=c == 0, stop=c == 7)
            give(ins, "lnv")
            proj_out("pw", xh, xl, "ln")
            if STOP < 9:
                return
            ffn("f1", FF_STEPS)


_OUT = ((1, T, DM), "float32")


def kernel(**inputs):
    import concourse.bacc as bacc
    from concourse.bass_utils import run_bass_kernel_spmd

    nc = bacc.Bacc("TRN2", target_bir_lowering=False, num_devices=1)
    arrays, A = {}, {}
    for name, value in inputs.items():
        a = np.ascontiguousarray(value)
        arrays[f"in_{name}"] = a
        A[name] = nc.dram_tensor(f"in_{name}", a.shape, mybir.dt.from_np(a.dtype), kind="ExternalInput").ap()
    arrays["shape_constants"] = CONSTS
    consts_d = nc.dram_tensor("shape_constants", CONSTS.shape, F32, kind="ExternalInput").ap()
    ext_d = nc.dram_tensor("rel_bias_extended", (8, 384), F32, kind="Internal").ap()
    out_d = nc.dram_tensor("out", _OUT[0], F32, kind="ExternalOutput").ap()
    build(nc, A, consts_d, ext_d, out_d)
    return run_bass_kernel_spmd(nc, [arrays], core_ids=[0]).results[0]["out"]
```

```python
from contextlib import ExitStack
import math

import numpy as np
import concourse.bass as bass
from concourse import mybir

F32 = mybir.dt.float32
F32R = mybir.dt.float32r
ALU = mybir.AluOpType
ACT = mybir.ActivationFunctionType
AX_X = mybir.AxisListType.X

P = 128
T = 256
NT = T // P
DM = 1024
KC = DM // P
HD = 64
NEG = -1e30
SCALE = HD ** -0.5
UNIT = 2048
RAWS, WBUFS = 4, 3
C = 32
NCH = T // C
DECAY = math.exp(-0.5)
TAPS = 31
PAD = TAPS - 1
POOL_WINDOWS = (2, 4, 8, 16)
FF_STEPS = 16

AX, AZ, BQ, BKV, BZ, CQ, CK, CV, CZ, GATES = 0, 512, 1024, 1536, 1792, 2304, 2816, 3328, 3840, 4352
Q2, K2, V2 = 1792, 2304, 2816


def shape_constants():
    names, parts, at = {}, [], 0

    def put(name, a):
        nonlocal at
        a = np.asarray(a, np.float32)
        names[name] = (at, at + a.shape[1])
        parts.append(a)
        at += a.shape[1]

    i = np.arange(P)[:, None]
    j = np.arange(P)[None, :]
    put("ident", i == j)
    put("ones", np.ones((P, P)))
    put("head_ones", (i // HD) == (j // HD))
    causal = np.where(j <= i, 0.0, NEG)
    prev = np.where(j > i, 0.0, NEG)
    put("mask_swa", np.concatenate([causal, prev, causal], 1))
    put("mask_causal", np.concatenate([causal, np.zeros((P, P)), causal], 1))
    same32, same16 = (i // 32) == (j // 32), (i // 16) == (j // 16)
    put("up16", same16 & (i < j))
    put("low16", same16 & (i > j))
    put("cross", same32 & ~same16 & (i < j))
    put("up32", same32 & (i < j))
    put("upinc32", same32 & (i <= j))
    keep = at
    t = np.arange(T)[None, :]
    for w in POOL_WINDOWS:
        put(f"pool{w}", ((i <= t) & (t < i + w)) / np.minimum(t + 1, w) - (i == t))
    for w in POOL_WINDOWS:
        put(f"late{w}", ((i <= j) & (j < i + w)) / w - (i == j))
    for p in range(4):
        put(f"unfold{p}", ((i == 32 * p) & (j < HD)) | ((i == 32 * p + 16) & (j >= HD)))
    put("scan_keep", np.tile((np.arange(T) % C != 0).astype(np.float32), (P, 4)))
    return names, keep, np.ascontiguousarray(np.concatenate(parts, 1))


CONST, NKEEP, CONSTS = shape_constants()

VECS = [("norm_g", 8), ("pool_scale", 4), ("l0_norm_mix_2", 8), ("l0_shift_mu_2", 14),
        ("l0_w0_2", 4), ("l0_a0_2", 4), ("l0_k_k_2", 4), ("l0_k_a_2", 4), ("l0_r_k_2", 4),
        ("l0_lnx_w_2", 4), ("l0_lnx_b_2", 4), ("l0_norm_ffn_2", 8), ("l1_norm_mix_2", 8),
        ("l1_pw1_b_2", 16), ("l1_dw_b_2", 8), ("l1_ln_w_2", 8), ("l1_ln_b_2", 8),
        ("l1_norm_ffn_2", 8)]
VROW = {}
NVROWS = 0
for _name, _k in VECS:
    VROW[_name] = NVROWS
    NVROWS += _k

INVERSE = [("GN", "dve"), ("GA", "dve"), ("GD", "dve"), ("AV", "act"), ("N2", "act"), ("D2", "dve"),
           ("N4", "act"), ("X2", "dve"), ("D4", "act"), ("X4", "dve"), ("D8", "act"), ("X8", "dve"),
           ("Z1", "act"), ("EZ", "act"), ("ZZ", "dve")]


class Plan:

    def __init__(self):
        self.units, self.uses, self.count, self.done = [], {}, [0] * 8, {}
        self.turn = 0

    def use(self, name, bank=None):
        if bank is None:
            bank = self.turn
            self.turn ^= 1
        assert name not in self.uses
        self.uses[name] = (bank, self.count[bank])
        self.count[bank] += 1
        return name

    def unit(self, kind, w, row, col, last):
        self.units.append((kind, w, row, col))
        self.done[len(self.units) - 1] = last


def plan():
    s = Plan()

    def norm(tag):
        for q in range(4):
            s.use(f"{tag}_t{q}", q)

    def t_units(tag, w, col, n):
        for i in range(n):
            s.unit("T", w, 0, col + 256 * i, s.use(f"{tag}{i}"))

    def nat_units(tag, w, col, banks):
        s.unit("N", w, 0, col, None)
        for b, bank in enumerate(banks):
            s.use(f"{tag}{b}", bank)
        s.unit("N", w, 512, col, f"{tag}1")

    def proj_out(tag, w):
        for c in range(2):
            nat_units(f"{tag}{c}_", w, 512 * c, (4 + 2 * c, 5 + 2 * c))

    def heads(first, n):
        for a in range(first, first + n):
            s.use(f"sc{a}", 2 + a % 2)
            s.use(f"pt{a}", 4)
            if a % 2:
                s.use(f"o{a // 2}", 5)

    s.use("vec0")
    norm("n0")
    nat_units("ax", "w_in", AX, (6, 7))
    t_units("az", "w_in", AZ, 2)
    s.use("vec1")
    for name in ("pool0", "pool1", "mix0", "mix1"):
        s.use(name)
    t_units("bq", "w_in", BQ, 2)
    s.unit("T", "w_in", 0, BKV, s.use("bkv"))
    s.unit("T", "w_in", 0, BZ, s.use("bz0"))
    s.use("bv")
    s.unit("T", "w_in", 0, BZ + 256, s.use("bz1"))
    t_units("cq", "w_in", CQ, 2)
    t_units("ck", "w_in", CK, 2)
    nat_units("cv", "w_in", CV, (6, 7))
    t_units("cz", "w_in", CZ, 2)
    for m, w in enumerate(("w_proj_a", "w_proj_b", "w_proj_c")):
        t_units(f"g{m}_", "w_in", GATES + m * DM, 4)
        for i in range(2):
            s.use(f"pr{m}_{2 * i}", 6)
            s.unit("TH", w, 0, 512 * i, s.use(f"pr{m}_{2 * i + 1}", 7))
    heads(0, 16)
    proj_out("wo", "w_out")
    norm("n2")
    t_units("q2_", "l0_w_in_2", Q2, 2)
    t_units("k2_", "l0_w_in_2", K2, 2)
    nat_units("v2_", "l0_w_in_2", V2, (6, 7))
    for i in RW_ORDER:
        s.unit("T", "l0_w_in_2", 0, 256 * i, s.use(f"rw{i}"))
    heads(16, 8)
    for name in ("z", "a", "gg"):
        s.use(f"{name}0", 6), s.use(f"{name}1", 7)
    s.use("kn", 6), s.use("kn_b0", 7), s.use("kn_b1", 6)
    s.use("bo0", 7), s.use("bo1", 6)
    for name in ("an", "vn", "kn", "bn"):
        s.use(f"nat_{name}0"), s.use(f"nat_{name}1")
    rot = 2
    for pair in range(2):
        for name, _ in INVERSE:
            for g in (2 * pair, 2 * pair + 1):
                s.use(f"{name}_{g}", rot % 8)
                rot += 1
    s.use("wt0"), s.use("wt1")
    for c in range(NCH):
        s.use(f"sae{c}", 2), s.use(f"sao{c}", 3)
        if c < NCH - 1:
            s.use(f"ste{c}", 4), s.use(f"sto{c}", 7)
    for g in range(4):
        s.use(f"A3_{g}"), s.use(f"A4_{g}")
    s.use("y0", 5), s.use("y1", 6)
    for name in ("gm0", "gm1", "gv", "gv_b0", "gv_b1"):
        s.use(name)
    for c in range(2):
        s.unit("N", "l0_w_out_2", 512, 512 * c, None)
        s.use(f"wp{c}_0", 4 + 2 * c), s.use(f"wp{c}_1", 5 + 2 * c)
    for c in range(2):
        s.unit("N", "l0_w_out_2", 0, 512 * c, f"wp{c}_1")

    def ffn(tag, up, down):
        norm(tag)
        for i in range(FF_STEPS + 1):
            if i < FF_STEPS:
                s.unit("T", up, 0, 256 * i, s.use(f"up{tag}_{i}"))
            if i >= 1:
                if i == FF_STEPS:
                    for b in range(4):
                        s.use(f"dn{tag}_{b}", 4 + b)
                s.unit("D", down, 256 * (i - 1), 0, f"dn{tag}_3" if i == FF_STEPS else None)

    ffn("f0", "l0_ffn_up_2", "l0_ffn_down_2")
    norm("n4")
    for i in range(4):
        s.unit("T", "l1_pw1_2", 0, 256 * i, s.use(f"pa{i}"))
        s.unit("T", "l1_pw1_2", 0, DM + 256 * i, s.use(f"pb{i}"))
        s.use(f"taps{i}", 4 + i)
    s.use("lnm"), s.use("lnv")
    proj_out("pw", "l1_pw2_2")
    ffn("f1", "l1_ffn_up_2", "l1_ffn_down_2")
    return s


RW_ORDER = (6, 2, 3, 0, 1, 4, 5)
PRODUCTS = [(name, g) for g in range(4) for name in ("A3", "A4")]
PE_TAPS = 12
DOWN = {"f0": "l0_ffn_down_2", "f1": "l1_ffn_down_2"}
UP = {"f0": "l0_ffn_up_2", "f1": "l1_ffn_up_2"}
GAIN = {"n0": "norm_g", "n2": "l0_norm_mix_2", "f0": "l0_norm_ffn_2", "n4": "l1_norm_mix_2",
        "f1": "l1_norm_ffn_2"}


def build(nc, A, consts_d, ext_d, out_d):
    PL = plan()
    UNITS = PL.units
    NU = len(UNITS)
    UID = {u: n for n, u in enumerate(UNITS)}
    PARTIAL = [n for n in range(NU) if PL.done[n] is None]

    def mat(name):
        a = A[name]
        return a[0] if len(a.shape) == 3 else a

    def vec(name):
        a = A[name]
        return a[0] if len(a.shape) == 2 else a

    ctx = ExitStack()
    with ctx:
        def sb(name, shape, dt=F32):
            return ctx.enter_context(nc.sbuf_tensor(name, shape, dt))

        sems = {}

        def E(name):
            if name not in sems:
                sems[name] = ctx.enter_context(nc.semaphore(name))
            return sems[name]

        raw = sb("raw", [P, RAWS, UNIT])
        wh = sb("wh", [P, WBUFS, UNIT], F32R)
        wl = sb("wl", [P, WBUFS, UNIT], F32R)
        with ExitStack() as y_ctx:
            yh = y_ctx.enter_context(nc.sbuf_tensor("yh", [P, 12, T], F32R))
            yl = y_ctx.enter_context(nc.sbuf_tensor("yl", [P, 12, T], F32R))
        yover = sb("yover", [P, 2 * 12 * T])
        xn = sb("xn", [P, NT, DM])
        cst = sb("cst", [P, NKEEP])
        vt = sb("vt", [P, NVROWS])
        dwt = sb("dwt", [P, TAPS * 8])
        small = sb("small", [P, 128])
        att = sb("att", [P, 2, 384])
        ptb = sb("ptb", [P, 2, 384])
        ytmp = sb("ytmp", [P, 2, 512])
        extra_t = sb("extra_t", [P, 2, 512])
        thb = sb("thb", [P, 2, 514])
        with ExitStack() as split_ctx:
            xh = split_ctx.enter_context(nc.sbuf_tensor("xh", [P, KC, T], F32R))
            xl = split_ctx.enter_context(nc.sbuf_tensor("xl", [P, KC, T], F32R))
        over = sb("over", [P, 2 * KC * T])
        NSLOT = 13
        arena = sb("arena", [P, NSLOT * 1024])
        banks = ctx.enter_context(nc.psum_tensor("banks", [P, 8, 512], F32))

        def const(name):
            a, b = CONST[name]
            return cst[:, a:b]

        ident = const("ident")
        at = CONST["mask_swa"][0]
        unfold = cst[:, at:at + 4 * P]

        def slot(n, count=1):
            return arena[:, n * 1024:(n + count) * 1024]

        def oslot(n, count=1):
            return over[:, n * 1024:(n + count) * 1024]

        def chunks(ap):
            return ap.rearrange("p (c t) -> p c t", t=T)

        def tiles(ap):
            return ap.rearrange("p (s n) -> p s n", s=NT)

        def vcol(name, i=0):
            return vt[:, VROW[name] + i:VROW[name] + i + 1]

        MS = small[:, 0:2]
        SS = small[:, 116:120]
        RSTD, MHALF, NMAX = small[:, 2:4], small[:, 4:6], small[:, 8:24]
        DEN, ES = small[:, 24:40], small[:, 40:56]
        HSCALE, EPSG, EPSL = small[:, 72:76], small[:, 76:77], small[:, 77:78]
        HW0, HA0 = small[:, 78:82], small[:, 82:86]
        sinkb = small[:, 86:94]
        hb = small[:, 94:102]
        hln = small[:, 56:72]
        omu = small[:, 102:116]
        pcs = sb("pcs", [P, 32])

        ax, pooled = tiles(slot(0)), chunks(slot(1))
        sz = [chunks(slot(2 + m)) for m in range(3)]
        bq, cq, ck = chunks(slot(5)), chunks(slot(6)), chunks(slot(7))
        cv = tiles(slot(8))
        bk = chunks(arena[:, 9216:9216 + 512])
        bv = tiles(arena[:, 9216 + 512:9216 + 768])
        bvt = arena[:, 9216 + 768:9216 + 1024]
        poolw = arena[:, 10240:10240 + 512].rearrange("p (g d) -> p g d", g=4)
        pool_m = arena[:, 10752:10752 + 1536]
        late = pool_m[:, 1024:1536]
        gate = chunks(slot(11, 2))
        merged = chunks(slot(0, 2))
        vrows = arena[:, 6 * 1024:6 * 1024 + P]
        dwrows = arena[:, 6 * 1024 + P:6 * 1024 + 3 * P]
        scratch = slot(11, 2)
        gained = slot(1, 2)
        SSG = small[:, 122:126]
        R12 = small[:, 126:128]
        gfin = slot(5)
        band = arena[:, 4096:6144].rearrange("p (h m) -> p h m", h=8)
        extr = arena[0:8, 3 * 1024:3 * 1024 + 384]
        rT, kT, vT = chunks(slot(0)), chunks(slot(1)), chunks(slot(2))
        xwa, xg = arena[:, 3072:3072 + T], arena[:, 3072 + T:3072 + 2 * T]
        q2, k2, v2 = chunks(slot(7)), chunks(slot(8)), tiles(slot(12))
        keep = slot(9)
        lora = arena[:, 10240:10240 + 1536].rearrange("p (m n) -> p m n", m=3)

        def spare(low, c):
            return yover[:, (12 * low + c) * T:(12 * low + c + 4) * T]

        LD, aT, gT = (ap.rearrange("p c t -> p (c t)") for ap in (ytmp[:, :, :], extra_t[:, :, :], chunks(slot(6))))
        kk, rk, Lc, Pprev = spare(1, 8), spare(0, 8), spare(1, 0), spare(0, 0)
        Pc, Pinv, bonus = slot(9), LD, oslot(3)
        aTil, bTil, kTil, rTil = oslot(2), slot(5), slot(1), slot(0)
        bHat, kHat = slot(7), slot(4)
        An, Bn, Kn, Vn = tiles(slot(8)), tiles(slot(3)), tiles(slot(10)), tiles(slot(11))
        Z = oslot(0, 2).rearrange("p (w s h d) -> p w s h d", w=2, s=NT, h=8)
        tset = [[slot(n)[:, 512 * (i % 2):512 * (i % 2) + 512] for i, n in enumerate(ns)]
                for ns in ((2, 2, 4, 4, 7, 7), (9, 9, 12, 12, 12, 12))]
        tset[1][4], tset[1][5] = extra_t[:, 0, :], extra_t[:, 1, :]
        WT = chunks(slot(2))

        def products(g):
            return slot((7, 9, 8, 12)[g])

        def S(c):
            place = extra_t if c < 4 else over[:, 2048:3072].rearrange("p (i n) -> p i n", i=2)
            return place[:, (c % 4) // 2, (c % 2) * 256:(c % 2) * 256 + 256]
        SA = tiles(slot(4))
        YT = chunks(LD)
        acc = chunks(slot(0, 2))
        upad = arena[:, 2048:2048 + 8 * (PAD + T)].rearrange("p (c t) -> p c t", t=PAD + T)
        lnsq = chunks(slot(5, 2))
        lnsd = slot(7)[:, T:2 * T]
        pw2b = slot(8)

        def tap_diag(i, j, tap):
            n = j * PE_TAPS + tap
            places = ((9, 10, 11), (12, 5, 6))[i % 2]
            return slot(places[n // 8])[:, (n % 8) * P:(n % 8 + 1) * P]

        filled = [E(f"filled{b}") for b in range(8)]
        emptied = [E(f"emptied{b}") for b in range(8)]

        def bank(name):
            return banks[:, PL.uses[name][0], :]

        def wait_full(eng, name):
            b, n = PL.uses[name]
            eng.wait_ge(filled[b], n + 1)

        def wait_empty(eng, name):
            b, n = PL.uses[name]
            eng.wait_ge(emptied[b], n + 1)

        def full(name):
            return filled[PL.uses[name][0]]

        def empty(name):
            return emptied[PL.uses[name][0]]

        def wait_unit_used(eng, u):
            if PL.done[u] is None:
                eng.wait_ge(E("unit_summed"), PARTIAL.index(u) + 1)
            else:
                wait_full(eng, PL.done[u])

        def wait_pv(eng, a):
            if a % 2:
                wait_full(eng, f"o{a // 2}")
            else:
                eng.wait_ge(E("pv_even"), a // 2 + 1)

        def head_views(a):
            kind, h = divmod(a, 8)
            hp, pair = HD * (h % 2), h // 2
            q = (bq, cq, q2)[kind][hp:hp + HD, pair, :]
            if kind == 0:
                return q, bk[hp:hp + HD, pair // 2, :], bv[:, :, HD * (h // 4):HD * (h // 4) + HD]
            return q, (ck, k2)[kind - 1][hp:hp + HD, pair, :], (cv, v2)[kind - 1][:, :, HD * h:HD * h + HD]

        def exps_done(a):
            return 3 * min(a + 1, 8) + 2 * max(0, a - 7)

        def combo_cols(g):
            tt, par = divmod(g, 2)
            return [(tt, par + 2 * i) for i in range(4)]

        block = ctx.enter_context(nc.Block())

        @block.sync
        def _(sp):
            for s in range(NT):
                sp.dma_start(xn[:, s, :], A["x"][0, s * P:(s + 1) * P, :]).then_inc(E("x_loaded"), 16)
            sp.dma_start(cst[:, :], consts_d[:, 0:NKEEP]).then_inc(E("consts_loaded"), 16)
            for n in range(NU):
                kind, w, r, c = UNITS[n]
                rows, cols = {"TH": (512, 512), "N": (512, 512), "D": (256, 1024)}.get(kind, (1024, 256))
                if n >= RAWS:
                    sp.wait_ge(E("lo_split"), n - RAWS + 1)
                sp.dma_start(raw[:, n % RAWS, :].rearrange("p (j n) -> p j n", n=cols),
                             mat(w)[r:r + rows, c:c + cols].rearrange("(j p) n -> p j n", p=P))\
                    .then_inc(E(f"unit_loaded{n % RAWS}"), 16)
            sp.wait_ge(E("out_ready"), 2)
            sp.dma_start(out_d[0].rearrange("(s p) n -> p s n", p=P), xn[:, :, :]).then_inc(E("out_stored"), 16)
            sp.wait_ge(E("out_stored"), 16)

        @block.gpsimd
        def _(pool):
            nc.gpsimd.memset(MHALF, -0.5).then_inc(E("pool_consts"), 1)
            nc.gpsimd.memset(EPSG, 64e-5).then_inc(E("pool_consts"), 1)
            nc.gpsimd.memset(EPSL, 1e-5).then_inc(E("pool_consts"), 1)
            pool.wait_ge(E("pool_consts"), 1)
            norms = [0]
            tiny = [0]

            def step(ins):
                tiny[0] += 1
                ins.then_inc(E("mean_square"), 1)
                pool.wait_ge(E("mean_square"), tiny[0])

            def two_rstds():
                for t in range(NT):
                    col = slice(t, t + 1)
                    pool.wait_ge(E("squares_summed"), 4 * norms[0] + (6, 8)[t])
                    step(nc.gpsimd.tensor_scalar(MS[:, col], SS[:, 2 * t:2 * t + 1], SS[:, 2 * t + 1:2 * t + 2], 1e-6,
                                                 ALU.add, ALU.add))
                    step(nc.gpsimd.tensor_tensor(RSTD[:, col], MS[:, col], MHALF[:, 0:1], ALU.pow))
                    step(nc.gpsimd.tensor_scalar(MS[:, col], SSG[:, 2 * t:2 * t + 1], SSG[:, 2 * t + 1:2 * t + 2],
                                                 RSTD[:, col], ALU.add, ALU.mult))
                    step(nc.gpsimd.tensor_scalar(MS[:, col], MS[:, col], RSTD[:, col], 1e-6, ALU.mult, ALU.add))
                    step(nc.gpsimd.tensor_tensor(R12[:, col], MS[:, col], MHALF[:, 0:1], ALU.pow))
                    nc.gpsimd.tensor_tensor(R12[:, col], R12[:, col], RSTD[:, col], ALU.mult)\
                        .then_inc(E("rstd_ready"), 1)
                norms[0] += 2

            def rstd(first):
                for t in range(NT):
                    pool.wait_ge(E("squares_summed"), 4 * norms[0] + (first, 4)[t])
                    step(nc.gpsimd.tensor_scalar(MS[:, t:t + 1], SS[:, 2 * t:2 * t + 1], SS[:, 2 * t + 1:2 * t + 2], 1e-6,
                                                 ALU.add, ALU.add))
                    nc.gpsimd.tensor_tensor(RSTD[:, t:t + 1], MS[:, t:t + 1], MHALF[:, 0:1], ALU.pow)\
                        .then_inc(E("rstd_ready"), 1)
                norms[0] += 1

            rstd(2)
            for name, k in VECS[1:]:
                r = VROW[name]
                pool.dma_start(vrows[r:r + k, :], vec(name).rearrange("(k c) -> k c", c=P))\
                    .then_inc(E("vectors_loaded"), 16)
            for i in range(2):
                pool.dma_start(dwrows[0:124, i * P:(i + 1) * P],
                               A["l1_dw_2"].rearrange("t (k c) -> (t k) c", c=P)[124 * i:124 * i + 124, :])\
                    .then_inc(E("vectors_loaded"), 16)
            pool.dma_start(poolw, A["pool_w"][0].rearrange("g c d -> c g d")).then_inc(E("poolw_loaded"), 16)
            pool.dma_start(sinkb, bass.AP(tensor=A["sink_logits"].tensor, offset=0, ap=[[0, P], [1, 8]]))\
                .then_inc(E("sinks_loaded"), 16)
            wait_full(pool, "n0_t2")
            wait_full(pool, "n0_t3")
            pool.dma_start(pool_m, consts_d[:, CONST["pool2"][0]:CONST["pool2"][0] + 1536])\
                .then_inc(E("pool_m_loaded"), 16)
            pool.wait_ge(E("merged_lo"), 8)
            pool.dma_start(gfin, bass.AP(tensor=A["final_norm_g"].tensor, offset=0, ap=[[0, P], [1, DM]]))\
                .then_inc(E("gain_loaded"), 16)
            pool.dma_start(unfold, consts_d[:, CONST["unfold0"][0]:CONST["unfold3"][1]]).then_inc(E("unfold_loaded"), 16)
            pool.dma_start(keep, consts_d[:, CONST["scan_keep"][0]:CONST["scan_keep"][1]]).then_inc(E("keep_loaded"), 16)
            pool.dma_start(extr[:, 0:257], A["l0_rel_bias_2"]).then_inc(E("rel_loaded"), 16)
            pool.wait_ge(E("rel_loaded"), 16)
            nc.gpsimd.tensor_copy(extr[:, 257:384], extr[:, 256:257].broadcast_to([8, 127])).then_inc(E("rel_extended"), 1)
            pool.wait_ge(E("rel_extended"), 1)
            pool.dma_start(ext_d, extr).then_inc(E("rel_stored"), 16)
            for i in range(2):
                for j in range(2):
                    nc.gpsimd.memset(thb[:, i, 257 * j:257 * j + 1], 0.0).then_inc(E("shift_zeroed"), 1)
            two_rstds()
            pool.wait_ge(E("gained"), 4)
            pool.wait_ge(E("rel_stored"), 16)
            pool.dma_start(band, bass.AP(tensor=ext_d.tensor, offset=1, ap=[[1, P], [384, 8], [1, T]]))\
                .then_inc(E("band_loaded"), 16)
            pool.wait_ge(E("band_loaded"), 16)
            nc.gpsimd.memset(band[0:64, :, 0:64], NEG).then_inc(E("band_ready"), 1)
            wait_full(pool, "n2_t2")
            wait_full(pool, "n2_t3")
            pool.dma_start(lora[0:64, 0, :], A["l0_w2_2"]).then_inc(E("lora_loaded"), 16)
            pool.dma_start(lora[64:128, 1, :], A["l0_a2_2"]).then_inc(E("lora_loaded"), 16)
            pool.dma_start(lora[:, 2, :], A["l0_g2_2"]).then_inc(E("lora_loaded"), 16)
            wait_empty(pool, "bo0")
            wait_empty(pool, "bo1")
            for c in range(4):
                nc.gpsimd.tensor_scalar(chunks(bonus)[:, c, :], chunks(bonus)[:, c, :], vcol("l0_lnx_b_2", c), None,
                                        ALU.add).then_inc(E("bonus_shifted"), 1)
            pool.wait_ge(E("bonus_shifted"), 4)
            wait_empty(pool, "gg0")
            wait_empty(pool, "gg1")
            nc.gpsimd.tensor_tensor(bonus, bonus, gT, ALU.mult).then_inc(E("bonus_gated"), 1)
            pool.wait_ge(E("bonus_gated"), 1)
            for c in range(4):
                nc.gpsimd.tensor_scalar(chunks(gT)[:, c, :], chunks(gT)[:, c, :], vcol("l0_lnx_w_2", c), None,
                                        ALU.mult).then_inc(E("gates_folded"), 1)
            rstd(3)
            rstd(2)
            for c in range(8):
                nc.gpsimd.memset(upad[:, c, 0:PAD], 0.0).then_inc(E("pad_zeroed"), 1)
            pool.dma_start(pw2b, bass.AP(tensor=A["l1_pw2_b_2"].tensor, offset=0, ap=[[0, P], [1, DM]]))\
                .then_inc(E("pw2b_loaded"), 16)
            rstd(3)
            pool.dma_start(gfin, bass.AP(tensor=A["final_norm_2"].tensor, offset=0, ap=[[0, P], [1, DM]]))\
                .then_inc(E("gain_loaded"), 16)
            rstd(2)

        @block.scalar
        def _(act):
            chain = [0]
            unit = [0]
            ysplit = [0]

            def mark(ins):
                chain[0] += 1
                ins.then_inc(E("act_steps"), 1)

            def sync():
                act.wait_ge(E("act_steps"), chain[0])

            def split(u):
                if u >= NU:
                    return
                act.wait_ge(E(f"unit_loaded{u % RAWS}"), 16 * (u // RAWS + 1))
                if u >= WBUFS:
                    wait_unit_used(act, u - WBUFS)
                nc.scalar.activation(wh[:, u % WBUFS, :], raw[:, u % RAWS, :], ACT.Copy).then_inc(E("hi_split"), 1)

            def next_unit():
                split(unit[0] + 2)
                unit[0] += 1

            def copy_out(dst, name, cols=512, scale=1.0):
                wait_full(act, name)
                src = bank(name)[:, 0:cols]
                if len(dst.shape) == 3:
                    src = src.rearrange("p (a b) -> p a b", a=dst.shape[1])
                nc.scalar.activation(dst, src, ACT.Copy, scale=scale).then_inc(empty(name), 1)

            def squares(residual=None, gain=False):
                order = [(0, 0), (0, 1), (1, 0), (1, 1)]
                if residual and not residual.startswith("dn"):
                    order = [(0, 0), (1, 0), (0, 1), (1, 1)]
                for t, c in order:
                    if residual:
                        wait_empty(act, f"{residual}_{2 * t + c}" if residual.startswith("dn") else f"{residual}{c}_{t}")
                    nc.scalar.activation(scratch[:, t * DM + c * 512:t * DM + c * 512 + 512],
                                         xn[:, t, 512 * c:512 * c + 512], ACT.Square, scale=DM ** -0.5,
                                         accum_out=SS[:, 2 * t + c:2 * t + c + 1]).then_inc(E("squares_summed"), 1)
                    if gain:
                        act.wait_ge(E("gained"), 2 * c + t + 1)
                        h = slice(t * DM + c * 512, t * DM + c * 512 + 512)
                        nc.scalar.activation(slot(6, 2)[:, h], gained[:, h], ACT.Square, scale=DM ** -0.5,
                                             accum_out=SSG[:, 2 * t + c:2 * t + c + 1]).then_inc(E("squares_summed"), 1)

            def split_norm(tag):
                for q in range(4):
                    wait_full(act, f"{tag}_t{q}")
                    for i in range(2):
                        k = 2 * q + i
                        nc.scalar.activation(xh[:, k, :], bank(f"{tag}_t{q}")[:, i * T:(i + 1) * T], ACT.Copy,
                                             scale=vcol(GAIN[tag], k)).then_inc(E("norm_hi"), 1)

            def silu_tanh(name, k):
                wait_full(act, name)
                if k >= 2:
                    wait_empty(act, f"{'abc'[k // 2 - 1]}z{k % 2}")
                nc.scalar.activation(thb[:, k % 2, 0:512], bank(name), ACT.Tanh, scale=0.5).then_inc(E("silu_tanh"), 1)

            def split_y(chunk, n, use):
                k = ysplit[0]
                ysplit[0] += 1
                wait_empty(act, use)
                nc.scalar.activation(yh[:, chunk:chunk + n, :], chunks(ytmp[:, k % 2, 0:n * T]), ACT.Copy)\
                    .then_inc(E("y_hi"), 1)

            def exps(a):
                act.wait_ge(E("neg_max"), a + 1)
                k = a % 8
                m = NMAX[:, 2 * k:2 * k + 2]
                for i, (lo, hi) in enumerate(((0, P), (P, 384))):
                    nc.scalar.activation(att[:, a % 2, lo:hi], att[:, a % 2, lo:hi], ACT.Exp, bias=m[:, i:i + 1],
                                         accum_out=DEN[:, 2 * k + i:2 * k + i + 1]).then_inc(E("exp_done"), 1)
                if a < 8:
                    nc.scalar.activation(ES[:, 2 * k:2 * k + 2], m, ACT.Exp, bias=sinkb[:, a:a + 1])\
                        .then_inc(E("exp_done"), 1)

            def heads_step(s, base, n, with_unit=True):
                if 1 <= s <= n:
                    a = base + s - 1
                    wait_full(act, f"pt{a}")
                    if a >= 2:
                        wait_pv(act, a - 2)
                    nc.scalar.activation(ptb[:, a % 2, :], bank(f"pt{a}")[:, 0:384], ACT.Copy).then_inc(emptied[4], 1)
                if with_unit:
                    next_unit()
                if s < n:
                    exps(base + s)
                a = base + s - 2
                if s >= 2 and a % 2:
                    if base == 0:
                        split_y(4 + a // 2, 1, f"o{a // 2}")
                    else:
                        wait_full(act, f"o{a // 2}")
                        nc.scalar.activation(yh[:, 4 + (a - base) // 2, :], bank(f"o{a // 2}")[:, 0:T], ACT.Copy)\
                            .then_inc(E("o_hi"), 1)

            act.dma_start(vrows[0:8, :], vec("norm_g").rearrange("(k c) -> k c", c=P)).then_inc(E("norm_g_loaded"), 16)
            act.wait_ge(E("x_loaded"), 32)
            squares()
            split(0)
            copy_out(vt[:, 0:8], "vec0", 8)
            wait_empty(act, "vec0")
            split_norm("n0")
            split(1)
            next_unit()
            next_unit()
            copy_out(ax[:, 0, :], "ax0")
            copy_out(ax[:, 1, :], "ax1")
            for i in range(2):
                next_unit()
                silu_tanh(f"az{i}", i)
            wait_full(act, "vec1")
            mark(nc.scalar.activation(dwt[:, :], bank("vec1")[:, 0:TAPS * 8], ACT.Copy))
            nc.scalar.activation(vt[:, 8:NVROWS], bank("vec1")[:, 256 + 8:256 + NVROWS], ACT.Copy)\
                .then_inc(empty("vec1"), 1)
            wait_empty(act, "vec1")
            a, b = VROW["pool_scale"], VROW["l0_w0_2"]
            mark(nc.scalar.activation(HSCALE, vt[:, a:a + 4], ACT.Copy, scale=0.5))
            mark(nc.scalar.activation(HW0, vt[:, b:b + 4], ACT.Copy, scale=0.5))
            mark(nc.scalar.activation(HA0, vt[:, b + 4:b + 8], ACT.Copy, scale=0.5))
            b = VROW["l1_pw1_b_2"]
            mark(nc.scalar.activation(hb, vt[:, b + 8:b + 16], ACT.Copy, scale=0.5))
            b = VROW["l1_ln_w_2"]
            mark(nc.scalar.activation(hln, vt[:, b:b + 16], ACT.Copy, scale=0.5))
            b = VROW["l0_shift_mu_2"]
            nc.scalar.activation(omu, vt[:, b:b + 14], ACT.Copy, scale=-1.0, bias=1.0).then_inc(E("vec_cols_ready"), 1)
            for i in range(2):
                copy_out(pooled[:, 2 * i:2 * i + 2, :], f"pool{i}")
            for i in range(2):
                split_y(2 * i, 2, f"mix{i}")
            for i in range(2):
                next_unit()
                copy_out(bq[:, 2 * i:2 * i + 2, :], f"bq{i}")
            next_unit()
            wait_full(act, "bkv")
            for g in range(2):
                r = slice(g * HD, (g + 1) * HD)
                nc.scalar.activation(bk[r, g, :], bank("bkv")[r, 0:T], ACT.Copy).then_inc(E("keys_out"), 1)
            nc.scalar.activation(bvt, bank("bkv")[:, T:2 * T], ACT.Copy).then_inc(empty("bkv"), 1)
            act.wait_ge(E("keys_out"), 2)
            for g in range(2):
                act.dma_start(bk[(1 - g) * HD:(2 - g) * HD, g, :], bk[g * HD:(g + 1) * HD, g, :])\
                    .then_inc(E("keys_doubled"), 16)
            act.wait_ge(E("sinks_loaded"), 16)
            heads = iter(range(18))

            def step():
                s = next(heads, None)
                if s is None:
                    next_unit()
                else:
                    heads_step(s, 0, 16)

            next_unit()
            for i in range(2):
                silu_tanh(f"bz{i}", 2 + i)
                if i == 0:
                    copy_out(bv, "bv", 256)
                step()
            for i in range(2):
                copy_out(cq[:, 2 * i:2 * i + 2, :], f"cq{i}")
                step()
            for i in range(2):
                copy_out(ck[:, 2 * i:2 * i + 2, :], f"ck{i}")
                step()
            step()
            copy_out(cv[:, 0, :], "cv0")
            copy_out(cv[:, 1, :], "cv1")
            step()
            for i in range(2):
                silu_tanh(f"cz{i}", 4 + i)
                step()
            for m in range(3):
                for i in range(4):
                    name = f"g{m}_{i}"
                    wait_full(act, name)
                    if m == 0:
                        wait_full(act, "mix1")
                    else:
                        wait_empty(act, f"pr{m - 1}_{i}")
                    nc.scalar.activation(gate[:, 2 * i:2 * i + 2, :], chunks(bank(name)), ACT.Tanh, scale=0.5)\
                        .then_inc(empty(name), 1)
                    step()
                for i in range(2):
                    step()
            for k in range(8):
                act.wait_ge(E("merged"), k // 2 + 1)
                nc.scalar.activation(xh[:, k, :], merged[:, k, :], ACT.Copy, scale=0.5).then_inc(E("merged_hi"), 1)
            for _ in range(3):
                next_unit()
            squares("wo", gain=True)
            split_norm("n2")
            for i in range(2):
                next_unit()
                copy_out(q2[:, 2 * i:2 * i + 2, :], f"q2_{i}")
            for i in range(2):
                next_unit()
                copy_out(k2[:, 2 * i:2 * i + 2, :], f"k2_{i}")
            next_unit()
            next_unit()
            copy_out(v2[:, 0, :], "v2_0")
            copy_out(v2[:, 1, :], "v2_1")
            act.wait_ge(E("shift_zeroed"), 4)
            next_unit()
            for n, u in enumerate(RW_ORDER):
                name = f"rw{u}"
                wait_full(act, name)
                if n >= 2:
                    wait_empty(act, f"rw{RW_ORDER[n - 2]}")
                for j in range(2):
                    nc.scalar.activation(thb[:, n % 2, 257 * j + 1:257 * j + 257], bank(name)[:, j * T:(j + 1) * T],
                                         ACT.Copy, scale=vcol("l0_shift_mu_2", 2 * u + j)).then_inc(E("mu_part"), 1)
                heads_step(n, 16, 8, with_unit=n < 6)
                if n == 0:
                    wait_empty(act, "rw6")
                    nc.scalar.activation(xwa[0:64, :], xwa[0:64, :], ACT.Tanh).then_inc(E("xw_tanh"), 1)
                    nc.scalar.activation(xg, xg, ACT.Tanh, scale=0.5).then_inc(E("xg_tanh"), 1)
                elif n == 1:
                    for tag, dst, bias in (("z", LD, HW0), ("a", aT, HA0)):
                        for i in range(2):
                            wait_full(act, f"{tag}{i}")
                            for j in range(2):
                                c = 2 * i + j
                                ins = nc.scalar.activation(chunks(dst)[:, c, :], bank(f"{tag}{i}")[:, j * T:(j + 1) * T],
                                                           ACT.Tanh, scale=0.5, bias=bias[:, c:c + 1])
                                if j:
                                    ins.then_inc(empty(f"{tag}{i}"), 1)
                                else:
                                    mark(ins)
                    for i in range(2):
                        copy_out(gT[:, 512 * i:512 * i + 512], f"gg{i}")
                elif n == 2:
                    wait_empty(act, "rw2")
                    wait_empty(act, "rw3")
                    for c in range(4):
                        mark(nc.scalar.activation(chunks(kk)[:, c, :], kT[:, c, :], ACT.Copy, scale=vcol("l0_k_k_2", c)))
                    sync()
                    nc.scalar.activation(rk, kk, ACT.Square).then_inc(E("kk_squares"), 1)
                elif n == 3:
                    wait_full(act, "kn")
                    nc.scalar.activation(rk[:, 0:T], bank("kn")[:, 0:T], ACT.Sqrt).then_inc(empty("kn"), 1)
                elif n == 5:
                    act.wait_ge(E("prev_log"), 1)
                    nc.scalar.activation(Pc, Lc, ACT.Exp).then_inc(E("decay_exps"), 1)
                    nc.scalar.activation(Pinv, Lc, ACT.Exp, scale=-1.0).then_inc(E("decay_exps"), 1)
                    nc.scalar.activation(Pprev, Pprev, ACT.Exp).then_inc(E("decay_exps"), 1)
                    nc.scalar.activation(pcs[:, :], Lc[:, C - 1::C], ACT.Exp).then_inc(E("decay_exps"), 1)
            for n in range(7, 10):
                heads_step(n, 16, 8, with_unit=False)
            for name, dst in (("an", An), ("vn", Vn), ("kn", Kn), ("bn", Bn)):
                copy_out(dst[:, 0, :], f"nat_{name}0")
                copy_out(dst[:, 1, :], f"nat_{name}1")
            next_unit()
            for pair in range(2):
                for name, who in INVERSE:
                    for g in (2 * pair, 2 * pair + 1):
                        if who != "act":
                            continue
                        ts = tset[g % 2]
                        use = f"{name}_{g}"
                        if name == "AV":
                            wait_full(act, use)
                            tt, par = divmod(g, 2)
                            nc.scalar.activation(Z[:, 1, tt, par::2, :],
                                                 bank(use)[:, 0:256].rearrange("p (h d) -> p h d", h=4), ACT.Copy)\
                                .then_inc(empty(use), 1)
                        else:
                            copy_out(ts[{"N2": 5, "N4": 0, "D4": 1, "D8": 5, "Z1": 0, "EZ": 1}[name]], use)
            for i in range(2):
                copy_out(WT[:, :, i * P:(i + 1) * P], f"wt{i}")
            for i in range(2):
                copy_out(YT[:, :, i * P:(i + 1) * P], f"y{i}")
            for i in range(2):
                h = slice(512 * i, 512 * i + 512)
                wait_empty(act, f"gm{i}")
                nc.scalar.activation(slot(7)[:, h], slot(2)[:, h], ACT.Square).then_inc(E("gn_squares"), 1)
            wait_full(act, "gv")
            nc.scalar.activation(slot(9)[:, 0:T], bank("gv")[:, 0:T], ACT.Sqrt, scale=1.0 / HD, bias=EPSG)\
                .then_inc(empty("gv"), 1)
            next_unit()
            for i in range(2):
                act.wait_ge(E("rwkv_out"), i + 1)
                nc.scalar.activation(yh[:, 2 * i:2 * i + 2, :], chunks(slot(2))[:, 2 * i:2 * i + 2, :], ACT.Copy)\
                    .then_inc(E("rwkv_hi"), 1)
            for _ in range(2):
                next_unit()

            def ffn(tag, k0, residual):
                squares(residual)
                split_norm(tag)
                for i in range(FF_STEPS + 1):
                    if i < FF_STEPS:
                        next_unit()
                        k = k0 + i
                        name = f"up{tag}_{i}"
                        wait_full(act, name)
                        if k >= 2:
                            act.wait_ge(E("hidden_lo"), k - 1)
                        nc.scalar.activation(ytmp[:, k % 2, :], bank(name), ACT.Relu).then_inc(empty(name), 1)
                        wait_empty(act, name)
                        if i >= 3:
                            wait_unit_used(act, UID[("D", DOWN[tag], 256 * (i - 3), 0)])
                        nc.scalar.activation(yh[:, 2 * (i % 3):2 * (i % 3) + 2, :], chunks(ytmp[:, k % 2, :]),
                                             ACT.Square).then_inc(E("hidden_hi"), 1)
                    if i >= 1:
                        next_unit()

            ffn("f0", 0, "wp")
            squares("dnf0")
            split_norm("n4")
            def tap_diagonals(i):
                if i >= 2:
                    wait_full(act, f"taps{i - 2}")
                for j in range(2):
                    for tap in range(PE_TAPS):
                        w = tap * 8 + 2 * i + j
                        nc.scalar.activation(tap_diag(i, j, tap), ident, ACT.Copy, scale=dwt[:, w:w + 1])\
                            .then_inc(E("diagonals"), 1)

            def taps_out(i):
                wait_full(act, f"taps{i}")
                if i:
                    act.wait_ge(E("convolved"), 2 * i)
                for j in range(2):
                    ins = nc.scalar.activation(ytmp[:, 1, j * T:(j + 1) * T], bank(f"taps{i}")[:, j * T:(j + 1) * T],
                                               ACT.Identity, scale=0.5, bias=vcol("l1_dw_b_2", 2 * i + j))
                    if j:
                        ins.then_inc(empty(f"taps{i}"), 1)
                    else:
                        mark(ins)

            tap_diagonals(0)
            for i in range(4):
                next_unit()
                if i:
                    act.wait_ge(E("glu"), i)
                for tag, dst, fn, scale, bias in (("pa", ytmp, ACT.Identity, 1.0, lambda c: vcol("l1_pw1_b_2", c)),
                                                  ("pb", thb, ACT.Tanh, 0.5, lambda c: hb[:, c:c + 1])):
                    if tag == "pb":
                        next_unit()
                    wait_full(act, f"{tag}{i}")
                    for j in range(2):
                        ins = nc.scalar.activation(dst[:, 0, j * T:(j + 1) * T], bank(f"{tag}{i}")[:, j * T:(j + 1) * T],
                                                   fn, scale=scale, bias=bias(2 * i + j))
                        if j:
                            ins.then_inc(empty(f"{tag}{i}"), 1)
                        else:
                            mark(ins)
                if i:
                    taps_out(i - 1)
                if i < 3:
                    tap_diagonals(i + 1)
            taps_out(3)
            for k in range(4):
                if k == 3:
                    wait_empty(act, "lnm")
                else:
                    act.wait_ge(E("ln_centred"), k + 1)
                nc.scalar.activation(lnsq[:, 2 * k:2 * k + 2, :], acc[:, 2 * k:2 * k + 2, :], ACT.Square)\
                    .then_inc(E("ln_squares"), 1)
            wait_full(act, "lnv")
            nc.scalar.activation(lnsd, bank("lnv")[:, 0:T], ACT.Sqrt, scale=1.0 / DM, bias=EPSL).then_inc(empty("lnv"), 1)
            def ln_tanh(k):
                act.wait_ge(E("ln_divided"), k + 1)
                for c in (2 * k, 2 * k + 1):
                    nc.scalar.activation(lnsq[:, c, :], acc[:, c, :], ACT.Tanh, scale=hln[:, c:c + 1],
                                         bias=hln[:, 8 + c:9 + c]).then_inc(E("ln_tanh"), 1)

            def ln_hi(k):
                act.wait_ge(E("ln_silu"), k + 1)
                nc.scalar.activation(xh[:, 2 * k:2 * k + 2, :], lnsq[:, 2 * k:2 * k + 2, :], ACT.Copy, scale=0.5)\
                    .then_inc(E("ln_hi"), 1)

            ln_tanh(0), ln_tanh(1), ln_hi(0), ln_hi(1)
            ln_tanh(2), ln_tanh(3), ln_hi(2), ln_hi(3)
            for _ in range(4):
                next_unit()
            ffn("f1", FF_STEPS, "pw")
            squares("dnf1")

        @block.vector
        def _(dve):
            chain = [0]
            unit = [0]
            ysplit = [0]

            def mark(ins):
                chain[0] += 1
                ins.then_inc(E("dve_steps"), 1)
                return chain[0]

            def sync(n=None):
                dve.wait_ge(E("dve_steps"), n or chain[0])

            def split(u):
                if u >= NU:
                    return
                dve.wait_ge(E("hi_split"), u + 1)
                if u >= WBUFS:
                    wait_unit_used(dve, u - WBUFS)
                nc.vector.tensor_tensor(wl[:, u % WBUFS, :], raw[:, u % RAWS, :], wh[:, u % WBUFS, :].bitcast(F32),
                                        ALU.subtract).then_inc(E("lo_split"), 1)

            def next_unit():
                split(unit[0] + 2)
                unit[0] += 1

            norms = [0]
            xsplits = [0]

            def scale_rows(last=False):
                for s in range(NT):
                    dve.wait_ge(E("rstd_ready"), norms[0] + s + 1)
                    if last:
                        nc.vector.scalar_tensor_tensor(out=xn[:, s, :], in0=xn[:, s, :], scalar=RSTD[:, s:s + 1],
                                                       in1=gfin, op0=ALU.mult, op1=ALU.mult).then_inc(E("out_ready"), 1)
                    else:
                        nc.vector.tensor_scalar(scratch[:, s * DM:(s + 1) * DM], xn[:, s, :], RSTD[:, s:s + 1], None,
                                                ALU.mult).then_inc(E("rows_scaled"), 1)
                norms[0] += NT

            def split_norm(tag):
                for q in range(4):
                    xsplits[0] += 2
                    dve.wait_ge(E("norm_hi"), xsplits[0])
                    for i in range(2):
                        k = 2 * q + i
                        ins = nc.vector.scalar_tensor_tensor(
                            out=xl[:, k, :], in0=bank(f"{tag}_t{q}")[:, i * T:(i + 1) * T], scalar=vcol(GAIN[tag], k),
                            in1=xh[:, k, :].bitcast(F32), op0=ALU.mult, op1=ALU.subtract)
                        if i:
                            ins.then_inc(empty(f"{tag}_t{q}"), 1)
                        else:
                            mark(ins)

            def silu(name, k):
                dve.wait_ge(E("silu_tanh"), k + 1)
                nc.vector.scalar_tensor_tensor(out=sz[k // 2][:, 2 * (k % 2):2 * (k % 2) + 2, :],
                                               in0=chunks(thb[:, k % 2, 0:512]), scalar=1.0, in1=chunks(bank(name)),
                                               op0=ALU.add, op1=ALU.mult).then_inc(empty(name), 1)

            def split_y(chunk, n):
                k = ysplit[0]
                ysplit[0] += 1
                dve.wait_ge(E("y_hi"), k + 1)
                nc.vector.tensor_tensor(yl[:, chunk:chunk + n, :], chunks(ytmp[:, k % 2, 0:n * T]),
                                        yh[:, chunk:chunk + n, :].bitcast(F32), ALU.subtract).then_inc(E("y_lo"), 1)

            def scores(a):
                k = a % 8
                buf = att[:, a % 2, :]
                wait_full(dve, f"sc{a}")
                if a >= 2:
                    wait_full(dve, f"pt{a - 2}")
                src = bank(f"sc{a}")
                if a < 16:
                    mask = const("mask_swa" if a < 8 else "mask_causal")
                    nc.vector.scalar_tensor_tensor(out=buf, in0=src[:, 0:384], scalar=SCALE, in1=mask, op0=ALU.mult,
                                                   op1=ALU.add).then_inc(empty(f"sc{a}"), 1)
                else:
                    b = band[:, a - 16, :]
                    mark(nc.vector.scalar_tensor_tensor(out=buf[:, 0:P], in0=src[:, 0:P], scalar=SCALE,
                                                        in1=b[:, P - 1::-1], op0=ALU.mult, op1=ALU.add))
                    nc.vector.scalar_tensor_tensor(out=buf[:, P:384], in0=src[:, P:384], scalar=SCALE,
                                                   in1=b[:, T - 1::-1], op0=ALU.mult, op1=ALU.add)\
                        .then_inc(empty(f"sc{a}"), 1)
                wait_empty(dve, f"sc{a}")
                mark(nc.vector.reduce_max(ES[:, 2 * k:2 * k + 1], buf[:, 0:P], AX_X))
                mark(nc.vector.reduce_max(ES[:, 2 * k + 1:2 * k + 2], buf[:, P:384], AX_X))
                sync()
                if a < 8:
                    nc.vector.tensor_scalar(NMAX[:, 2 * k:2 * k + 2], ES[:, 2 * k:2 * k + 2], sinkb[:, a:a + 1], -1.0,
                                            ALU.max, ALU.mult).then_inc(E("neg_max"), 1)
                else:
                    nc.vector.tensor_scalar(NMAX[:, 2 * k:2 * k + 2], ES[:, 2 * k:2 * k + 2], -1.0, None, ALU.mult)\
                        .then_inc(E("neg_max"), 1)

            def probabilities(a):
                k = a % 8
                dve.wait_ge(E("exp_done"), exps_done(a))
                den = DEN[:, 2 * k:2 * k + 2]
                if a < 8:
                    mark(nc.vector.tensor_tensor(den, den, ES[:, 2 * k:2 * k + 2], ALU.add))
                    sync()
                mark(nc.vector.reciprocal(den, den))
                sync()
                for i, (lo, hi) in enumerate(((0, P), (P, 384))):
                    nc.vector.tensor_scalar(att[:, a % 2, lo:hi], att[:, a % 2, lo:hi], den[:, i:i + 1], None, ALU.mult)\
                        .then_inc(E("probs_ready"), 1)

            def heads_step(s, base, n):
                if s < n:
                    scores(base + s)
                a = base + s - 2
                if s >= 2 and a % 2:
                    pair = a // 2
                    if base == 0:
                        k = ysplit[0]
                        wait_full(dve, f"o{pair}")
                        nc.vector.scalar_tensor_tensor(out=ytmp[:, k % 2, 0:T], in0=bank(f"o{pair}")[:, 0:T], scalar=0.5,
                                                       in1=sz[1 + pair // 4][:, pair % 4, :], op0=ALU.mult, op1=ALU.mult)\
                            .then_inc(empty(f"o{pair}"), 1)
                        split_y(4 + pair, 1)
                    else:
                        c = 4 + pair - base // 2
                        dve.wait_ge(E("o_hi"), pair - base // 2 + 1)
                        nc.vector.tensor_tensor(yl[:, c, :], bank(f"o{pair}")[:, 0:T], yh[:, c, :].bitcast(F32),
                                                ALU.subtract).then_inc(empty(f"o{pair}"), 1)

            def heads_after(s, base, n):
                if s < n:
                    probabilities(base + s)

            scale_rows()
            split(0)
            split_norm("n0")
            split(1)
            next_unit()
            next_unit()
            for i in range(2):
                next_unit()
                silu(f"az{i}", i)
            dve.wait_ge(E("vec_cols_ready"), 1)
            for i in range(2):
                wait_full(dve, f"mix{i}")
                for j in range(2):
                    g = 2 * i + j
                    ins = nc.vector.scalar_tensor_tensor(
                        out=ytmp[:, i, j * T:(j + 1) * T], in0=bank(f"mix{i}")[:, j * T:(j + 1) * T],
                        scalar=HSCALE[:, g:g + 1], in1=sz[0][:, g, :], op0=ALU.mult, op1=ALU.mult)
                    if j:
                        ins.then_inc(empty(f"mix{i}"), 1)
                    else:
                        mark(ins)
                split_y(2 * i, 2)
            for i in range(3):
                next_unit()
            head = [0]

            def step():
                if head[0] < 18:
                    heads_step(head[0], 0, 16)

            def after():
                next_unit()
                heads_after(head[0], 0, 16)
                head[0] += 1

            next_unit()
            for i in range(2):
                silu(f"bz{i}", 2 + i)
                step()
                after()
            for i in range(6):
                step()
                after()
            for i in range(2):
                silu(f"cz{i}", 4 + i)
                step()
                after()
            for m in range(3):
                for i in range(4):
                    step()
                    after()
                for i in range(2):
                    step()
                    for j in range(2):
                        q = 2 * i + j
                        name = f"pr{m}_{q}"
                        wait_full(dve, name)
                        wait_empty(dve, f"g{m}_{q}")
                        dst = merged[:, 2 * q:2 * q + 2, :] if m == 0 else chunks(thb[:, q % 2, 0:512])
                        nc.vector.scalar_tensor_tensor(out=dst, in0=gate[:, 2 * q:2 * q + 2, :], scalar=1.0,
                                                       in1=chunks(bank(name)), op0=ALU.add, op1=ALU.mult)\
                            .then_inc(empty(name), 1)
                        if m:
                            wait_empty(dve, name)
                            if m == 1:
                                wait_empty(dve, f"pr0_{q}")
                            else:
                                dve.wait_ge(E("gated"), q + 1)
                            nc.vector.tensor_tensor(merged[:, 2 * q:2 * q + 2, :], merged[:, 2 * q:2 * q + 2, :], dst,
                                                    ALU.add).then_inc(E("merged" if m == 2 else "gated"), 1)
                    after()
            for k in range(8):
                dve.wait_ge(E("merged_hi"), k + 1)
                nc.vector.scalar_tensor_tensor(out=xl[:, k, :], in0=merged[:, k, :], scalar=0.5,
                                               in1=xh[:, k, :].bitcast(F32), op0=ALU.mult, op1=ALU.subtract)\
                    .then_inc(E("merged_lo"), 1)
            def add_residual(tag, split_before=0, gain=False):
                for c in range(2):
                    for i in range(2):
                        if 2 * c + i >= split_before:
                            next_unit()
                    for s in range(NT):
                        name = f"{tag}{c}_{s}"
                        wait_full(dve, name)
                        nc.vector.tensor_tensor(xn[:, s, 512 * c:512 * c + 512], xn[:, s, 512 * c:512 * c + 512],
                                                bank(name), ALU.add).then_inc(empty(name), 1)
                        if gain:
                            dve.wait_ge(E("gain_loaded"), 16)
                            wait_empty(dve, name)
                            nc.vector.tensor_tensor(gained[:, s * DM + 512 * c:s * DM + 512 * c + 512],
                                                    xn[:, s, 512 * c:512 * c + 512], gfin[:, 512 * c:512 * c + 512],
                                                    ALU.mult).then_inc(E("gained"), 1)

            add_residual("wo", split_before=1, gain=True)
            dve.wait_ge(E("gained"), 4)
            for s in range(NT):
                dve.wait_ge(E("rstd_ready"), norms[0] + s + 1)
                nc.vector.tensor_scalar(scratch[:, s * DM:(s + 1) * DM], gained[:, s * DM:(s + 1) * DM], R12[:, s:s + 1], None,
                                        ALU.mult).then_inc(E("rows_scaled"), 1)
            norms[0] += NT
            split_norm("n2")
            for s in range(NT):
                mark(nc.vector.tensor_scalar(xn[:, s, :], gained[:, s * DM:(s + 1) * DM], RSTD[:, s:s + 1], None, ALU.mult))
            sync()
            for i in range(6):
                next_unit()
            dve.wait_ge(E("band_ready"), 1)
            next_unit()
            for n, u in enumerate(RW_ORDER):
                dve.wait_ge(E("mu_part"), 2 * n + 2)
                name = f"rw{u}"
                for j in range(2):
                    c = 2 * u + j
                    dst = (rT, kT, vT)[c // 4][:, c % 4, :] if c < 12 else (xwa, xg)[c - 12]
                    ins = nc.vector.scalar_tensor_tensor(
                        out=dst, in0=bank(name)[:, j * T:(j + 1) * T], scalar=omu[:, c:c + 1],
                        in1=thb[:, n % 2, 257 * j:257 * j + T], op0=ALU.mult, op1=ALU.add)
                    if j:
                        ins.then_inc(empty(name), 1)
                    else:
                        mark(ins)
                heads_step(n, 16, 8)
                if n < 6:
                    next_unit()
                heads_after(n, 16, 8)
                if n == 0:
                    dve.wait_ge(E("xg_tanh"), 1)
                    nc.vector.tensor_scalar(xg, xg, 1.0, 0.5, ALU.add, ALU.mult).then_inc(E("xg_ready"), 1)
                elif n == 2:
                    wait_empty(dve, "z0")
                    wait_empty(dve, "z1")
                    mark(nc.vector.tensor_scalar(LD, LD, 1.0, -0.5 * DECAY, ALU.add, ALU.mult))
                    wait_empty(dve, "a0")
                    wait_empty(dve, "a1")
                    mark(nc.vector.tensor_scalar(aT, aT, 1.0, 0.5, ALU.add, ALU.mult))
                    dve.wait_ge(E("keep_loaded"), 16)
                    sync()
                    nc.vector.tensor_tensor_scan(Lc, keep, LD, 0.0, ALU.mult, ALU.add).then_inc(E("cumulated"), 1)
                elif n == 3:
                    dve.wait_ge(E("cumulated"), 1)
                    nc.vector.tensor_tensor(Pprev, Lc, LD, ALU.subtract).then_inc(E("prev_log"), 1)
                    wait_empty(dve, "kn")
                    mark(nc.vector.tensor_scalar(rk[:, 0:T], rk[:, 0:T], 1e-12, None, ALU.max))
                    sync()
                    nc.vector.reciprocal(rk[:, 0:T], rk[:, 0:T]).then_inc(E("key_norms"), 1)
                elif n == 5:
                    for i in range(2):
                        h = slice(512 * i, 512 * i + 512)
                        wait_full(dve, f"kn_b{i}")
                        nc.vector.tensor_tensor(kk[:, h], kk[:, h], bank(f"kn_b{i}"), ALU.mult)\
                            .then_inc(empty(f"kn_b{i}"), 1)
            wait_full(dve, "rw5")
            for n in range(7, 10):
                heads_step(n, 16, 8)
                if n == 7:
                    for c in range(4):
                        mark(nc.vector.tensor_scalar(chunks(rk)[:, c, :], chunks(aT)[:, c, :], 1.0, vcol("l0_k_a_2", c),
                                                     ALU.subtract, ALU.mult))
                    sync()
                    mark(nc.vector.scalar_tensor_tensor(out=slot(1), in0=rk, scalar=1.0, in1=slot(1), op0=ALU.add,
                                                        op1=ALU.mult))
                heads_after(n, 16, 8)
                if n == 7:
                    sync()
                    mark(nc.vector.tensor_tensor(rk, slot(0), slot(1), ALU.mult))
                    dve.wait_ge(E("decay_exps"), 4)
                    wait_empty(dve, "kn_b0")
                    wait_empty(dve, "kn_b1")
                    nc.vector.scalar_tensor_tensor(out=aTil, in0=kk, scalar=-1.0, in1=Pprev, op0=ALU.mult, op1=ALU.mult)\
                        .then_inc(E("scaled_keys"), 1)
                elif n == 8:
                    sync()
                    for c in range(4):
                        nc.vector.tensor_scalar(chunks(rk)[:, c, :], chunks(rk)[:, c, :], vcol("l0_r_k_2", c), None,
                                                ALU.mult).then_inc(E("bonus_terms"), 1)
                    mark(nc.vector.tensor_tensor(aT, aT, kk, ALU.mult))
                    mark(nc.vector.tensor_tensor(slot(1), slot(1), Pinv, ALU.mult))
            sync()
            wait_full(dve, "sc23")
            wait_empty(dve, "sc22")
            wait_empty(dve, "sc23")

            def by_chunk(ap):
                return ap.rearrange("p (c t) -> p c t", t=C)

            pcb = pcs[:, :].rearrange("p (c o) -> p c o", o=1).broadcast_to([P, 32, C])
            nc.vector.tensor_tensor(by_chunk(kHat), by_chunk(kTil), pcb, ALU.mult).then_inc(E("scaled_keys"), 1)
            nc.vector.tensor_tensor(bTil, aT, Pinv, ALU.mult).then_inc(E("scaled_keys"), 1)
            dve.wait_ge(E("scaled_keys"), 3)
            nc.vector.tensor_tensor(by_chunk(bHat), by_chunk(bTil), pcb, ALU.mult).then_inc(E("scaled_keys"), 1)
            nc.vector.tensor_tensor(rTil, rTil, Pc, ALU.mult).then_inc(E("scaled_keys"), 1)
            for i in range(2):
                wait_full(dve, f"bo{i}")
                nc.vector.tensor_tensor(bonus[:, 512 * i:512 * i + 512], bank(f"bo{i}"), slot(2)[:, 512 * i:512 * i + 512],
                                        ALU.mult).then_inc(empty(f"bo{i}"), 1)
            next_unit()
            wait_empty(dve, "bo1")
            wait_full(dve, "nat_bn1")

            def four(ap):
                return ap.rearrange("p (h t) -> p h t", h=4)

            def masked(dst, use, mask, last=True):
                m = const(mask).rearrange("p (o t) -> p o t", o=1).broadcast_to([P, 4, P])
                ins = nc.vector.tensor_tensor(four(dst), four(bank(use)), m, ALU.mult)
                if last:
                    ins.then_inc(empty(use), 1)
                else:
                    mark(ins)

            for pair in range(2):
                for name, who in INVERSE:
                    for g in (2 * pair, 2 * pair + 1):
                        if who != "dve":
                            continue
                        use = f"{name}_{g}"
                        ts = tset[g % 2]
                        wait_full(dve, use)
                        if name == "GN":
                            if pair:
                                wait_empty(dve, f"ZZ_{g - 2}")
                            masked(ts[0], use, "up16", last=False)
                            masked(ts[2], use, "cross")
                            sync()
                            idb = ident.rearrange("p (o t) -> p o t", o=1).broadcast_to([P, 4, P])
                            nc.vector.tensor_tensor(four(ts[4]), four(ts[0]), idb, ALU.add).then_inc(E("series_begun"), 1)
                        elif name == "GA":
                            masked(ts[3], use, "up32")
                        elif name == "GD":
                            masked(ts[1], use, "low16")
                        elif name == "D2":
                            nc.vector.tensor_copy(ts[3], bank(use)).then_inc(empty(use), 1)
                        elif name in ("X2", "X4", "X8"):
                            if name == "X2":
                                dve.wait_ge(E("series_begun"), g + 1)
                            else:
                                wait_empty(dve, f"X{int(name[1]) // 2}_{g}")
                            nc.vector.tensor_tensor(ts[4], ts[4], bank(use), ALU.add).then_inc(empty(use), 1)
                        elif name == "ZZ":
                            tt, par = divmod(g, 2)
                            wait_empty(dve, f"Z1_{g}")
                            nc.vector.tensor_tensor(Z[:, :, tt, par::2, :].rearrange("p w h d -> p h w d"),
                                                    bank(use).rearrange("p (h w d) -> p h w d", h=4, w=2),
                                                    ts[0].rearrange("p (h w d) -> p h w d", h=4, w=2), ALU.add)\
                                .then_inc(empty(use), 1)
            nc.vector.memset(S(0), 0.0).then_inc(E("state_zeroed"), 1)
            dve.wait_ge(E("state_zeroed"), 1)
            halves = (("e", slice(0, HD)), ("o", slice(HD, P)))
            for c in range(NCH):
                tt, pb = c // 4, 32 * (c % 4)
                if c < NCH - 1:
                    pc1 = pcs[:, c::NCH].rearrange("p (c o) -> p c o", o=1).broadcast_to([P, 4, HD])
                    decayed = thb[:, 0, 0:256].rearrange("p (c d) -> p c d", c=4)
                    for par, rows in halves:
                        if c:
                            wait_empty(dve, f"st{par}{c - 1}")
                        mark(nc.vector.tensor_tensor(decayed[rows], S(c).rearrange("p (c d) -> p c d", c=4)[rows],
                                                     pc1[rows], ALU.mult))
                if c == 0:
                    wait_empty(dve, "wt1")
                for i, (par, _) in enumerate(halves):
                    wait_full(dve, f"sa{par}{c}")
                    dst = SA[pb:pb + C, tt, :].rearrange("p (h d) -> p h d", h=8)[:, i::2, :]
                    nc.vector.tensor_tensor(dst, bank(f"sa{par}{c}")[pb:pb + C, 0:256].rearrange("p (h d) -> p h d", h=4),
                                            Z[pb:pb + C, 1, tt, i::2, :], ALU.add).then_inc(empty(f"sa{par}{c}"), 1)
                if c < NCH - 1:
                    for par, rows in halves:
                        wait_full(dve, f"st{par}{c}")
                        sync()
                        nc.vector.tensor_tensor(S(c + 1)[rows], bank(f"st{par}{c}")[rows, 0:256], thb[rows, 0, 0:256],
                                                ALU.add).then_inc(empty(f"st{par}{c}"), 1)
                tag, g = PRODUCTS[c]
                wait_full(dve, f"{tag}_{g}")
                off = 512 * (tag == "A4")
                masked(products(g)[:, off:off + 512], f"{tag}_{g}", "upinc32")
            wait_empty(dve, "y1")
            wait_empty(dve, "y0")
            for i in range(2):
                wait_full(dve, f"gm{i}")
                nc.vector.scalar_tensor_tensor(out=slot(2)[:, 512 * i:512 * i + 512], in0=bank(f"gm{i}"), scalar=-1.0 / HD,
                                               in1=LD[:, 512 * i:512 * i + 512], op0=ALU.mult, op1=ALU.add)\
                    .then_inc(empty(f"gm{i}"), 1)
            wait_empty(dve, "gm0")
            wait_empty(dve, "gm1")
            wait_empty(dve, "gv")
            nc.vector.reciprocal(slot(9)[:, 0:T], slot(9)[:, 0:T]).then_inc(E("group_rstd"), 1)
            next_unit()
            dve.wait_ge(E("gates_folded"), 4)

            def halves_of(ap):
                return [ap[:, 0:512], ap[:, 512:1024]]

            y2, folded, shift = (halves_of(ap) for ap in (slot(2), gT, bonus))
            for i in range(2):
                wait_full(dve, f"gv_b{i}")
                nc.vector.tensor_tensor(y2[i], y2[i], bank(f"gv_b{i}"), ALU.mult).then_inc(empty(f"gv_b{i}"), 1)
            for i in range(2):
                wait_empty(dve, f"gv_b{i}")
                mark(nc.vector.tensor_tensor(y2[i], y2[i], folded[i], ALU.mult))
            sync()
            for i in range(2):
                nc.vector.tensor_tensor(y2[i], y2[i], shift[i], ALU.add).then_inc(E("rwkv_out"), 1)
            for i in range(2):
                dve.wait_ge(E("rwkv_hi"), i + 1)
                nc.vector.tensor_tensor(yl[:, 2 * i:2 * i + 2, :], chunks(slot(2))[:, 2 * i:2 * i + 2, :],
                                        yh[:, 2 * i:2 * i + 2, :].bitcast(F32), ALU.subtract).then_inc(E("rwkv_lo"), 1)
            add_residual("wp", split_before=2)

            def ffn(tag, k0):
                scale_rows()
                split_norm(tag)
                for i in range(FF_STEPS + 1):
                    if i < FF_STEPS:
                        next_unit()
                        k = k0 + i
                        hid = ytmp[:, k % 2, :]
                        dve.wait_ge(E("hidden_hi"), k + 1)
                        mark(nc.vector.tensor_tensor(hid, hid, hid, ALU.mult))
                        sync()
                        nc.vector.tensor_tensor(yl[:, 2 * (i % 3):2 * (i % 3) + 2, :], chunks(hid),
                                                yh[:, 2 * (i % 3):2 * (i % 3) + 2, :].bitcast(F32), ALU.subtract)\
                            .then_inc(E("hidden_lo"), 1)
                    if i >= 1:
                        next_unit()
                for s in range(NT):
                    for c in range(2):
                        name = f"dn{tag}_{2 * s + c}"
                        wait_full(dve, name)
                        nc.vector.tensor_tensor(xn[:, s, 512 * c:512 * c + 512], xn[:, s, 512 * c:512 * c + 512],
                                                bank(name), ALU.add).then_inc(empty(name), 1)

            ffn("f0", 0)
            scale_rows()
            split_norm("n4")
            dve.wait_ge(E("pad_zeroed"), 8)
            def glu(i):
                wait_empty(dve, f"pa{i}")
                wait_empty(dve, f"pb{i}")
                nc.vector.scalar_tensor_tensor(out=upad[:, 2 * i:2 * i + 2, PAD:PAD + T], in0=chunks(thb[:, 0, 0:512]),
                                               scalar=1.0, in1=chunks(ytmp[:, 0, :]), op0=ALU.add, op1=ALU.mult)\
                    .then_inc(E("glu"), 1)

            next_unit()
            next_unit()
            glu(0)
            taps = [0] * 8
            for i in range(4):
                dve.wait_ge(E("glu"), i + 1)
                for tap in range(PE_TAPS, TAPS):
                    for c in (2 * i, 2 * i + 1):
                        src, w = upad[:, c, tap:tap + T], dwt[:, tap * 8 + c:tap * 8 + c + 1]
                        if tap == PE_TAPS:
                            taps[c] = mark(nc.vector.tensor_scalar(acc[:, c, :], src, w, None, ALU.mult))
                        else:
                            sync(taps[c])
                            taps[c] = mark(nc.vector.scalar_tensor_tensor(out=acc[:, c, :], in0=src, scalar=w,
                                                                          in1=acc[:, c, :], op0=ALU.mult, op1=ALU.add))
                    if i < 3 and tap == PE_TAPS + 8:
                        next_unit()
                    if i < 3 and tap == PE_TAPS + 13:
                        next_unit()
                        glu(i + 1)
                wait_empty(dve, f"taps{i}")
                for j in range(2):
                    c = 2 * i + j
                    sync(taps[c])
                    nc.vector.scalar_tensor_tensor(out=acc[:, c, :], in0=acc[:, c, :], scalar=0.5,
                                                   in1=ytmp[:, 1, j * T:(j + 1) * T], op0=ALU.mult, op1=ALU.add)\
                        .then_inc(E("convolved"), 1)
            wait_full(dve, "lnm")

            def on_pairs(col):
                return col.rearrange("p (o t) -> p o t", o=1).broadcast_to([P, 2, T])

            for k in range(4):
                ins = nc.vector.scalar_tensor_tensor(out=acc[:, 2 * k:2 * k + 2, :], in0=on_pairs(bank("lnm")[:, 0:T]),
                                                     scalar=-1.0 / DM, in1=acc[:, 2 * k:2 * k + 2, :], op0=ALU.mult,
                                                     op1=ALU.add)
                ins.then_inc(empty("lnm") if k == 3 else E("ln_centred"), 1)
            wait_empty(dve, "lnv")
            dve.wait_ge(E("ln_centred"), 3)
            wait_empty(dve, "lnm")
            mark(nc.vector.reciprocal(lnsd, lnsd))
            sync()
            def ln_divide(k):
                nc.vector.tensor_tensor(acc[:, 2 * k:2 * k + 2, :], acc[:, 2 * k:2 * k + 2, :], on_pairs(lnsd), ALU.mult)\
                    .then_inc(E("ln_divided"), 1)

            def ln_silu(k):
                dve.wait_ge(E("ln_tanh"), 2 * k + 2)
                for c in (2 * k, 2 * k + 1):
                    mark(nc.vector.tensor_scalar(acc[:, c, :], acc[:, c, :], vcol("l1_ln_w_2", c), vcol("l1_ln_b_2", c),
                                                 ALU.mult, ALU.add))
                sync()
                nc.vector.scalar_tensor_tensor(out=lnsq[:, 2 * k:2 * k + 2, :], in0=lnsq[:, 2 * k:2 * k + 2, :], scalar=1.0,
                                               in1=acc[:, 2 * k:2 * k + 2, :], op0=ALU.add, op1=ALU.mult)\
                    .then_inc(E("ln_silu"), 1)

            def ln_lo(k):
                dve.wait_ge(E("ln_hi"), k + 1)
                nc.vector.scalar_tensor_tensor(out=xl[:, 2 * k:2 * k + 2, :], in0=lnsq[:, 2 * k:2 * k + 2, :], scalar=0.5,
                                               in1=xh[:, 2 * k:2 * k + 2, :].bitcast(F32), op0=ALU.mult,
                                               op1=ALU.subtract).then_inc(E("ln_lo"), 1)

            ln_divide(0), ln_divide(1), ln_silu(0), ln_silu(1), ln_lo(0), ln_lo(1)
            ln_divide(2), ln_divide(3), ln_silu(2), ln_silu(3), ln_lo(2), ln_lo(3)
            dve.wait_ge(E("pw2b_loaded"), 16)
            for s in range(NT):
                mark(nc.vector.tensor_tensor(xn[:, s, :], xn[:, s, :], pw2b, ALU.add))
            sync()
            add_residual("pw")
            ffn("f1", FF_STEPS)
            dve.wait_ge(E("gain_loaded"), 32)
            scale_rows(last=True)

        @block.tensor
        def _(pe):
            mm = nc.tensor.matmul
            seen = [0] * 8
            unit = [0]

            def take(name):
                b, n = PL.uses[name]
                assert n == seen[b], name
                seen[b] += 1
                if n:
                    pe.wait_ge(emptied[b], n)
                return bank(name)

            def give(ins, name):
                ins.then_inc(full(name), 1)

            def wait_chunk(source, k):
                if source == "merged":
                    pe.wait_ge(E("merged_lo"), k + 1)
                elif source == "ln":
                    pe.wait_ge(E("ln_lo"), k // 2 + 1)
                elif source == "rwkv":
                    pe.wait_ge(E("rwkv_lo"), k // 2 + 1)
                elif source:
                    wait_empty(pe, f"{source}_t{k // 2}")

            def three(out, hh, hl, mh, ml, start, stop):
                mm(out, hh, mh, start=start, stop=False)
                mm(out, hh, ml, start=False, stop=False)
                return mm(out, hl, mh, start=False, stop=stop)

            def arrived(u):
                assert u == unit[0], (u, unit)
                unit[0] += 1
                pe.wait_ge(E("hi_split"), u + 1)
                pe.wait_ge(E("lo_split"), u + 1)

            def w_views(u, cols):
                return (wh[:, u % WBUFS, :].rearrange("p (j n) -> p j n", n=cols),
                        wl[:, u % WBUFS, :].rearrange("p (j n) -> p j n", n=cols))

            def t_unit(name, source=None):
                u = unit[0]
                arrived(u)
                h, l = w_views(u, 256)
                out = take(name)
                for t in range(2):
                    for k in range(KC):
                        if t == 0:
                            wait_chunk(source, k)
                        c = slice(t * P, (t + 1) * P)
                        ins = three(out[:, t * T:(t + 1) * T], h[:, k, c], l[:, k, c], xh[:, k, :], xl[:, k, :],
                                    k == 0, k == KC - 1)
                give(ins, name)

            def th_unit(names, chunk):
                u = unit[0]
                arrived(u)
                h, l = w_views(u, 512)
                for t in range(4):
                    if t % 2 == 0:
                        out = take(names[t // 2])
                    for k in range(4):
                        c = slice(t * P, (t + 1) * P)
                        ins = three(out[:, (t % 2) * T:(t % 2 + 1) * T], h[:, k, c], l[:, k, c], yh[:, chunk + k, :],
                                    yl[:, chunk + k, :], k == 0, k == 3)
                    if t % 2:
                        give(ins, names[t // 2])

            def nat_unit(names, half, ah=xh, al=xl, source=None, turn=None, part=None):
                turn = half if turn is None else turn
                u = unit[0]
                if part != 1:
                    arrived(u)
                else:
                    u -= 1
                h, l = w_views(u, 512)
                for s in range(NT) if part is None else (part,):
                    out = bank(names[s]) if turn else take(names[s])
                    for k in range(4):
                        c, rows = 4 * half + k, slice(s * P, (s + 1) * P)
                        if s == 0:
                            wait_chunk(source, c)
                        ins = three(out, ah[:, c, rows], al[:, c, rows], h[:, k, :], l[:, k, :],
                                    turn == 0 and k == 0, turn == 1 and k == 3)
                    if turn:
                        give(ins, names[s])
                if not turn and part != 0:
                    ins.then_inc(E("unit_summed"), 1)

            def proj_out(tag, ah, al, source=None):
                for c in range(2):
                    for half in range(2):
                        nat_unit((f"{tag}{c}_0", f"{tag}{c}_1"), half, ah, al, None if c else source)

            rows_scaled = [0]

            def norm_transposes(tag):
                for s in range(NT):
                    rows_scaled[0] += 1
                    pe.wait_ge(E("rows_scaled"), rows_scaled[0])
                    for q in range(4):
                        out = take(f"{tag}_t{q}") if s == 0 else bank(f"{tag}_t{q}")
                        for i in range(2):
                            k = 2 * q + i
                            ins = nc.tensor.transpose(out[:, i * T + s * P:i * T + s * P + P],
                                                      scratch[:, s * DM + k * P:s * DM + k * P + P], ident)
                        if s:
                            give(ins, f"{tag}_t{q}")

            def heads_step(s, base, n):
                if s < n:
                    a = base + s
                    q, k, _ = head_views(a)
                    out = take(f"sc{a}")
                    mm(out[:, 0:P], q[:, 0:P], k[:, 0:P], start=True, stop=True)
                    give(mm(out[:, P:384], q[:, P:T], k, start=True, stop=True), f"sc{a}")
                if 1 <= s <= n:
                    a = base + s - 1
                    pe.wait_ge(E("probs_ready"), 2 * (a + 1))
                    out = take(f"pt{a}")
                    for i in range(3):
                        ins = nc.tensor.transpose(out[:, i * P:(i + 1) * P], att[:, a % 2, i * P:(i + 1) * P], ident)
                    give(ins, f"pt{a}")
                if s >= 2:
                    a = base + s - 2
                    h = a % 8
                    _, _, v = head_views(a)
                    name = f"o{a // 2}"
                    out = take(name) if a % 2 == 0 else bank(name)
                    out = out[HD * (h % 2):HD * (h % 2) + HD, 0:T]
                    wait_empty(pe, f"pt{a}")
                    p = ptb[:, a % 2, :]
                    mm(out, v[:, 0, :], p[:, 0:T], start=True, stop=False)
                    ins = mm(out[:, P:T], v[:, 1, :], p[:, T:384], start=False, stop=True)
                    if a % 2 == 0:
                        ins.then_inc(E("pv_even"), 1)
                    else:
                        give(ins, name)

            pe.wait_ge(E("consts_loaded"), 16)
            pe.wait_ge(E("norm_g_loaded"), 16)
            out = take("vec0")
            give(nc.tensor.transpose(out[:, 0:8], vrows[0:8, :], ident[0:8, 0:8]), "vec0")
            norm_transposes("n0")
            nat_unit(("ax0", "ax1"), 0, source="n0")
            nat_unit(("ax0", "ax1"), 1, source="n0")
            t_unit("az0")
            t_unit("az1")
            pe.wait_ge(E("vectors_loaded"), 16 * (len(VECS) + 1))
            out = take("vec1")
            for i in range(2):
                ins = nc.tensor.transpose(out[:, 124 * i:124 * i + 124], dwrows[0:124, i * P:(i + 1) * P],
                                          ident[0:124, 0:124])
            ins = nc.tensor.transpose(out[:, 256:256 + NVROWS], vrows[0:NVROWS, :], ident[0:NVROWS, 0:NVROWS])
            give(ins, "vec1")
            pe.wait_ge(E("pool_m_loaded"), 16)
            pe.wait_ge(E("poolw_loaded"), 16)
            wait_empty(pe, "ax0")
            wait_empty(pe, "ax1")
            for i in range(2):
                out = take(f"pool{i}")
                for j in range(2):
                    g = 2 * i + j
                    m = pool_m[:, g * T:(g + 1) * T]
                    o = out[:, j * T:(j + 1) * T]
                    mm(o, ax[:, 0, g * P:(g + 1) * P], m, start=True, stop=False)
                    ins = mm(o[:, P:T], ax[:, 1, g * P:(g + 1) * P], late[:, g * P:(g + 1) * P], start=False, stop=True)
                give(ins, f"pool{i}")
            for i in range(2):
                out = take(f"mix{i}")
                wait_empty(pe, f"pool{i}")
                for j in range(2):
                    g = 2 * i + j
                    ins = mm(out[:, j * T:(j + 1) * T], poolw[:, g, :], pooled[:, g, :], start=True, stop=True)
                give(ins, f"mix{i}")
            t_unit("bq0")
            t_unit("bq1")
            t_unit("bkv")
            heads = iter(range(18))

            def step():
                s = next(heads, None)
                if s is not None:
                    heads_step(s, 0, 16)
                if s == 7:
                    wait_empty(pe, "cq0"), wait_empty(pe, "cq1"), wait_empty(pe, "ck0"), wait_empty(pe, "ck1")
                if s == 9:
                    wait_empty(pe, "cv0"), wait_empty(pe, "cv1")

            for name in ("bz0", "bz1", "cq0", "cq1", "ck0", "ck1"):
                t_unit(name)
                if name == "bz0":
                    out = take("bv")
                    wait_empty(pe, "bkv")
                    for s in range(NT):
                        ins = nc.tensor.transpose(out[:, s * P:(s + 1) * P], bvt[:, s * P:(s + 1) * P], ident)
                    give(ins, "bv")
                    wait_empty(pe, "bv")
                    pe.wait_ge(E("keys_doubled"), 32)
                step()
            for half in range(2):
                nat_unit(("cv0", "cv1"), half)
                step()
            for name in ("cz0", "cz1"):
                t_unit(name)
                step()
            for m in range(3):
                for i in range(4):
                    t_unit(f"g{m}_{i}")
                    step()
                if m == 0:
                    pe.wait_ge(E("y_lo"), 2)
                else:
                    pe.wait_ge(E("y_lo"), 2 + 4 * m)
                for i in range(2):
                    th_unit((f"pr{m}_{2 * i}", f"pr{m}_{2 * i + 1}"), 4 * m)
                    step()
            proj_out("wo", xh, xl, "merged")
            norm_transposes("n2")
            for name in ("q2_0", "q2_1", "k2_0", "k2_1"):
                t_unit(name, "n2" if name == "q2_0" else None)
            for half in range(2):
                nat_unit(("v2_0", "v2_1"), half)
            head_ones = const("head_ones")

            def head_rows(use, src):
                out = take(use)
                for p in range(4):
                    if use == "gv":
                        pe.wait_ge(E("gn_squares"), p // 2 + 1)
                    ins = mm(out[32 * p:32 * p + 32, 0:T], head_ones[:, 48:80], src[:, p * T:(p + 1) * T],
                             start=True, stop=True)
                give(ins, use)

            def unfold_rows(use, src):
                for i in range(2):
                    out = take(f"{use}{i}")
                    for j in range(2):
                        p = 2 * i + j
                        ins = mm(out[:, j * T:(j + 1) * T], unfold[:, p * P:(p + 1) * P], src[:, 0:T], start=True, stop=True)
                    give(ins, f"{use}{i}")

            for n, u in enumerate(RW_ORDER):
                t_unit(f"rw{u}")
                if n == 0:
                    for name in ("q2_0", "q2_1", "k2_0", "k2_1", "v2_0", "v2_1"):
                        wait_empty(pe, name)
                heads_step(n, 16, 8)
                if n == 1:
                    pe.wait_ge(E("lora_loaded"), 48)
                    pe.wait_ge(E("xw_tanh"), 1)
                    for tag, rows, m, x in (("z", slice(0, 64), 0, xwa), ("a", slice(64, 128), 1, xwa),
                                            ("gg", slice(0, 128), 2, xg)):
                        if tag == "gg":
                            pe.wait_ge(E("xg_ready"), 1)
                        for i in range(2):
                            out = take(f"{tag}{i}")
                            for j in range(2):
                                c = 2 * i + j
                                ins = mm(out[:, j * T:(j + 1) * T], lora[rows, m, c * P:(c + 1) * P], x[rows, :],
                                         start=True, stop=True)
                            give(ins, f"{tag}{i}")
                elif n == 3:
                    pe.wait_ge(E("kk_squares"), 1)
                    head_rows("kn", rk)
                elif n == 5:
                    pe.wait_ge(E("unfold_loaded"), 16)
                    pe.wait_ge(E("key_norms"), 1)
                    unfold_rows("kn_b", rk)
            for n in range(7, 10):
                heads_step(n, 16, 8)
                if n == 9:
                    pe.wait_ge(E("bonus_terms"), 4)
                    for i in range(2):
                        give(mm(take(f"bo{i}"), head_ones, rk[:, 512 * i:512 * i + 512], start=True, stop=True), f"bo{i}")
            for name, src, n in (("an", aTil, 1), ("vn", slot(2), 0), ("kn", kHat, 2), ("bn", bHat, 4)):
                if n:
                    pe.wait_ge(E("scaled_keys"), n)
                for tt in range(NT):
                    out = take(f"nat_{name}{tt}")
                    for p in range(4):
                        ins = nc.tensor.transpose(out[:, p * P:(p + 1) * P], src[:, p * T + tt * P:p * T + tt * P + P], ident)
                    give(ins, f"nat_{name}{tt}")

            def htile(ap, tt, h):
                hp = HD * (h % 2)
                return ap[hp:hp + HD, (h // 2) * T + tt * P:(h // 2) * T + tt * P + P]

            pe.wait_ge(E("scaled_keys"), 3)
            needs = {"AV": ("GA",), "N2": ("GD", "GN"), "D2": ("AV",), "N4": ("N2", "D2"), "X2": (), "D4": ("N4",),
                     "X4": ("D4", "X2"), "D8": (), "X8": ("D8", "X4"), "Z1": ("X8", "AV"), "EZ": ("Z1",), "ZZ": ("EZ",)}
            for pair in range(2):
                for name, _ in INVERSE:
                    for g in (2 * pair, 2 * pair + 1):
                        ts = tset[g % 2]
                        for need in needs.get(name, ()):
                            wait_empty(pe, f"{need}_{g}")
                        if name == "X2":
                            pe.wait_ge(E("series_begun"), g + 1)
                        elif name in ("AV", "Z1") and g < 2:
                            for t2 in range(NT):
                                wait_empty(pe, f"nat_{'vn' if name == 'AV' else 'an'}{t2}")
                        out = take(f"{name}_{g}")
                        for i, (tt, h) in enumerate(combo_cols(g)):
                            def m(ap):
                                return ap[:, i * P:(i + 1) * P]
                            o = m(out)
                            if name == "GN":
                                ins = mm(o, htile(bTil, tt, h), htile(aTil, tt, h), start=True, stop=True)
                            elif name == "GA":
                                ins = mm(o, htile(kTil, tt, h), htile(aTil, tt, h), start=True, stop=True)
                            elif name == "GD":
                                ins = mm(o, htile(aTil, tt, h), htile(bTil, tt, h), start=True, stop=True)
                            elif name == "AV":
                                ins = mm(out[:, i * HD:(i + 1) * HD], m(ts[3]), Vn[:, tt, h * HD:(h + 1) * HD],
                                         start=True, stop=True)
                            elif name == "Z1":
                                mm(o[:, 0:HD], m(ts[4]), An[:, tt, h * HD:(h + 1) * HD], start=True, stop=True)
                                ins = mm(o[:, HD:P], m(ts[4]), Z[:, 1, tt, h, :], start=True, stop=True)
                            else:
                                lhs, rhs = {"N2": (1, 0), "D2": (0, 1), "N4": (3, 5), "X2": (3, 4), "D4": (5, 3),
                                            "X4": (1, 4), "D8": (0, 1), "X8": (5, 4), "EZ": (2, 0), "ZZ": (4, 1)}[name]
                                ins = mm(o, m(ts[lhs]), m(ts[rhs]), start=True, stop=True)
                        give(ins, f"{name}_{g}")
            for g in range(4):
                wait_empty(pe, f"ZZ_{g}")
            for tt in range(NT):
                out = take(f"wt{tt}")
                for p in range(4):
                    ins = nc.tensor.transpose(out[:, p * P:(p + 1) * P], Z[:, 0, tt, 2 * p:2 * p + 2, :].rearrange("p h d -> p (h d)"), ident)
                give(ins, f"wt{tt}")
            wait_empty(pe, "wt0"), wait_empty(pe, "wt1")
            pe.wait_ge(E("state_zeroed"), 1)
            pe.wait_ge(E("scaled_keys"), 5)
            for name in ("kn", "bn"):
                for t2 in range(NT):
                    wait_empty(pe, f"nat_{name}{t2}")
            for c in range(NCH):
                tt, pb = c // 4, 32 * (c % 4)
                rows = slice(pb, pb + C)

                def state_mms(par, left, right, start):
                    for p in range(4):
                        h = 2 * p + par
                        hc = slice(h * HD, (h + 1) * HD)
                        ins = mm(bank(f"st{'eo'[par]}{c}")[HD * par:HD * par + HD, p * HD:(p + 1) * HD],
                                 left[rows, tt, hc], right[rows, tt, hc], start=start and p == 0, stop=not start and p == 3)
                    return ins

                for par in range(2):
                    if c:
                        wait_empty(pe, f"st{'eo'[par]}{c - 1}")
                    tag = f"sa{'eo'[par]}{c}"
                    out = take(tag)
                    hp = HD * par
                    for p in range(4):
                        ins = mm(out[rows, p * HD:(p + 1) * HD], WT[hp:hp + HD, p, c * C:(c + 1) * C],
                                 S(c)[hp:hp + HD, p * HD:(p + 1) * HD], start=True, stop=True)
                    give(ins, tag)
                    if c < NCH - 1:
                        take(f"st{'eo'[par]}{c}")
                        state_mms(par, Kn, Vn, True)
                tag, g = PRODUCTS[c]
                out = take(f"{tag}_{g}")
                for i, (t2, h) in enumerate(combo_cols(g)):
                    ins = mm(out[:, i * P:(i + 1) * P], htile(bTil if tag == "A3" else kTil, t2, h), htile(rTil, t2, h),
                             start=True, stop=True)
                give(ins, f"{tag}_{g}")
                if c < NCH - 1:
                    for par in range(2):
                        wait_empty(pe, f"sa{'eo'[par]}{c}")
                        give(state_mms(par, Bn, SA, False), f"st{'eo'[par]}{c}")
            wait_empty(pe, f"sae{NCH - 1}"), wait_empty(pe, f"sao{NCH - 1}")
            for g in range(4):
                wait_empty(pe, f"A3_{g}"), wait_empty(pe, f"A4_{g}")
                out = take(f"y{g // 2}") if g % 2 == 0 else bank(f"y{g // 2}")
                am = products(g)
                for i, (tt, h) in enumerate(combo_cols(g)):
                    hp = HD * (h % 2)
                    o = out[hp:hp + HD, (h // 2) * P:(h // 2) * P + P]
                    hc = slice(h * HD, (h + 1) * HD)
                    mm(o, SA[:, tt, hc], am[:, i * P:(i + 1) * P], start=True, stop=False)
                    mm(o, Vn[:, tt, hc], am[:, 512 + i * P:512 + (i + 1) * P], start=False, stop=False)
                    for j in range(4):
                        c = 4 * tt + j
                        ins = mm(o[:, j * C:(j + 1) * C], S(c)[hp:hp + HD, (h // 2) * HD:(h // 2) * HD + HD],
                                 rTil[hp:hp + HD, (h // 2) * T + c * C:(h // 2) * T + (c + 1) * C], start=False, stop=j == 3)
                if g % 2:
                    give(ins, f"y{g // 2}")
            wait_empty(pe, "y0"), wait_empty(pe, "y1")
            for i in range(2):
                out = take(f"gm{i}")
                give(mm(out, head_ones, LD[:, 512 * i:512 * i + 512], start=True, stop=True), f"gm{i}")
            wait_empty(pe, "o11")
            nat_unit(("wp0_0", "wp0_1"), 1, yh, yl, turn=0, part=0)
            head_rows("gv", slot(7))
            nat_unit(("wp0_0", "wp0_1"), 1, yh, yl, turn=0, part=1)
            pe.wait_ge(E("group_rstd"), 1)
            unfold_rows("gv_b", slot(9))
            nat_unit(("wp1_0", "wp1_1"), 1, yh, yl, turn=0)
            for c in range(2):
                nat_unit((f"wp{c}_0", f"wp{c}_1"), 0, yh, yl, source=None if c else "rwkv", turn=1)

            def ffn(tag, k0):
                norm_transposes(tag)
                for i in range(FF_STEPS + 1):
                    if i < FF_STEPS:
                        t_unit(f"up{tag}_{i}", None if i else tag)
                    if i == 0:
                        continue
                    u, j = unit[0], i - 1
                    arrived(u)
                    h, l = w_views(u, DM)
                    pe.wait_ge(E("hidden_lo"), k0 + j + 1)
                    buf = 2 * (j % 3)
                    for s in range(NT):
                        for c in range(2):
                            b = 4 + 2 * s + c
                            if j == 0:
                                pe.wait_ge(emptied[b], PL.uses[f"dn{tag}_{2 * s + c}"][1])
                                seen[b] += 1
                            for k in range(2):
                                cs, rs = slice(512 * c, 512 * c + 512), slice(s * P, (s + 1) * P)
                                ins = three(banks[:, b, :], yh[:, buf + k, rs], yl[:, buf + k, rs], h[:, k, cs], l[:, k, cs],
                                            j == 0 and k == 0, j == FF_STEPS - 1 and k == 1)
                            if j == FF_STEPS - 1:
                                give(ins, f"dn{tag}_{2 * s + c}")
                    if j < FF_STEPS - 1:
                        ins.then_inc(E("unit_summed"), 1)

            ffn("f0", 0)
            norm_transposes("n4")
            def conv_taps(i):
                pe.wait_ge(E("diagonals"), 2 * PE_TAPS * (i + 1))
                pe.wait_ge(E("glu"), i + 1)
                out = take(f"taps{i}")
                for j in range(2):
                    for tap in range(PE_TAPS):
                        ins = mm(out[:, j * T:(j + 1) * T], tap_diag(i, j, tap), upad[:, 2 * i + j, tap:tap + T],
                                 start=tap == 0, stop=tap == PE_TAPS - 1)
                give(ins, f"taps{i}")

            for i in range(4):
                t_unit(f"pa{i}", None if i else "n4")
                t_unit(f"pb{i}")
                if i:
                    conv_taps(i - 1)
            conv_taps(3)
            ones = const("ones")
            out = take("lnm")
            for c in range(8):
                pe.wait_ge(E("convolved"), c + 1)
                ins = mm(out[:, 0:T], ones, acc[:, c, :], start=c == 0, stop=c == 7)
            give(ins, "lnm")
            out = take("lnv")
            for c in range(8):
                pe.wait_ge(E("ln_squares"), c // 2 + 1)
                ins = mm(out[:, 0:T], ones, lnsq[:, c, :], start=c == 0, stop=c == 7)
            give(ins, "lnv")
            proj_out("pw", xh, xl, "ln")
            ffn("f1", FF_STEPS)


_OUT = ((1, T, DM), "float32")


def kernel(**inputs):
    import concourse.bacc as bacc
    from concourse.bass_utils import run_bass_kernel_spmd

    nc = bacc.Bacc("TRN2", target_bir_lowering=False, num_devices=1)
    arrays, A = {}, {}
    for name, value in inputs.items():
        a = np.ascontiguousarray(value)
        arrays[f"in_{name}"] = a
        A[name] = nc.dram_tensor(f"in_{name}", a.shape, mybir.dt.from_np(a.dtype), kind="ExternalInput").ap()
    arrays["shape_constants"] = CONSTS
    consts_d = nc.dram_tensor("shape_constants", CONSTS.shape, F32, kind="ExternalInput").ap()
    ext_d = nc.dram_tensor("rel_bias_extended", (8, 384), F32, kind="Internal").ap()
    out_d = nc.dram_tensor("out", _OUT[0], F32, kind="ExternalOutput").ap()
    build(nc, A, consts_d, ext_d, out_d)
    return run_bass_kernel_spmd(nc, [arrays], core_ids=[0]).results[0]["out"]
```
